# Optimizing a Trainium2 kernel written in Bass

```python
import jax, jax.numpy as jnp
from jax import lax
import numpy as np

D_MODEL = 1024
BATCH = 1
SEQ = 256
DEPTH = 2

N_HEADS_A = 8
HEAD_DIM_A = 64
KV_LATENT = 256
IDX_HEADS = 8
IDX_DIM = 64
TOPK_MAX = 256
Q_BLOCK = 128
SSM_D_INNER = 1024
SSM_HEADS = 16
SSM_HEAD_DIM = SSM_D_INNER // SSM_HEADS
SSM_GROUPS = 2
SSM_STATE = 128
SSM_CONV = 4
SSM_CHUNK = 128
SC_WIDTH = D_MODEL
SC_CONV = 3
D_FF = -(-8 * D_MODEL // (3 * 256)) * 256
EPS = 1e-6

A_SIZES = (N_HEADS_A * HEAD_DIM_A, KV_LATENT, IDX_HEADS * IDX_DIM, IDX_DIM, IDX_HEADS)
B_SIZES = (SSM_D_INNER, SSM_D_INNER + 2 * SSM_GROUPS * SSM_STATE, SSM_HEADS)
D_IN_EVEN = sum(A_SIZES) + sum(B_SIZES)
D_OUT_EVEN = N_HEADS_A * HEAD_DIM_A + SSM_D_INNER


def _rmsnorm(x, w):
    xf = x.astype(jnp.float32)
    y = xf * lax.rsqrt(jnp.mean(xf * xf, axis=-1, keepdims=True) + EPS)
    return y.astype(x.dtype) * w

def _split(h, sizes):
    cuts = [int(c) for c in np.cumsum(sizes)[:-1]]
    return jnp.split(h, cuts, axis=-1)

def _causal_dwconv(x, w):
    K = w.shape[0]
    return lax.conv_general_dilated(
        x, w[:, None, :], window_strides=(1,), padding=[(K - 1, 0)],
        dimension_numbers=("NWC", "WIO", "NWC"), feature_group_count=x.shape[-1])

def _dsa_attention(q, ckv, iq, ik, iw, w_uk, w_uv):
    b, S, _ = q.shape
    topk = min(TOPK_MAX, S // 4)
    nb = S // Q_BLOCK
    qb = jnp.moveaxis(q.reshape(b, nb, Q_BLOCK, N_HEADS_A, HEAD_DIM_A), 1, 0)
    iqb = jnp.moveaxis(iq.reshape(b, nb, Q_BLOCK, IDX_HEADS, IDX_DIM), 1, 0)
    iwb = jnp.moveaxis(iw.reshape(b, nb, Q_BLOCK, IDX_HEADS), 1, 0) * (IDX_HEADS ** -0.5)
    t0s = jnp.arange(nb, dtype=jnp.int32) * Q_BLOCK
    s_pos = jnp.arange(S, dtype=jnp.int32)

    def block(args):
        q_blk, iq_blk, iw_blk, t0 = args
        t_pos = t0 + jnp.arange(Q_BLOCK, dtype=jnp.int32)
        causal = s_pos[None, :] <= t_pos[:, None]
        il = jnp.einsum('bthd,bsd->bths', iq_blk, ik) * (IDX_DIM ** -0.5)
        score = jnp.einsum('bths,bth->bts', jax.nn.relu(il), iw_blk)
        score = jnp.where(causal[None], score, -jnp.inf)
        _, sel = lax.top_k(score, topk)
        c_sel = jax.vmap(lambda c, i: c[i])(ckv, sel)
        q_lat = jnp.einsum('bthd,hdc->bthc', q_blk, w_uk)
        logits = jnp.einsum('bthc,btkc->bthk', q_lat, c_sel).astype(jnp.float32) * (HEAD_DIM_A ** -0.5)
        valid = sel <= t_pos[None, :, None]
        logits = jnp.where(valid[:, :, None, :], logits, -jnp.inf)
        p = jax.nn.softmax(logits, axis=-1).astype(c_sel.dtype)
        o_lat = jnp.einsum('bthk,btkc->bthc', p, c_sel)
        o = jnp.einsum('bthc,hcd->bthd', o_lat, w_uv)
        return o.reshape(b, Q_BLOCK, N_HEADS_A * HEAD_DIM_A)

    out = lax.map(block, (qb, iqb, iwb, t0s))
    return jnp.moveaxis(out, 0, 1).reshape(b, S, N_HEADS_A * HEAD_DIM_A)

def _ssd_chunked(xs, dt, A, Bm, Cm):
    b, S, h, p = xs.shape
    g, n = Bm.shape[2], Bm.shape[3]
    r = h // g
    L = SSM_CHUNK
    c = S // L
    a = (dt * A).reshape(b, c, L, g, r)
    xdt = (xs * dt[..., None]).reshape(b, c, L, g, r, p)
    Bc = Bm.reshape(b, c, L, g, n)
    Cc = Cm.reshape(b, c, L, g, n)
    a_cs = jnp.cumsum(a, axis=2)
    tri = jnp.tril(jnp.ones((L, L), dtype=bool))
    seg = a_cs[:, :, :, None] - a_cs[:, :, None, :]
    decay = jnp.exp(jnp.where(tri[:, :, None, None], seg, -jnp.inf))
    cb = jnp.einsum('bclgn,bcsgn->bclsg', Cc, Bc)
    y_diag = jnp.einsum('bclsgr,bcsgrp->bclgrp', cb[..., None] * decay, xdt)
    decay_end = jnp.exp(a_cs[:, :, -1:] - a_cs)
    states = jnp.einsum('bclgn,bclgr,bclgrp->bcgrpn', Bc, decay_end, xdt)
    chunk_decay = jnp.exp(a_cs[:, :, -1])

    def step(hs, inp):
        dec, st = inp
        return hs * dec[..., None, None] + st, hs

    _, prev = lax.scan(step, jnp.zeros_like(states[:, 0]),
                       (jnp.moveaxis(chunk_decay, 1, 0), jnp.moveaxis(states, 1, 0)))
    prev = jnp.moveaxis(prev, 0, 1)
    y_off = jnp.einsum('bclgn,bcgrpn,bclgr->bclgrp', Cc, prev, jnp.exp(a_cs))
    return (y_diag + y_off).reshape(b, S, h, p)

def _mamba2(z, xbc, dt, conv_w, conv_b, dt_bias, A_log, D, norm_w):
    b, S, _ = z.shape
    xbc = jax.nn.silu(_causal_dwconv(xbc, conv_w) + conv_b)
    xs, Bm, Cm = _split(xbc, (SSM_D_INNER, SSM_GROUPS * SSM_STATE, SSM_GROUPS * SSM_STATE))
    xs = xs.reshape(b, S, SSM_HEADS, SSM_HEAD_DIM)
    Bm = Bm.reshape(b, S, SSM_GROUPS, SSM_STATE)
    Cm = Cm.reshape(b, S, SSM_GROUPS, SSM_STATE)
    dt = jax.nn.softplus(dt + dt_bias)
    A = -jnp.exp(A_log)
    y = _ssd_chunked(xs, dt, A, Bm, Cm) + xs * D[:, None]
    y = y.reshape(b, S, SSM_D_INNER) * jax.nn.silu(z)
    y = _rmsnorm(y.reshape(b, S, SSM_GROUPS, SSM_D_INNER // SSM_GROUPS),
                 norm_w.reshape(SSM_GROUPS, SSM_D_INNER // SSM_GROUPS))
    return y.reshape(b, S, SSM_D_INNER)

def _parallel_mixer_layer(x, attn_norm, in_w, kv_norm, w_uk, w_uv, conv_w, conv_b,
                          dt_bias, A_log, D, ssm_norm, out_w):
    h = _rmsnorm(x, attn_norm) @ in_w
    q, ckv, iq, ik, iw, z, xbc, dt = _split(h, A_SIZES + B_SIZES)
    y_a = _dsa_attention(q, _rmsnorm(ckv, kv_norm), iq, ik, iw, w_uk, w_uv)
    y_b = _mamba2(z, xbc, dt, conv_w, conv_b, dt_bias, A_log, D, ssm_norm)
    return x + jnp.concatenate([y_a, y_b], axis=-1) @ out_w

def _short_conv_layer(x, norm_w, in_w, conv_w, out_w):
    h = _rmsnorm(x, norm_w) @ in_w
    gate_b, gate_c, v = _split(h, (SC_WIDTH, SC_WIDTH, SC_WIDTH))
    y = gate_b * _causal_dwconv(gate_c * v, conv_w)
    return x + y @ out_w

def _swiglu_ffn(x, norm_w, w_gate, w_up, w_down):
    h = _rmsnorm(x, norm_w)
    return x + (jax.nn.silu(h @ w_gate) * (h @ w_up)) @ w_down

def first_inputs(seed: int = 0) -> dict:
    key = jax.random.key(seed)
    ks = jax.random.split(key, 32)

    def nrm(k, shape, fan_in):
        return jax.random.normal(k, shape, jnp.float32) * (fan_in ** -0.5)

    def gain(k, n):
        return 1.0 + 0.02 * jax.random.normal(k, (n,), jnp.float32)

    dt0 = jnp.exp(jax.random.uniform(ks[10], (SSM_HEADS,), jnp.float32, np.log(1e-3), np.log(1e-1)))
    return {
        "x": jax.random.normal(ks[0], (BATCH, SEQ, D_MODEL), jnp.float32),
        "l0_attn_norm": gain(ks[1], D_MODEL),
        "l0_in_w": nrm(ks[2], (D_MODEL, D_IN_EVEN), D_MODEL),
        "l0_kv_norm": gain(ks[3], KV_LATENT),
        "l0_w_uk": nrm(ks[4], (N_HEADS_A, HEAD_DIM_A, KV_LATENT), KV_LATENT),
        "l0_w_uv": nrm(ks[5], (N_HEADS_A, KV_LATENT, HEAD_DIM_A), KV_LATENT),
        "l0_conv_w": nrm(ks[6], (SSM_CONV, SSM_D_INNER + 2 * SSM_GROUPS * SSM_STATE), SSM_CONV),
        "l0_conv_b": 0.02 * jax.random.normal(ks[7], (SSM_D_INNER + 2 * SSM_GROUPS * SSM_STATE,), jnp.float32),
        "l0_dt_bias": dt0 + jnp.log(-jnp.expm1(-dt0)),
        "l0_A_log": jnp.log(jax.random.uniform(ks[8], (SSM_HEADS,), jnp.float32, 1.0, 16.0)),
        "l0_D": 1.0 + 0.1 * jax.random.normal(ks[9], (SSM_HEADS,), jnp.float32),
        "l0_ssm_norm": gain(ks[11], SSM_D_INNER),
        "l0_out_w": nrm(ks[12], (D_OUT_EVEN, D_MODEL), D_OUT_EVEN),
        "l0_ffn_norm": gain(ks[13], D_MODEL),
        "l0_w_gate": nrm(ks[14], (D_MODEL, D_FF), D_MODEL),
        "l0_w_up": nrm(ks[15], (D_MODEL, D_FF), D_MODEL),
        "l0_w_down": nrm(ks[16], (D_FF, D_MODEL), D_FF),
        "l1_conv_norm": gain(ks[17], D_MODEL),
        "l1_in_w": nrm(ks[18], (D_MODEL, 3 * SC_WIDTH), D_MODEL),
        "l1_conv_w": nrm(ks[19], (SC_CONV, SC_WIDTH), SC_CONV),
        "l1_out_w": nrm(ks[20], (SC_WIDTH, D_MODEL), SC_WIDTH),
        "l1_ffn_norm": gain(ks[21], D_MODEL),
        "l1_w_gate": nrm(ks[22], (D_MODEL, D_FF), D_MODEL),
        "l1_w_up": nrm(ks[23], (D_MODEL, D_FF), D_MODEL),
        "l1_w_down": nrm(ks[24], (D_FF, D_MODEL), D_FF),
        "final_norm": gain(ks[25], D_MODEL),
    }

def first_block(x, l0_attn_norm, l0_in_w, l0_kv_norm, l0_w_uk, l0_w_uv, l0_conv_w, l0_conv_b,
              l0_dt_bias, l0_A_log, l0_D, l0_ssm_norm, l0_out_w, l0_ffn_norm, l0_w_gate,
              l0_w_up, l0_w_down, l1_conv_norm, l1_in_w, l1_conv_w, l1_out_w, l1_ffn_norm,
              l1_w_gate, l1_w_up, l1_w_down, final_norm):
    layers = (
        ((l0_attn_norm, l0_in_w, l0_kv_norm, l0_w_uk, l0_w_uv, l0_conv_w, l0_conv_b,
          l0_dt_bias, l0_A_log, l0_D, l0_ssm_norm, l0_out_w),
         (l0_ffn_norm, l0_w_gate, l0_w_up, l0_w_down)),
        ((l1_conv_norm, l1_in_w, l1_conv_w, l1_out_w),
         (l1_ffn_norm, l1_w_gate, l1_w_up, l1_w_down)),
    )
    for i in range(DEPTH):
        mix_p, ffn_p = layers[i]
        if i % 2 == 0:
            x = _parallel_mixer_layer(x, *mix_p)
        else:
            x = _short_conv_layer(x, *mix_p)
        x = _swiglu_ffn(x, *ffn_p)
    return _rmsnorm(x, final_norm)


DEPTH_2 = 1

HEAD_DIM = 64
FOX_HEADS = 8
SWA_HEADS = 8
SWA_KV_HEADS = 2
SWA_GROUP = SWA_HEADS // SWA_KV_HEADS
WINDOW = 128
ROPE_THETA = 10000.0
N_GROUPS = 8
EXPERTS_PER_GROUP = 8
N_EXPERTS = N_GROUPS * EXPERTS_PER_GROUP
TOP_K = 2
D_EXPERT = D_MODEL // 2
MOE_BLOCK = 128

FOX_W = FOX_HEADS * HEAD_DIM
SWA_W = SWA_HEADS * HEAD_DIM
SWA_KV_W = SWA_KV_HEADS * HEAD_DIM
IN_SPLITS = (FOX_W, FOX_W, FOX_W, FOX_HEADS, SWA_W, SWA_KV_W, SWA_KV_W, D_MODEL, D_MODEL)
N_IN = sum(IN_SPLITS)
SPLIT_POINTS = tuple(int(v) for v in np.cumsum(IN_SPLITS)[:-1])


def rms_norm(x, g):
    xf = x.astype(jnp.float32)
    y = xf * lax.rsqrt(jnp.mean(xf * xf, axis=-1, keepdims=True) + EPS)
    return (y * g.astype(jnp.float32)).astype(x.dtype)

def rotary(x, positions):
    half = HEAD_DIM // 2
    inv_freq = ROPE_THETA ** (-jnp.arange(half, dtype=jnp.float32) * 2.0 / HEAD_DIM)
    ang = positions.astype(jnp.float32)[..., None] * inv_freq
    cos = jnp.cos(ang)[:, :, None, :]
    sin = jnp.sin(ang)[:, :, None, :]
    xf = x.astype(jnp.float32)
    x1, x2 = xf[..., :half], xf[..., half:]
    return jnp.concatenate([x1 * cos - x2 * sin, x2 * cos + x1 * sin], axis=-1).astype(x.dtype)

def fox_attention(q, k, v, log_f):
    B, S, H, Dh = q.shape
    nb = S // Q_BLOCK
    c = jnp.cumsum(log_f, axis=1)
    c_k = jnp.transpose(c, (0, 2, 1))
    q_blocks = q.reshape(B, nb, Q_BLOCK, H, Dh).transpose(1, 0, 2, 3, 4)
    c_blocks = c.reshape(B, nb, Q_BLOCK, H).transpose(1, 0, 3, 2)
    key_pos = jnp.arange(S)
    scale = HEAD_DIM ** -0.5

    def one_block(args):
        qb, cb, i = args
        s = jnp.einsum('bqhd,bkhd->bhqk', qb, k).astype(jnp.float32) * scale
        s = s + cb[..., None] - c_k[:, :, None, :]
        q_pos = i * Q_BLOCK + jnp.arange(Q_BLOCK)
        causal = key_pos[None, :] <= q_pos[:, None]
        p = jax.nn.softmax(jnp.where(causal, s, -jnp.inf), axis=-1)
        return jnp.einsum('bhqk,bkhd->bqhd', p.astype(v.dtype), v)

    o = lax.map(one_block, (q_blocks, c_blocks, jnp.arange(nb)))
    return o.transpose(1, 0, 2, 3, 4).reshape(B, S, H * Dh)

def swa_sink_attention(q, k, v, sinks):
    B, S, _, Dh = q.shape
    nb = S // WINDOW
    qb = q.reshape(B, nb, WINDOW, SWA_KV_HEADS, SWA_GROUP, Dh)

    def with_prev(t):
        t = t.reshape(B, nb, WINDOW, SWA_KV_HEADS, Dh)
        prev = jnp.pad(t[:, :-1], ((0, 0), (1, 0), (0, 0), (0, 0), (0, 0)))
        return jnp.concatenate([prev, t], axis=2)

    kw, vw = with_prev(k), with_prev(v)
    s = jnp.einsum('bnqhgd,bnkhd->bnhgqk', qb, kw).astype(jnp.float32) * (HEAD_DIM ** -0.5)
    i = jnp.arange(WINDOW)[:, None]
    j = jnp.arange(2 * WINDOW)[None, :]
    dist = WINDOW + i - j
    band = (dist >= 0) & (dist < WINDOW)
    valid = jnp.where((jnp.arange(nb) == 0)[:, None, None], band & (j >= WINDOW), band)
    s = jnp.where(valid[None, :, None, None], s, -jnp.inf)
    sink = jnp.broadcast_to(
        sinks.astype(jnp.float32).reshape(SWA_KV_HEADS, SWA_GROUP)[None, None, :, :, None, None],
        s.shape[:-1] + (1,))
    p = jax.nn.softmax(jnp.concatenate([s, sink], axis=-1), axis=-1)[..., :-1]
    o = jnp.einsum('bnhgqk,bnkhd->bnqhgd', p.astype(v.dtype), vw)
    return o.reshape(B, S, SWA_HEADS * Dh)

def hybrid_mixer(h, positions, w_in, b_forget, b_gate, sinks, w_proj_fox, w_proj_swa, w_out):
    B, S, _ = h.shape
    proj = h @ w_in
    q_f, k_f, v_f, f_logit, q_s, k_s, v_s, gl_f, gl_s = jnp.split(proj, SPLIT_POINTS, axis=-1)
    heads = lambda t, n: t.reshape(B, S, n, HEAD_DIM)
    log_f = jax.nn.log_sigmoid(f_logit.astype(jnp.float32) + b_forget.astype(jnp.float32))
    o_f = fox_attention(heads(q_f, FOX_HEADS), heads(k_f, FOX_HEADS), heads(v_f, FOX_HEADS), log_f)
    o_s = swa_sink_attention(rotary(heads(q_s, SWA_HEADS), positions),
                             rotary(heads(k_s, SWA_KV_HEADS), positions),
                             heads(v_s, SWA_KV_HEADS), sinks)
    g_f = jax.nn.sigmoid(gl_f + b_gate[0])
    g_s = jax.nn.sigmoid(gl_s + b_gate[1])
    merged = g_f * (o_f @ w_proj_fox) + g_s * (o_s @ w_proj_swa)
    return merged @ w_out

def hier_moe(h, w_group, b_group, w_expert, b_expert, w1, w3, w2):
    B, S, D = h.shape
    T = B * S
    hf = h.reshape(T, D)
    g_prob = jax.nn.softmax((hf @ w_group).astype(jnp.float32) + b_group.astype(jnp.float32), axis=-1)
    g_w, g_idx = lax.top_k(g_prob, 1)
    e_logits = ((hf @ w_expert).astype(jnp.float32) + b_expert.astype(jnp.float32)
                ).reshape(T, N_GROUPS, EXPERTS_PER_GROUP)
    e_sel = e_logits[jnp.arange(T), g_idx[:, 0]]
    top_v, top_i = lax.top_k(e_sel, TOP_K)
    gate = (g_w * jax.nn.softmax(top_v, axis=-1)).reshape(-1)
    expert_id = (g_idx * EXPERTS_PER_GROUP + top_i).reshape(-1)
    token_id = jnp.repeat(jnp.arange(T, dtype=jnp.int32), TOP_K)
    A = T * TOP_K
    order = jnp.argsort(expert_id)
    e_sorted = expert_id[order]
    counts = jnp.bincount(expert_id, length=N_EXPERTS)
    padded = (counts + MOE_BLOCK - 1) // MOE_BLOCK * MOE_BLOCK
    start = jnp.cumsum(counts) - counts
    pad_end = jnp.cumsum(padded)
    pad_start = pad_end - padded
    dest = pad_start[e_sorted] + jnp.arange(A) - start[e_sorted]
    P = A + N_EXPERTS * MOE_BLOCK
    n_blk = P // MOE_BLOCK
    row_token = jnp.full((P,), T, jnp.int32).at[dest].set(token_id[order])
    row_gate = jnp.zeros((P,), jnp.float32).at[dest].set(gate[order])
    blk_expert = jnp.minimum(jnp.searchsorted(pad_end, jnp.arange(n_blk) * MOE_BLOCK, side='right'),
                             N_EXPERTS - 1)
    h_pad = jnp.concatenate([hf, jnp.zeros((1, D), hf.dtype)], axis=0)
    xs = h_pad[row_token].reshape(n_blk, MOE_BLOCK, D)

    def expert_block(args):
        xb, e = args
        return (jax.nn.silu(xb @ w1[e]) * (xb @ w3[e])) @ w2[e]

    ys = lax.map(expert_block, (xs, blk_expert)).reshape(P, D)
    out = jnp.zeros((T + 1, D), jnp.float32).at[row_token].add(row_gate[:, None] * ys.astype(jnp.float32))
    return out[:T].reshape(B, S, D).astype(h.dtype)

def second_inputs(seed: int = 0) -> dict:
    key = jax.random.key(seed)
    ks = jax.random.split(key, 20)
    L, D = DEPTH_2, D_MODEL
    nrm = lambda k, shape, fan_in: jax.random.normal(k, shape, jnp.float32) * fan_in ** -0.5
    return {
        "x": jax.random.normal(ks[0], (BATCH, SEQ, D), jnp.float32),
        "positions": (jnp.arange(SEQ, dtype=jnp.int32)[None, :]
                      + jax.random.randint(ks[1], (BATCH, 1), 0, 1024, jnp.int32)),
        "attn_norm": 1.0 + 0.1 * jax.random.normal(ks[2], (L, D), jnp.float32),
        "w_in": nrm(ks[3], (L, D, N_IN), D),
        "b_forget": jax.random.uniform(ks[4], (L, FOX_HEADS), jnp.float32, 1.0, 4.0),
        "b_gate": 0.02 * jax.random.normal(ks[5], (L, 2, D), jnp.float32),
        "attn_sinks": jax.random.normal(ks[6], (L, SWA_HEADS), jnp.float32),
        "w_proj_fox": nrm(ks[7], (L, FOX_W, D), FOX_W),
        "w_proj_swa": nrm(ks[8], (L, SWA_W, D), SWA_W),
        "w_out": nrm(ks[9], (L, D, D), D),
        "ffn_norm": 1.0 + 0.1 * jax.random.normal(ks[10], (L, D), jnp.float32),
        "w_group": nrm(ks[11], (L, D, N_GROUPS), D),
        "b_group": 0.01 * jax.random.normal(ks[12], (L, N_GROUPS), jnp.float32),
        "w_expert": nrm(ks[13], (L, D, N_EXPERTS), D),
        "b_expert": 0.01 * jax.random.normal(ks[14], (L, N_EXPERTS), jnp.float32),
        "w1": nrm(ks[15], (L, N_EXPERTS, D, D_EXPERT), D),
        "w3": nrm(ks[16], (L, N_EXPERTS, D, D_EXPERT), D),
        "w2": nrm(ks[17], (L, N_EXPERTS, D_EXPERT, D), D_EXPERT),
        "final_norm": 1.0 + 0.1 * jax.random.normal(ks[18], (D,), jnp.float32),
    }

def second_block(x, positions, attn_norm, w_in, b_forget, b_gate, attn_sinks, w_proj_fox, w_proj_swa,
              w_out, ffn_norm, w_group, b_group, w_expert, b_expert, w1, w3, w2, final_norm):
    for l in range(DEPTH_2):
        h = rms_norm(x, attn_norm[l])
        x = x + hybrid_mixer(h, positions, w_in[l], b_forget[l], b_gate[l], attn_sinks[l],
                             w_proj_fox[l], w_proj_swa[l], w_out[l])
        h = rms_norm(x, ffn_norm[l])
        x = x + hier_moe(h, w_group[l], b_group[l], w_expert[l], b_expert[l], w1[l], w3[l], w2[l])
    return rms_norm(x, final_norm)


def setup_inputs(seed=0):
    out = dict(first_inputs(seed))
    for name, value in second_inputs(seed + 1).items():
        if name != "x":
            out[name + "_2"] = value
    return out


def reference(
    x, l0_attn_norm, l0_in_w, l0_kv_norm, l0_w_uk, l0_w_uv, l0_conv_w, l0_conv_b, l0_dt_bias,
    l0_A_log, l0_D, l0_ssm_norm, l0_out_w, l0_ffn_norm, l0_w_gate, l0_w_up, l0_w_down,
    l1_conv_norm, l1_in_w, l1_conv_w, l1_out_w, l1_ffn_norm, l1_w_gate, l1_w_up, l1_w_down,
    final_norm, positions_2, attn_norm_2, w_in_2, b_forget_2, b_gate_2, attn_sinks_2,
    w_proj_fox_2, w_proj_swa_2, w_out_2, ffn_norm_2, w_group_2, b_group_2, w_expert_2,
    b_expert_2, w1_2, w3_2, w2_2, final_norm_2,
):
    x = first_block(
        x, l0_attn_norm, l0_in_w, l0_kv_norm, l0_w_uk, l0_w_uv, l0_conv_w, l0_conv_b,
        l0_dt_bias, l0_A_log, l0_D, l0_ssm_norm, l0_out_w, l0_ffn_norm, l0_w_gate, l0_w_up,
        l0_w_down, l1_conv_norm, l1_in_w, l1_conv_w, l1_out_w, l1_ffn_norm, l1_w_gate, l1_w_up,
        l1_w_down, final_norm,
    )
    return second_block(
        x, positions_2, attn_norm_2, w_in_2, b_forget_2, b_gate_2, attn_sinks_2, w_proj_fox_2,
        w_proj_swa_2, w_out_2, ffn_norm_2, w_group_2, b_group_2, w_expert_2, b_expert_2, w1_2,
        w3_2, w2_2, final_norm_2,
    )


_drawn_inputs = setup_inputs


def setup_inputs(seed=0):
    import zlib

    import numpy as np

    out = dict(_drawn_inputs(seed))
    spreads = {}
    factors = {'l0_kv_norm': 5.283,
     'l1_ffn_norm': 3.944,
     'b_gate_2': 8.0,
     'attn_sinks_2': 5.156,
     'b_group_2': 8.0,
     'b_expert_2': 7.894,
     'l0_conv_b': 2.671,
     'l0_ssm_norm': 3.369}
    for name, (base, spread) in spreads.items():
        noise = np.random.default_rng([zlib.crc32(name.encode()), seed]).standard_normal(out[name].shape)
        drawn = base * np.exp(spread * noise) if base else spread * noise
        out[name] = __import__('jax').numpy.asarray(drawn.astype(out[name].dtype))
    for name, factor in factors.items():
        out[name] = (out[name] * factor).astype(out[name].dtype)
    return out
```

```python
from contextlib import ExitStack

import numpy as np

import concourse.bass as bass
from concourse import mybir

F32 = mybir.dt.float32
I32 = mybir.dt.int32
ALU = mybir.AluOpType
ACT = mybir.ActivationFunctionType
AX_X = mybir.AxisListType.X

P = 128
T = 256
NT = T // P
D = 1024
KD = D // P
EPS = 1e-6
NEG = -1e30
TAKEN = -3e38

HEADS = 8
DH = 64
LATENT = 256
TOPK = 64
SSM_HEADS = 16
SSM_IN = 1024
D_STATE = 128
CONV_CH = 1536
NX = CONV_CH // P
D_FF = 2816
NF = D_FF // P
N_GROUPS = 8
PER_GROUP = 8
N_EXPERTS = 64
D_EXPERT = 512
NE = D_EXPERT // P
CAP = 64

SLOTS = 6
SLOT = 4096
FFN_RING = 4
PI = 3.1415925
TWO_PI = (6.28125, 0.0019350051879882812, 3.019915981956753e-07)
ROUND = 12582912.0
ARENA = 18176
STAT = 1100
LOG1P = [1 / (2 * k + 1) for k in range(8, 0, -1)]

UNITS = [(0, 0, (0, 2, 4, 6), P), (0, 4, (1, 3, 5, 7), P),
         (1, 8, (0, 2), T), (1, 10, (1, 3), T), (1, 12, (4, 6), T), (1, 14, (5, 7), T)]

SMALL = [
    ("ident", P), ("tri", P), ("strict", P), ("ones", P), ("open", P), ("causal", P), ("band", P), ("causal2", P),
    ("causal_t", P), ("iota", CAP), ("down8", N_GROUPS), ("freq", DH // 2), ("half", 8),
    ("attn_norm", KD), ("ffn_norm", KD), ("l1_norm", KD), ("ffn1_norm", KD), ("attn2_norm", KD), ("moe_norm", KD),
    ("kv_norm", 2), ("conv_w", 4 * NX), ("conv_b", NX), ("dt_bias", 16), ("A_log", 16), ("Dskip", 16),
    ("ssm_norm", KD), ("sc_w", 3 * KD), ("b_forget", 8), ("b_gate", 2 * KD), ("sinks", 8), ("b_router", 72),
]
AT = {}
_at = 0
for _name, _width in SMALL:
    AT[_name] = (_at, _width)
    _at += _width
N_SMALL = _at


class PsumOrder:

    def __init__(self, tile_ready, act_drained, dve_drained):
        self.tile_ready = tile_ready
        self.sem = {"act": act_drained, "dve": dve_drained}
        self.at, self.info, self.count = {}, [], {"act": 0, "dve": 0}
        self.n = 0

    def add(self, name, drainer):
        assert name not in self.at, name
        self.at[name] = len(self.info)
        self.n += 1
        self.count[drainer] += 1
        self.info.append((name, drainer, self.n, self.count[drainer]))

    def skip(self):
        self.info.append(None)

    def bank(self, name):
        return self.at[name] % 8

    def ready(self, name):
        return self.tile_ready, self.info[self.at[name]][2]

    def drained(self, name):
        _, drainer, _, k = self.info[self.at[name]]
        return self.sem[drainer], k

    def bank_free(self, name):
        before = self.at[name] - 8
        if before < 0 or self.info[before] is None:
            return None
        return self.drained(self.info[before][0])


class WeightRing:

    def __init__(self, landed):
        self.landed_sem = landed
        self.next = 0
        self.dmas = [0] * SLOTS
        self.last = [None] * SLOTS
        self.unit = {}

    def add(self, name, n_dma, release, slot=None):
        if slot is None:
            slot, self.next = self.next % SLOTS, self.next + 1
        before = self.last[slot]
        self.dmas[slot] += n_dma
        self.unit[name] = (slot, before, 16 * self.dmas[slot])
        self.last[slot] = release
        return slot

    def slot(self, name):
        return self.unit[name][0]

    def landed(self, name):
        slot, _, value = self.unit[name]
        return self.landed_sem[slot], value

    def vacated(self, name):
        return self.unit[name][1]


class Steps:

    def __init__(self, eng, sem):
        self.eng, self.sem, self.base = eng, sem, 0

    def __call__(self, ins):
        self.base = self.base + 1
        ins.then_inc(self.sem, 1)
        self.eng.wait_ge(self.sem, self.base)


def program(nc, d, out):
    with ExitStack() as ctx:
        def sb(name, shape, dt=F32):
            return ctx.enter_context(nc.sbuf_tensor(name, shape, dt))

        def sem(name):
            return ctx.enter_context(nc.semaphore(name))

        ring = sb("ring", [P, SLOTS, SLOT])
        small = sb("small", [P, N_SMALL])
        pos = sb("pos", [P, NT], I32)
        passes_i = sb("passes_i", [P, 1], I32)
        x = sb("x", [P, NT, D])
        xn = sb("xn", [P, NT, D])
        xnT = sb("xnT", [P, KD, T])
        norm_row = sb("norm_row", [P, D])
        arena = sb("arena", [P, ARENA])
        stat = sb("stat", [P, STAT])
        w_router = sb("w_router", [P, KD, 72])

        def part(of, at, shape):
            n = int(np.prod(shape))
            assert at + n <= of.shape[-1], (at, shape)
            v = of[:, at:at + n]
            if len(shape) == 2:
                v = v.rearrange("p (a b) -> p a b", a=shape[0])
            if len(shape) == 3:
                v = v.rearrange("p (a b c) -> p a b c", a=shape[0], b=shape[1])
            return v

        arena_at, stat_at = [0], [0]

        def carve(*shape):
            v = part(arena, arena_at[0], shape)
            arena_at[0] += int(np.prod(shape))
            return v

        def few(*shape):
            v = part(stat, stat_at[0], shape)
            stat_at[0] += int(np.prod(shape))
            return v

        def c(name, a=None, b=None):
            at, width = AT[name]
            a, b = (0, width) if a is None else (a, a + 1 if b is None else b)
            return small[:, at + a:at + b]

        ident, tri, strict, ones = c("ident"), c("tri"), c("strict"), c("ones")

        def two(name):
            return small[:, AT[name][0]:AT[name][0] + T]

        causal_mask = [c("causal"), two("open")]
        window_mask = [c("causal"), two("band")]

        ss, mean, rstd = few(8, NT), few(8, NT), few(8, NT)
        top_max = few(3, 2 * HEADS)
        neg_max = few(3, 2 * HEADS)
        row_sum = few(3, 2 * HEADS)
        row_inv = few(3, 2 * HEADS)

        qT, kT, v_tok = carve(4, T), carve(4, T), carve(NT, 512)
        lm, pr, pT = carve(2, 512), carve(2, 512), carve(2, 512)
        mixT = carve(12, T)
        shared = arena_at[0]
        iqT, ikT = carve(4, T), carve(T)
        xp = part(arena, shared, (2, 2, 259))
        sel_mask, ckvT, ckv = carve(NT, T), carve(2, T), carve(NT, LATENT)
        score, work = carve(NT, T), carve(NT, T)
        z, convT = carve(NT, D), carve(NX, T)
        y_tok = xn
        xs = xnT[:, :, :].rearrange("p k t -> p (k t)").rearrange("p (a b) -> p a b", a=NT)
        xdt = convT[:, 0:8, :].rearrange("p k t -> p (k t)").rearrange("p (a b) -> p a b", a=NT)
        xdt_end = norm_row
        state = qT.rearrange("p a b -> p (a b)").rearrange("p (g n) -> p g n", g=2)
        cbT = kT.rearrange("p a b -> p (a b)")[:, 0:512].rearrange("p (a b) -> p a b", a=4)
        B_tok = kT.rearrange("p a b -> p (a b)")[:, 512:768].rearrange("p (a b) -> p a b", a=2)
        y_part = v_tok
        iw, dt_in, dt, a_dt = few(NT, 8), few(NT, 16), few(NT, 16), few(NT, 16)
        neg_A = few(16)
        acs, acs_exp, end_exp = few(3, 16), few(16), few(16)
        top8 = few(NT, 8)
        sp = few(7, NT * 16)
        ssg, mean_g, rstd_g = few(NT, 2), few(NT, 2), few(NT, 2)
        ss_kv, mean_kv, rstd_kv = few(NT, 1), few(NT, 1), few(NT, 1)

        arena_at[0] = 0
        sg_f, h_f = carve(2, T), carve(2, T)
        c_sb, cv, sc_conv = carve(2, T), carve(2, T + 2), carve(2, T)
        scT = carve(KD, T)

        arena_at[0] = shared
        mixT2 = mixT[:, 0:8, :]
        arena_at[0] = shared - 4 * T
        sqT, skT, sv = carve(4, T), carve(2, T), carve(NT, P)
        rope_x, rope_a, rope_b = carve(NT, 640), carve(640), carve(640)
        fox_d = carve(2, 512)
        gates = carve(2, KD, T)
        mergedT = xn[:, :, :].rearrange("p a b -> p (a b)").rearrange("p (k t) -> p k t", k=KD)
        stat_mark = stat_at[0]
        stat_at[0] = 240
        f_in, log_f, fox_c, f_neg, f_u, f_tmp = few(NT, 8), few(NT, 8), few(NT, 8), few(NT * 8), few(NT * 8), few(5, NT * 8)
        pos_f, rope_k = few(NT), few(NT, 32)
        ang, red, cosr = few(NT, 32), few(NT, 32), few(NT, 32)
        sin_t, cos_t = few(NT, 32), few(NT, 32)
        sink_d, sink_e = few(2 * HEADS), few(2 * HEADS)

        arena_at[0] = 0
        sel_g = carve(NT, CAP)
        sel_gT = carve(T)
        xg = carve(KD, CAP)
        gate_g = carve(PER_GROUP, CAP)
        sg_e, hh_e, hg_e = carve(2, NE * CAP), carve(2, NE * CAP), carve(2, NE * CAP)
        yT_g = carve(KD * CAP)
        y_g = carve(D)
        stat_at[0] = 48
        r_log = few(NT, 72)
        g_max, g_exp, g_sum, g_w = few(NT), few(NT, 8), few(NT), few(NT)
        g_eq, g_first, g_hot = few(NT, 8), few(NT), few(NT, 8)
        e_all, e_sel = few(64), few(NT, 8)
        e_m1, e_eq1, e_f1, e_hot1 = few(NT), few(NT, 8), few(NT), few(NT, 8)
        e_rest, e_m2, e_eq2, e_f2, e_hot2 = few(NT, 8), few(NT), few(NT, 8), few(NT), few(NT, 8)
        e_d, e_x, e_den, e_w1, e_w2 = few(NT), few(NT), few(NT), few(NT), few(NT)
        gate8, rank8, rank = few(NT, 8), few(NT, 8), few(NT)
        total, most, over, passes_f = few(8), few(1), few(1), few(1)

        psum = ctx.enter_context(nc.psum_tensor("psum", [P, 8, 512], F32))

        small_in, x_in, row_in, router_in = sem("small_in"), sem("x_in"), sem("row_in"), sem("router_in")
        landed = [sem(f"landed{i}") for i in range(SLOTS)]
        tile_ready, act_drained, dve_drained = sem("tile_ready"), sem("act_drained"), sem("dve_drained")
        act_step, dve_step, pool_step = sem("act_step"), sem("dve_step"), sem("pool_step")
        squares, rstd_ready, xn_ready = sem("squares"), sem("rstd_ready"), sem("xn_ready")
        part_used = sem("part_used")
        kv_sq, kv_rstd, ckv_ready = sem("kv_sq"), sem("kv_rstd"), sem("ckv_ready")
        pads_zero = sem("pads_zero")
        logits_masked, probs_raw, sums_inverted, probs_ready = (
            sem("logits_masked"), sem("probs_raw"), sem("sums_inverted"), sem("probs_ready"))
        conv_sum, conv_done = sem("conv_sum"), sem("conv_done")
        il_used, ssm_y, end_sub = sem("il_used"), sem("ssm_y"), sem("end_sub")
        sp_abs, sp_exp, a_ready, a_log_exp = sem("sp_abs"), sem("sp_exp"), sem("a_ready"), sem("a_log_exp")
        xdt_ready, decays_ready = sem("xdt_ready"), sem("decays_ready")
        seg_ready, seg_exp, ssm_w = sem("seg_ready"), sem("seg_exp"), sem("ssm_w")
        state_ready, y_sq, y_rstd, y_ready = sem("state_ready"), sem("y_sq"), sem("y_rstd"), sem("y_ready")
        f_abs, f_exp, log_f_ready = sem("f_abs"), sem("f_exp"), sem("log_f_ready")
        angles, sincos, roped = sem("angles"), sem("sincos"), sem("roped")
        sink_sub, sink_exp = sem("sink_sub"), sem("sink_exp")
        merged = sem("merged")
        ffn_in, ffn_silu, ffn_h, ffn_part = sem("ffn_in"), sem("ffn_silu"), sem("ffn_h"), sem("ffn_part")
        sc_ready, x_final, scaled_ready = sem("sc_ready"), sem("x_final"), sem("scaled_ready")
        y_gated = sem("y_gated")
        r_sub, r_exp, r_gate, r_pass = sem("r_sub"), sem("r_exp"), sem("r_gate"), sem("r_pass")
        m_sel, m_selT, m_selT_sb, m_xg, m_xg_sb, m_gate, m_gate_sb = (
            sem("m_sel"), sem("m_selT"), sem("m_selT_sb"), sem("m_xg"), sem("m_xg_sb"), sem("m_gate"), sem("m_gate_sb"))
        m_w1, m_h, m_silu, m_hg, m_y, m_yT, m_tp, m_yg, m_sc, m_scd = (
            sem("m_w1"), sem("m_h"), sem("m_silu"), sem("m_hg"), sem("m_y"), sem("m_yT"), sem("m_tp"), sem("m_yg"),
            sem("m_sc"), sem("m_scd"))
        moe_done, out_ready, out_sent = sem("moe_done"), sem("out_ready"), sem("out_sent")

        O = PsumOrder(tile_ready, act_drained, dve_drained)
        RES = [(tc, h) for tc in range(NT) for h in range(2)]

        def plan_norm(n):
            for j in range(4):
                O.add(f"norm{n}_{j}", "act" if j % 2 == 0 else "dve")

        def plan_attention(kind, before=lambda u: None):
            for u in range(len(UNITS) + 2):
                if u < len(UNITS):
                    before(u)
                    O.add(f"{kind}_l{u}", "dve")
                if 1 <= u <= len(UNITS):
                    O.add(f"{kind}_t{u - 1}", "act")
                if u >= 2:
                    O.add(f"{kind}_o{u - 2}", "dve")

        def plan_out(name):
            for tc, h in RES:
                O.add(f"{name}_{tc}{h}", "dve")

        def plan_ffn(n):
            plan_norm(2 * n + 1)
            plan_out(f"ffn{n}")
            O.skip()
            O.skip()

        plan_norm(0)
        for j in range(2):
            O.add(f"iq{j}", "act" if j == 0 else "dve")
        O.add("ik", "act")
        for tc in range(NT):
            O.add(f"misc{tc}", "dve")
        for u in range(len(UNITS)):
            O.add(f"il{u}", "act")
        for j in range(2):
            O.add(f"q{j}", "act")
        for j in range(NX // 2):
            O.add(f"xb{j}", "act")
        for h in range(2):
            for tc in range(NT):
                O.add(f"z{tc}{h}", "act")
        O.add("ckvT", "act")
        for j in range(2):
            O.add(f"k{j}", "act")
        for s in range(NT):
            O.add(f"v{s}", "act")
        plan_attention("mla")
        for tc in range(NT):
            for h in range(2):
                O.add(f"xs{tc}{h}", "act" if h == 0 else "dve")
        O.add("B_tok", "act")
        O.add("cbT", "act")
        O.add("acs", "dve")
        for name, drainer in (("bc00", "dve"), ("bc01", "dve"), ("st0", "act"), ("st1", "act"), ("bc02", "dve"),
                              ("bc03", "dve"), ("y00", "dve"), ("bc10", "dve"), ("bc11", "dve"), ("y01", "dve"),
                              ("bc12", "dve"), ("bc13", "dve"), ("y10", "dve"), ("yo0", "dve"), ("y11", "dve"),
                              ("yo1", "dve")):
            O.add(name, drainer)
        for j in range(4):
            O.add(f"yT{j}", "act" if j % 2 == 0 else "dve")
        plan_out("out0")
        plan_ffn(0)
        plan_norm(2)
        for j in range(KD):
            O.add(f"cv{j}", "dve")
            O.add(f"b{j}", "dve")
        plan_out("out1")
        plan_ffn(1)
        plan_norm(4)
        for n in ("fq", "fk"):
            for j in range(2):
                O.add(f"{n}{j}", "act" if j == 0 else "dve")
        for tc in range(NT):
            O.add(f"fv{tc}", "act")
        for tc in range(NT):
            O.add(f"misc2_{tc}", "act")
        for tc in range(NT):
            O.add(f"sq{tc}", "act")
        for n in ("gf", "gs"):
            for j in range(4):
                O.add(f"{n}{j}", "act")
        O.add("fox_c", "dve")
        plan_attention("fox", lambda u: O.add(f"fox_b{u}", "dve"))
        for j in range(2):
            O.add(f"sqT{j}", "act")
        O.add("skT", "act")
        plan_attention("swa")
        for j in range(4):
            O.add(f"pf{j}", "dve")
            O.add(f"ps{j}", "dve")
        plan_out("out2")
        plan_norm(5)
        for tc in range(NT):
            O.add(f"router{tc}", "dve")
        O.add("rank", "dve")

        W = WeightRing(landed)
        for n, last in (("iq", "iq1"), ("misc", "misc1"), ("q", "q1"), ("xb0", "xb1"), ("xb1", "xb3"), ("xb2", "xb5"),
                        ("z0", "z10"), ("z1", "z11")):
            W.add(n, 1, O.ready(last))
        W.add("kv", 2, O.ready("v1"))
        parts = [0]

        def part_release():
            parts[0] += 1
            return part_used, parts[0]

        def plan_rows(name, n, tiles):
            for i in range(n):
                W.add(f"{name}w{i}", 1, O.ready(f"{tiles}_11") if i == n - 1 else part_release())

        plan_rows("out0", 3, "out0")
        FFN_SLOT = {}

        def plan_ffn_weights(n):
            for j in range(NF):
                first = W.next
                slot = (first + j % FFN_RING) % SLOTS
                W.add(f"ffn{n}_{j}", 3, (ffn_part, n * (NF - 1) + j + 1) if j < NF - 1 else O.ready(f"ffn{n}_11"), slot)
            FFN_SLOT[n] = [(W.next + b) % SLOTS for b in range(FFN_RING)]
            W.next += FFN_RING

        plan_ffn_weights(0)
        for j in range(KD):
            W.add(f"l1_{j}", 1, O.ready(f"b{j}"))
        plan_rows("out1", 2, "out1")
        plan_ffn_weights(1)
        for n, last in (("fq", "fq1"), ("fk", "fk1"), ("fv", "fv1"), ("misc2", "misc2_1"), ("sq", "sq1"),
                        ("gf0", "gf1"), ("gf1", "gf3"), ("gs0", "gs1"), ("gs1", "gs3"), ("pf", "pf3"), ("ps", "ps3")):
            W.add(n, 1, O.ready(last))
        plan_rows("out2", 2, "out2")
        MOE = []
        for e in range(PER_GROUP):
            MOE += [("w1", e), ("w3", e)] + ([("w2", e - 1)] if e else [])
        MOE.append(("w2", PER_GROUP - 1))
        assert len(MOE) == 3 * PER_GROUP and len(MOE) % SLOTS == 0
        MOE_SLOT = [(W.next + u) % SLOTS for u in range(len(MOE))]
        MOE_BEFORE = [W.last[s] for s in MOE_SLOT[:SLOTS]]
        MOE_BASE = [W.dmas[s] * 16 for s in MOE_SLOT]
        PER_SLOT = len(MOE) // SLOTS
        MOE_USED = {"w1": m_w1, "w3": m_h, "w2": m_y}

        def slot8(s, n=512):
            return ring[:, s, 0:KD * n].rearrange("p (k n) -> p k n", k=KD)

        def bank(name):
            return psum[:, O.bank(name), :]

        def bank2(name, w=T):
            return bank(name)[:, 0:2 * w].rearrange("p (a b) -> p a b", a=2)

        block = ctx.enter_context(nc.Block())

        def unit_rows(name):
            return ring[:, W.slot(name), :].rearrange("p (k n) -> p k n", k=4)

        def y_rows_used(i):
            cc, hq = i // 4, i % 4
            return O.ready(f"y{cc}{hq // 2}") if hq % 2 else (ssm_y, 2 * cc + hq // 2 + 1)

        NORMS = {0: 0, 1: 1, 2: 2, 3: 3, "first": 4, 4: 5, 5: 6, "last": 7}
        GAIN = ["attn_norm", "ffn_norm", "l1_norm", "ffn1_norm", "attn2_norm", "moe_norm"]
        KINDS = {"mla": 0, "fox": 1, "swa": 2}
        NU = len(UNITS)
        H_BANK, Y_BANK, XG_BANK, G_BANK, T_BANK, S_BANK = (0, 1), 2, 3, 4, (5, 6), (7, 3, 4, 5)
        PREFETCH = MOE[:SLOTS]

        @block.sync
        def _(sp):
            sp.dma_start(small[:, :], d["small"]).then_inc(small_in, 16)
            sp.dma_start(x[:, :, :], d["x"].rearrange("(a p) n -> p a n", p=P)).then_inc(x_in, 16)
            sp.dma_start(pos[:, :], d["positions"]).then_inc(small_in, 16)
            sp.dma_start(w_router[:, :, :], d["w_router"].rearrange("(p k) n -> p k n", k=KD)).then_inc(router_in, 16)

            def load(name, *pieces):
                if W.vacated(name):
                    sp.wait_ge(*W.vacated(name))
                for dst, src in pieces:
                    sp.dma_start(dst, src).then_inc(landed[W.slot(name)], 16)

            def columns(name, w, n=512):
                load(name, (slot8(W.slot(name), n), w.rearrange("(p k) n -> p k n", k=KD)))

            def rows(name, w, n):
                for i in range(n):
                    load(f"{name}w{i}", (unit_rows(f"{name}w{i}"), w[i * 512:(i + 1) * 512].rearrange("(k p) n -> p k n", p=P)))

            def ffn(n, gate, up, down):
                def pieces(slot, j):
                    yield ring[:, slot, 0:1024].rearrange("p (k n) -> p k n", k=KD), gate[j]
                    yield ring[:, slot, 1024:2048].rearrange("p (k n) -> p k n", k=KD), up[j]
                    yield ring[:, slot, 2048:3072], down[j]

                for j in range(FFN_RING):
                    load(f"ffn{n}_{j}", *pieces(FFN_SLOT[n][j], j))
                with sp.Fori(1, NF // FFN_RING) as i:
                    for b in range(FFN_RING):
                        sp.wait_ge(ffn_part, i * FFN_RING + (n * (NF - 1) + b - FFN_RING + 1))
                        for dst, src in pieces(FFN_SLOT[n][b], i * FFN_RING + b):
                            sp.dma_start(dst, src).then_inc(landed[FFN_SLOT[n][b]], 16)
                for j in range(NF // FFN_RING * FFN_RING, NF):
                    load(f"ffn{n}_{j}", *pieces(FFN_SLOT[n][j % FFN_RING], j))

            in_w = d["in_w"]
            columns("iq", in_w[:, 768:1280])
            columns("misc", d["misc"], 344)
            columns("q", in_w[:, 0:512])
            for i in range(3):
                columns(f"xb{i}", in_w[:, 2376 + 512 * i:2888 + 512 * i])
            for i in range(2):
                columns(f"z{i}", in_w[:, 1352 + 512 * i:1864 + 512 * i])
            s = W.slot("kv")
            load("kv", (ring[:, s, 0:1024].rearrange("p (k n) -> p k n", k=2), d["w_uk"].rearrange("(k p) n -> p k n", p=P)),
                 (ring[:, s, 1024:2048].rearrange("p (k n) -> p k n", k=2), d["w_uv"].rearrange("(k p) n -> p k n", p=P)))
            rows("out0", d["out_w0"], 3)
            ffn(0, d["gate0"], d["up0"], d["down0"])
            for j in range(KD):
                load(f"l1_{j}", (ring[:, W.slot(f"l1_{j}"), 0:3072], d["l1_in"][j]))
            rows("out1", d["out_w1"], 2)
            sp.wait_ge(*O.ready("st1"))
            sp.dma_start(norm_row[:, :], d["final_norm"].to_broadcast([P, D])).then_inc(row_in, 16)
            ffn(1, d["gate1"], d["up1"], d["down1"])
            w2 = d["w_in2"]
            columns("fq", w2[:, 0:512])
            columns("fk", w2[:, 512:1024])
            columns("fv", w2[:, 1024:1536])
            columns("misc2", d["misc2"], 264)
            columns("sq", w2[:, 1544:2056])
            for i in range(2):
                columns(f"gf{i}", w2[:, 2312 + 512 * i:2824 + 512 * i])
            for i in range(2):
                columns(f"gs{i}", w2[:, 3336 + 512 * i:3848 + 512 * i])
            load("pf", (unit_rows("pf"), d["proj_fox"].rearrange("(k p) n -> p k n", p=P)))
            load("ps", (unit_rows("ps"), d["proj_swa"].rearrange("(k p) n -> p k n", p=P)))
            rows("out2", d["out_w2"], 2)
            sp.wait_ge(x_final, NT)
            sp.dma_start(norm_row[:, :], d["final_norm2"].to_broadcast([P, D])).then_inc(row_in, 16)

            def expert_load(kind, e, u):
                slot = MOE_SLOT[u]
                if kind == "w2":
                    dst, src = unit_rows_at(slot), d["w2"][bass.ds(e * NE, NE)].rearrange("k p n -> p k n")
                else:
                    dst, src = ring[:, slot, :], d[kind][bass.ds(e, 1)].rearrange("a p n -> p (a n)")
                sp.dma_start(dst, src).then_inc(landed[slot], 16)

            def unit_rows_at(slot):
                return ring[:, slot, :].rearrange("p (k n) -> p k n", k=NE)

            for u, (kind, e) in enumerate(PREFETCH):
                if MOE_BEFORE[u]:
                    sp.wait_ge(*MOE_BEFORE[u])
                expert_load(kind, e, u)
            sp.wait_ge(r_pass, 1)
            passes = sp.value_load(passes_i[0:1, 0:1], min_val=1, max_val=T // CAP)

            def rest_of_group(n8, g8):
                for u in range(SLOTS, len(MOE)):
                    kind, e = MOE[u]
                    before, eb = MOE[u - SLOTS]
                    sp.wait_ge(MOE_USED[before], n8 + eb + 1)
                    expert_load(kind, g8 + e, u)

            def first_of_group(n8, g8):
                for u, (kind, e) in enumerate(PREFETCH):
                    before, eb = MOE[len(MOE) - SLOTS + u]
                    sp.wait_ge(MOE_USED[before], n8 + eb + 1)
                    expert_load(kind, g8 + e, u)

            with sp.Fori(0, passes) as p:
                with sp.Fori(0, N_GROUPS - 1) as g:
                    rest_of_group(p * N_EXPERTS + g * PER_GROUP, g * PER_GROUP)
                    first_of_group(p * N_EXPERTS + g * PER_GROUP, g * PER_GROUP + PER_GROUP)
                rest_of_group(p * N_EXPERTS + (N_EXPERTS - PER_GROUP), N_EXPERTS - PER_GROUP)
                with sp.If(p + 1 < passes):
                    first_of_group(p * N_EXPERTS + (N_EXPERTS - PER_GROUP), 0)
            for tc in range(NT):
                sp.wait_ge(out_ready, tc + 1)
                sp.dma_start(out[tc * P:(tc + 1) * P, :], x[:, tc, :]).then_inc(out_sent, 16)
            sp.wait_ge(out_sent, 16 * NT)

        @block.tensor
        def _(pe):
            mm = nc.tensor.matmul
            seen = [0]

            def begin(name):
                if O.bank_free(name):
                    pe.wait_ge(*O.bank_free(name))

            def end(name, ins):
                seen[0] += 1
                assert O.ready(name)[1] == seen[0], name
                ins.then_inc(tile_ready, 1)

            def norm_T(n):
                pe.wait_ge(xn_ready, NT * (n + 1))
                for j in range(4):
                    name = f"norm{n}_{j}"
                    begin(name)
                    for kk in range(2):
                        for tc in range(NT):
                            at = kk * T + tc * P
                            last = nc.tensor.transpose(bank(name)[:, at:at + P], xn[:, tc, 2 * j + kk::KD], ident)
                    end(name, last)

            def normed(n):
                for j in (2, 3):
                    pe.wait_ge(*O.drained(f"norm{n}_{j}"))

            def channels(name, unit, first, count=2, n=512):
                w = slot8(W.slot(unit), n)
                begin(name)
                for m in range(count):
                    for k in range(KD):
                        last = mm(bank(name)[:, m * T:(m + 1) * T], w[:, k, (first + m) * P:(first + m + 1) * P],
                                  xnT[:, k, :], start=(k == 0), stop=(k == KD - 1))
                end(name, last)

            def tokens(name, unit, tc, width, n=512):
                w = slot8(W.slot(unit), n)
                begin(name)
                for k in range(KD):
                    last = mm(bank(name)[:, 0:width], xnT[:, k, tc * P:(tc + 1) * P], w[:, k, 0:width],
                              start=(k == 0), stop=(k == KD - 1))
                end(name, last)

            def out_rows(name, src, n):
                for tc, h in RES:
                    begin(f"{name}_{tc}{h}")
                for kc in range(4 * n):
                    unit = f"{name}w{kc // 4}"
                    if kc % 4 == 0:
                        pe.wait_ge(*W.landed(unit))
                    for tc, h in RES:
                        last = mm(bank(f"{name}_{tc}{h}"), src[:, kc, tc * P:(tc + 1) * P],
                                  unit_rows(unit)[:, kc % 4, h * 512:(h + 1) * 512],
                                  start=(kc == 0), stop=(kc == 4 * n - 1))
                        if kc == 4 * n - 1:
                            end(f"{name}_{tc}{h}", last)
                    if kc % 4 == 3 and kc < 4 * n - 1:
                        last.then_inc(part_used, 1)

            def attention(kind, q, k_of, v_of, before=lambda u: None):
                K = KINDS[kind] * NU

                def logits(u):
                    tc, _, heads, w = UNITS[u]
                    name = f"{kind}_l{u}"
                    begin(name)
                    for i, h in enumerate(heads):
                        a = DH * (h % 2)
                        last = mm(bank(name)[:, i * w:(i + 1) * w], q[a:a + DH, h // 2, tc * P:(tc + 1) * P],
                                  k_of(h)[a:a + DH, 0:w], start=True, stop=True)
                    end(name, last)

                def turn(u):
                    name = f"{kind}_t{u}"
                    pe.wait_ge(probs_ready, K + u + 1)
                    begin(name)
                    for blk in range(4):
                        last = nc.tensor.transpose(bank(name)[:, blk * P:(blk + 1) * P],
                                                   pr[:, u % 2, blk * P:(blk + 1) * P], ident)
                    end(name, last)

                def mix(u):
                    tc, _, heads, w = UNITS[u]
                    name = f"{kind}_o{u}"
                    pe.wait_ge(*O.drained(f"{kind}_t{u}"))
                    begin(name)
                    ns = w // P
                    for i, h in enumerate(heads):
                        a = DH * (h % 2)
                        for s in range(ns):
                            last = mm(bank(name)[a:a + DH, i * P:(i + 1) * P], v_of(h, s),
                                      pT[:, u % 2, (i * ns + s) * P:(i * ns + s + 1) * P],
                                      start=(s == 0), stop=(s == ns - 1))
                    end(name, last)

                for u in range(NU + 2):
                    if u < NU:
                        before(u)
                        logits(u)
                    if 1 <= u <= NU:
                        turn(u - 1)
                    if u >= 2:
                        mix(u - 2)

            def ffn(n):
                norm_T(2 * n + 1)
                normed(2 * n + 1)
                base = O.at[f"ffn{n}_11"] + 1
                gu = [psum[:, (base + b) % 8, :] for b in range(2)]
                for tc, h in RES:
                    begin(f"ffn{n}_{tc}{h}")

                def gate_up(b, slot):
                    w = ring[:, slot, 0:2048].rearrange("p (g k n) -> p g k n", g=2, k=KD)
                    for m in range(2):
                        for k in range(KD):
                            last = mm(gu[b % 2][:, m * T:(m + 1) * T], w[:, m, k, :], xnT[:, k, :],
                                      start=(k == 0), stop=(k == KD - 1))
                    last.then_inc(ffn_in, 1)

                def down(b, slot, start=False, stop=False):
                    for tc, h in RES:
                        last = mm(bank(f"ffn{n}_{tc}{h}"), h_f[:, b % 2, tc * P:(tc + 1) * P],
                                  ring[:, slot, 2048 + h * 512:2560 + h * 512], start=start, stop=stop,
                                  skip_group_check=True)
                        if stop:
                            end(f"ffn{n}_{tc}{h}", last)
                    if not stop:
                        last.then_inc(ffn_part, 1)

                s = FFN_SLOT[n]
                pe.wait_ge(*W.landed(f"ffn{n}_0"))
                gate_up(0, s[0])
                pe.wait_ge(*W.landed(f"ffn{n}_1"))
                gate_up(1, s[1])
                pe.wait_ge(ffn_h, n * NF + 1)
                down(0, s[0], start=True)
                with pe.Fori(0, NF // FFN_RING) as i:
                    for b in range(1, FFN_RING + 1):
                        nxt = b + 1
                        slot = s[nxt % FFN_RING]
                        if b < FFN_RING or True:
                            pe.wait_ge(landed[slot], i * (16 * 3) + W.landed(f"ffn{n}_{nxt}")[1])
                        gate_up(nxt, slot)
                        pe.wait_ge(ffn_h, i * FFN_RING + (n * NF + b + 1))
                        down(b, s[b % FFN_RING])
                pe.wait_ge(ffn_h, (n + 1) * NF)
                down(NF - 1, s[(NF - 1) % FFN_RING], stop=True)

            pe.wait_ge(small_in, 32)
            norm_T(0)
            normed(0)
            pe.wait_ge(*W.landed("iq"))
            for j in range(2):
                channels(f"iq{j}", "iq", 2 * j)
            pe.wait_ge(*W.landed("misc"))
            w = slot8(W.slot("misc"), 344)
            begin("ik")
            for half in range(2):
                for k in range(KD):
                    last = mm(bank("ik")[half * DH:(half + 1) * DH, 0:T], w[:, k, 280:344], xnT[:, k, :],
                              start=(k == 0), stop=(k == KD - 1))
            end("ik", last)
            for tc in range(NT):
                tokens(f"misc{tc}", "misc", tc, 280, 344)
            for name in ("iq0", "iq1", "ik"):
                pe.wait_ge(*O.drained(name))
            for u, (tc, _, heads, wd) in enumerate(UNITS):
                name = f"il{u}"
                begin(name)
                for i, h in enumerate(heads):
                    a = DH * (h % 2)
                    last = mm(bank(name)[:, i * wd:(i + 1) * wd], iqT[a:a + DH, h // 2, tc * P:(tc + 1) * P],
                              ikT[a:a + DH, 0:wd], start=True, stop=True)
                end(name, last)
            pe.wait_ge(*W.landed("q"))
            for j in range(2):
                channels(f"q{j}", "q", 2 * j)
            for j in range(6):
                if j % 2 == 0:
                    pe.wait_ge(*W.landed(f"xb{j // 2}"))
                channels(f"xb{j}", f"xb{j // 2}", 2 * (j % 2))
            for h in range(2):
                pe.wait_ge(*W.landed(f"z{h}"))
                for tc in range(NT):
                    tokens(f"z{tc}{h}", f"z{h}", tc, 512)
            pe.wait_ge(ckv_ready, NT)
            begin("ckvT")
            for cc in range(2):
                for tc in range(NT):
                    last = nc.tensor.transpose(bank("ckvT")[:, cc * T + tc * P:cc * T + (tc + 1) * P],
                                               ckv[:, tc, cc * P:(cc + 1) * P], ident)
            end("ckvT", last)
            pe.wait_ge(*W.landed("kv"))
            pe.wait_ge(*O.drained("ckvT"))
            w_uk = ring[:, W.slot("kv"), 0:1024].rearrange("p (k n) -> p k n", k=2)
            w_uv = ring[:, W.slot("kv"), 1024:2048].rearrange("p (k n) -> p k n", k=2)
            for j in range(2):
                begin(f"k{j}")
                for m in range(2):
                    for kc in range(2):
                        last = mm(bank(f"k{j}")[:, m * T:(m + 1) * T], w_uk[:, kc, (2 * j + m) * P:(2 * j + m + 1) * P],
                                  ckvT[:, kc, :], start=(kc == 0), stop=(kc == 1))
                end(f"k{j}", last)
            for s in range(NT):
                begin(f"v{s}")
                for kc in range(2):
                    last = mm(bank(f"v{s}"), ckvT[:, kc, s * P:(s + 1) * P], w_uv[:, kc, :],
                              start=(kc == 0), stop=(kc == 1))
                end(f"v{s}", last)
            pe.wait_ge(*O.drained("v1"))
            attention("mla", qT, lambda h: kT[:, h // 2, :], lambda h, s: v_tok[:, s, h * DH:(h + 1) * DH])
            pe.wait_ge(conv_done, 6)
            for tc in range(NT):
                for h in range(2):
                    name = f"xs{tc}{h}"
                    begin(name)
                    for q in range(4):
                        last = nc.tensor.transpose(bank(name)[:, q * P:(q + 1) * P],
                                                   convT[:, 4 * h + q, tc * P:(tc + 1) * P], ident)
                    end(name, last)
            begin("B_tok")
            for g in range(2):
                last = nc.tensor.transpose(bank("B_tok")[:, g * P:(g + 1) * P], convT[:, 8 + g, 0:P], ident)
            end("B_tok", last)
            begin("cbT")
            for cc in range(NT):
                for g in range(2):
                    at = (2 * cc + g) * P
                    last = mm(bank("cbT")[:, at:at + P], convT[:, 8 + g, cc * P:(cc + 1) * P],
                              convT[:, 10 + g, cc * P:(cc + 1) * P], start=True, stop=True)
            end("cbT", last)
            pe.wait_ge(a_ready, 1)
            begin("acs")
            mm(bank("acs")[:, 0:16], tri, a_dt[:, 0, :], start=True, stop=True)
            mm(bank("acs")[:, 16:32], tri, a_dt[:, 1, :], start=True, stop=True)
            end("acs", mm(bank("acs")[:, 32:48], ones, a_dt[:, 0, :], start=True, stop=True))

            def cumulative(cc, hq):
                name = f"bc{cc}{hq}"
                begin(name)
                for i in range(4):
                    last = mm(bank(name)[:, i * P:(i + 1) * P],
                              a_dt[:, cc, 4 * hq + i:4 * hq + i + 1].to_broadcast([P, P]), tri, start=True, stop=True)
                end(name, last)

            def states(g):
                begin(f"st{g}")
                end(f"st{g}", mm(bank(f"st{g}"), B_tok[:, g, :], xdt_end[:, g * 512:(g + 1) * 512],
                                 start=True, stop=True))

            def within(cc, g):
                name = f"y{cc}{g}"
                begin(name)
                for hq in (2 * g, 2 * g + 1):
                    pe.wait_ge(ssm_w, 4 * cc + hq + 1)
                    for i in range(4):
                        h = 4 * hq + i
                        last = mm(bank(name)[:, (h % 8) * DH:(h % 8 + 1) * DH], pT[:, hq % 2, i * P:(i + 1) * P],
                                  xdt[:, cc, h * DH:(h + 1) * DH], start=True, stop=True)
                    if hq % 2 == 0:
                        last.then_inc(ssm_y, 1)
                end(name, last)

            def across(g):
                pe.wait_ge(*O.drained(f"st{g}"))
                begin(f"yo{g}")
                end(f"yo{g}", mm(bank(f"yo{g}"), convT[:, 10 + g, P:T], state[:, g, :], start=True, stop=True))

            cumulative(0, 0)
            cumulative(0, 1)
            pe.wait_ge(xdt_ready, 3)
            pe.wait_ge(*O.drained("B_tok"))
            states(0)
            states(1)
            cumulative(0, 2)
            cumulative(0, 3)
            within(0, 0)
            cumulative(1, 0)
            cumulative(1, 1)
            within(0, 1)
            cumulative(1, 2)
            cumulative(1, 3)
            within(1, 0)
            across(0)
            within(1, 1)
            across(1)
            pe.wait_ge(y_ready, 4)
            for j in range(4):
                name = f"yT{j}"
                begin(name)
                for kk in range(2):
                    for tc in range(NT):
                        at = kk * T + tc * P
                        last = nc.tensor.transpose(bank(name)[:, at:at + P],
                                                   y_tok[:, tc, (2 * j + kk) * P:(2 * j + kk + 1) * P], ident)
                end(name, last)
            for j in (2, 3):
                pe.wait_ge(*O.drained(f"yT{j}"))
            out_rows("out0", mixT, 3)
            ffn(0)
            norm_T(2)
            normed(2)
            for j in range(KD):
                pe.wait_ge(*W.landed(f"l1_{j}"))
                w = ring[:, W.slot(f"l1_{j}"), 0:3072].rearrange("p (k m n) -> p k m n", k=KD, m=3)
                begin(f"cv{j}")
                for m in range(2):
                    for k in range(KD):
                        last = mm(bank(f"cv{j}")[:, m * T:(m + 1) * T], w[:, k, m, :], xnT[:, k, :],
                                  start=(k == 0), stop=(k == KD - 1))
                end(f"cv{j}", last)
                begin(f"b{j}")
                for k in range(KD):
                    last = mm(bank(f"b{j}")[:, 0:T], w[:, k, 2, :], xnT[:, k, :], start=(k == 0), stop=(k == KD - 1))
                end(f"b{j}", last)
            pe.wait_ge(*O.drained(f"b{KD - 1}"))
            out_rows("out1", scT, 2)
            ffn(1)
            norm_T(4)
            normed(4)
            for n in ("fq", "fk"):
                pe.wait_ge(*W.landed(n))
                for j in range(2):
                    channels(f"{n}{j}", n, 2 * j)
            pe.wait_ge(*W.landed("fv"))
            for tc in range(NT):
                tokens(f"fv{tc}", "fv", tc, 512)
            pe.wait_ge(*W.landed("misc2"))
            for tc in range(NT):
                tokens(f"misc2_{tc}", "misc2", tc, 264, 264)
            pe.wait_ge(*W.landed("sq"))
            for tc in range(NT):
                tokens(f"sq{tc}", "sq", tc, 512)
            for n in ("gf", "gs"):
                for j in range(4):
                    if j % 2 == 0:
                        pe.wait_ge(*W.landed(f"{n}{j // 2}"))
                    channels(f"{n}{j}", f"{n}{j // 2}", 2 * (j % 2))
            pe.wait_ge(log_f_ready, 1)
            begin("fox_c")
            mm(bank("fox_c")[:, 0:8], tri, log_f[:, 0, :], start=True, stop=True)
            mm(bank("fox_c")[:, 8:16], ones, log_f[:, 0, :], start=True, stop=False)
            end("fox_c", mm(bank("fox_c")[:, 8:16], tri, log_f[:, 1, :], start=False, stop=True))

            def forget_sums(u):
                tc, _, heads, wd = UNITS[u]
                name = f"fox_b{u}"
                begin(name)
                for i, h in enumerate(heads):
                    f0 = log_f[:, 0, h:h + 1].to_broadcast([P, P])
                    last = mm(bank(name)[:, i * wd:i * wd + P], f0, tri, start=True, stop=True)
                    if wd == T:
                        f1 = log_f[:, 1, h:h + 1].to_broadcast([P, P])
                        mm(bank(name)[:, i * wd + P:(i + 1) * wd], f0, ones, start=True, stop=False)
                        last = mm(bank(name)[:, i * wd + P:(i + 1) * wd], f1, tri, start=False, stop=True)
                end(name, last)

            for name in ("fq1", "fk1", "fv1"):
                pe.wait_ge(*O.drained(name))
            attention("fox", qT, lambda h: kT[:, h // 2, :], lambda h, s: v_tok[:, s, h * DH:(h + 1) * DH], forget_sums)
            pe.wait_ge(roped, NT)
            for j in range(2):
                name = f"sqT{j}"
                begin(name)
                for m in range(2):
                    for tc in range(NT):
                        at = m * T + tc * P
                        last = nc.tensor.transpose(bank(name)[:, at:at + P],
                                                   rope_x[:, tc, (2 * j + m) * P:(2 * j + m + 1) * P], ident)
                end(name, last)
            begin("skT")
            for kv in range(2):
                for tc in range(NT):
                    at = kv * T + tc * P
                    for half in range(2):
                        last = mm(bank("skT")[half * DH:(half + 1) * DH, at:at + P],
                                  rope_x[:, tc, 512 + kv * DH:512 + (kv + 1) * DH], ident, start=True, stop=True)
            end("skT", last)
            pe.wait_ge(*O.drained("skT"))
            attention("swa", sqT, lambda h: skT[:, h // 4, :],
                      lambda h, s: sv[:, s, (h // 4) * DH:(h // 4 + 1) * DH])
            pe.wait_ge(*O.drained("swa_o5"))
            for n in ("pf", "ps"):
                pe.wait_ge(*W.landed(n))
            for j in range(4):
                for gi, n in enumerate(("pf", "ps")):
                    begin(f"{n}{j}")
                    for m in range(2):
                        for kc in range(4):
                            last = mm(bank(f"{n}{j}")[:, m * T:(m + 1) * T],
                                      unit_rows(n)[:, kc, (2 * j + m) * P:(2 * j + m + 1) * P], mixT[:, 4 * gi + kc, :],
                                      start=(kc == 0), stop=(kc == 3))
                    end(f"{n}{j}", last)
            pe.wait_ge(merged, 4)
            out_rows("out2", mergedT, 2)
            norm_T(5)
            normed(5)
            pe.wait_ge(router_in, 16)
            for tc in range(NT):
                begin(f"router{tc}")
                for k in range(KD):
                    last = mm(bank(f"router{tc}")[:, 0:72], xnT[:, k, tc * P:(tc + 1) * P], w_router[:, k, :],
                              start=(k == 0), stop=(k == KD - 1))
                end(f"router{tc}", last)
            pe.wait_ge(r_gate, 1)
            begin("rank")
            mm(bank("rank")[:, 0:8], strict, g_hot[:, 0, :], start=True, stop=True)
            mm(bank("rank")[:, 8:16], ones, g_hot[:, 0, :], start=True, stop=False)
            mm(bank("rank")[:, 8:16], strict, g_hot[:, 1, :], start=False, stop=True)
            mm(bank("rank")[:, 16:24], ones, g_hot[:, 0, :], start=True, stop=False)
            end("rank", mm(bank("rank")[:, 16:24], ones, g_hot[:, 1, :], start=False, stop=True))
            pe.wait_ge(r_pass, 1)
            pe.wait_ge(r_gate, 2)
            passes = pe.value_load(passes_i[0:1, 0:1], min_val=1, max_val=T // CAP)

            def moe_landed(u, n):
                pe.wait_ge(landed[MOE_SLOT[u]], n * (16 * PER_SLOT) + (MOE_BASE[u] + 16 * (u // SLOTS + 1)))

            def expert_in(e, n, n8):
                for m, kind in enumerate(("w1", "w3")):
                    u = MOE.index((kind, e))
                    moe_landed(u, n)
                    if m == 0 and e >= 2:
                        pe.wait_ge(m_hg, n8 + e - 1)
                    w = slot8(MOE_SLOT[u])
                    for j in range(NE):
                        at = (m * NE + j) * CAP
                        for k in range(KD):
                            last = mm(psum[:, H_BANK[e % 2], at:at + CAP], w[:, k, j * P:(j + 1) * P], xg[:, k, :],
                                      start=(k == 0), stop=(k == KD - 1))
                    last.then_inc(m_w1 if kind == "w1" else m_h, 1)

            def expert_out(e, n, n8):
                u = MOE.index(("w2", e))
                moe_landed(u, n)
                pe.wait_ge(m_hg, n8 + e + 1)
                w = ring[:, MOE_SLOT[u], :].rearrange("p (k n) -> p k n", k=NE)
                for kd in range(KD):
                    for j in range(NE):
                        last = mm(psum[:, Y_BANK, kd * CAP:(kd + 1) * CAP], w[:, j, kd * P:(kd + 1) * P],
                                  hg_e[:, e % 2, j * CAP:(j + 1) * CAP], start=(e == 0 and kd == 0 and j == 0),
                                  stop=(e == PER_GROUP - 1 and j == NE - 1), skip_group_check=True)
                last.then_inc(m_y, 1)

            with pe.Fori(0, passes) as p:
                with pe.Fori(0, N_GROUPS) as g:
                    n = pe.snap(p * N_GROUPS + g)
                    n8 = pe.snap(n * PER_GROUP)
                    pe.wait_ge(m_sel, n + 1)
                    pe.wait_ge(m_scd, n * 4)
                    for k in range(KD):
                        for tc in range(NT):
                            last = mm(psum[:, XG_BANK, k * CAP:(k + 1) * CAP], xn[:, tc, k::KD], sel_g[:, tc, :],
                                      start=(tc == 0), stop=(tc == NT - 1))
                    last.then_inc(m_xg, 1)
                    for e in range(PER_GROUP):
                        for tc in range(NT):
                            last = mm(psum[:, G_BANK, e * CAP:(e + 1) * CAP],
                                      gate8[:, tc, e:e + 1].to_broadcast([P, P]), sel_g[:, tc, :],
                                      start=(tc == 0), stop=(tc == NT - 1))
                    last.then_inc(m_gate, 1)
                    for tc in range(NT):
                        last = nc.tensor.transpose(psum[0:CAP, T_BANK[1], tc * P:(tc + 1) * P], sel_g[:, tc, :], ident)
                    last.then_inc(m_selT, 1)
                    pe.wait_ge(m_xg_sb, n + 1)
                    for e in range(PER_GROUP + 1):
                        if e < PER_GROUP:
                            expert_in(e, n, n8)
                        if e >= 1:
                            expert_out(e - 1, n, n8)
                    pe.wait_ge(m_yT, n + 1)
                    pe.wait_ge(m_selT_sb, n + 1)
                    for j in range(KD // 2):
                        last = nc.tensor.transpose(psum[:, T_BANK[0], j * P:(j + 1) * P],
                                                   yT_g[:, 2 * j * CAP:(2 * j + 2) * CAP], ident)
                    last.then_inc(m_tp, 1)
                    pe.wait_ge(m_yg, n * 2 + 2)
                    for i, (tc, h) in enumerate(RES):
                        mm(psum[:, S_BANK[i], :], sel_gT[0:CAP, tc * P:(tc + 1) * P],
                           y_g[0:CAP, h * 512:(h + 1) * 512], start=True, stop=True).then_inc(m_sc, 1)

        @block.scalar
        def _(act):
            A = nc.scalar.activation

            def square(n, source):
                for tc in range(NT):
                    act.wait_ge(*source(tc))
                    A(xn[:, tc, :], x[:, tc, :], ACT.Square, accum_out=ss[:, NORMS[n], tc:tc + 1]).then_inc(squares, 1)

            def added(name):
                return lambda tc: O.drained(f"{name}_{tc}1")

            def norm_T(n):
                for j in (0, 2):
                    act.wait_ge(*O.ready(f"norm{n}_{j}"))
                    for kk in range(2):
                        k = 2 * j + kk
                        last = A(xnT[:, k, :], bank(f"norm{n}_{j}")[:, kk * T:(kk + 1) * T], ACT.Copy, scale=c(GAIN[n], k))
                    last.then_inc(act_drained, 1)

            def copy(name, dst, width=512, func=ACT.Copy):
                act.wait_ge(*O.ready(name))
                src = bank(name)[:, 0:width]
                if len(dst.shape) == 3:
                    src = src.rearrange("p (a b) -> p a b", a=dst.shape[1])
                A(dst, src, func).then_inc(act_drained, 1)

            def attention(kind):
                K = KINDS[kind]

                def probs(u):
                    tc, at, heads, w = UNITS[u]
                    nh = len(heads)
                    act.wait_ge(logits_masked, K * NU + u + 1)
                    if u >= 2:
                        act.wait_ge(*O.ready(f"{kind}_t{u - 2}"))
                    for i in range(nh):
                        col = at + i
                        last = A(pr[:, u % 2, i * w:(i + 1) * w], lm[:, u % 2, i * w:(i + 1) * w], ACT.Exp,
                                 bias=neg_max[:, K, col:col + 1], accum_out=row_sum[:, K, col:col + 1])
                    last.then_inc(probs_raw, 1)
                    if kind == "swa":
                        act.wait_ge(sink_sub, u + 1)
                        A(sink_e[:, at:at + nh], sink_d[:, at:at + nh], ACT.Exp).then_inc(sink_exp, 1)

                for u in range(NU + 1):
                    if u < NU:
                        probs(u)
                    if u >= 1:
                        copy(f"{kind}_t{u - 1}", pT[:, (u - 1) % 2, :])

            def ffn(n):
                norm_T(2 * n + 1)
                base = O.at[f"ffn{n}_11"] + 1
                with act.Fori(0, NF // 2) as i:
                    for b in range(2):
                        act.wait_ge(ffn_in, i * 2 + (n * NF + b + 1))
                        A(sg_f[:, b, :], psum[:, (base + b) % 8, 0:T], ACT.Silu).then_inc(ffn_silu, 1)

            act.wait_ge(small_in, 32)
            square(0, lambda tc: (x_in, 16))
            norm_T(0)
            act.wait_ge(*O.ready("iq0"))
            copy("iq0", iqT[:, 0:2, :])
            copy("ik", ikT, T)
            for tc in range(NT):
                act.wait_ge(*O.drained(f"misc{tc}"))
                A(work[:, tc, :], ckv[:, tc, :], ACT.Square, accum_out=ss_kv[:, tc, :]).then_inc(kv_sq, 1)
            for u in range(NU):
                if u >= 2:
                    act.wait_ge(il_used, u - 1)
                copy(f"il{u}", lm[:, u % 2, :], 512, ACT.Relu)
            for j in range(2):
                copy(f"q{j}", qT[:, 2 * j:2 * j + 2, :])
            act.wait_ge(sp_abs, 1)
            A(sp[:, 1, :], sp[:, 0, :], ACT.Exp, scale=-1.0).then_inc(sp_exp, 1)
            A(neg_A, c("A_log"), ACT.Exp).then_inc(a_log_exp, 1)
            act.wait_ge(pads_zero, 1)

            def conv_silu(j):
                act.wait_ge(conv_sum, j + 1)
                for m in range(2):
                    ch = 2 * j + m
                    last = A(convT[:, ch, :], convT[:, ch, :], ACT.Silu, bias=c("conv_b", ch))
                last.then_inc(conv_done, 1)

            for j in range(6):
                if j >= 2:
                    act.wait_ge(conv_sum, j - 1)
                act.wait_ge(*O.ready(f"xb{j}"))
                A(xp[:, j % 2, :, 3:259], bank2(f"xb{j}"), ACT.Copy).then_inc(act_drained, 1)
                if j >= 1:
                    conv_silu(j - 1)
            conv_silu(5)
            for h in range(2):
                for tc in range(NT):
                    copy(f"z{tc}{h}", z[:, tc, h * 512:(h + 1) * 512], 512, ACT.Silu)
            act.wait_ge(*O.ready("ckvT"))
            for cc in range(2):
                last = A(ckvT[:, cc, :], bank("ckvT")[:, cc * T:(cc + 1) * T], ACT.Copy, scale=c("kv_norm", cc))
            last.then_inc(act_drained, 1)
            for j in range(2):
                copy(f"k{j}", kT[:, 2 * j:2 * j + 2, :])
            for s in range(NT):
                copy(f"v{s}", v_tok[:, s, :])
            attention("mla")
            for tc in range(NT):
                copy(f"xs{tc}0", xs[:, tc, 0:512])
            copy("B_tok", B_tok[:, :, :], 256)
            copy("cbT", cbT[:, :, :])
            act.wait_ge(end_sub, 1)
            A(end_exp, sp[:, 2, 0:16], ACT.Exp).then_inc(decays_ready, 1)
            A(acs_exp, acs[:, 1, :], ACT.Exp).then_inc(decays_ready, 1)

            def seg(i):
                act.wait_ge(*O.drained(f"bc{i // 4}{i % 4}"))
                if i >= 2:
                    act.wait_ge(ssm_w, i - 1)
                A(pr[:, i % 2, :], lm[:, i % 2, :], ACT.Exp).then_inc(seg_exp, 1)

            seg(0)
            seg(1)
            copy("st0", state[:, 0, :])
            copy("st1", state[:, 1, :])
            for i in range(2, 8):
                seg(i)
            for i in range(4):
                cc, g = i // 2, i % 2
                act.wait_ge(y_gated, i + 1)
                A(xs[:, cc, g * 512:(g + 1) * 512], y_tok[:, cc, g * 512:(g + 1) * 512], ACT.Square,
                  accum_out=ssg[:, cc, g:g + 1]).then_inc(y_sq, 1)
            for j in (0, 2):
                act.wait_ge(*O.ready(f"yT{j}"))
                for kk in range(2):
                    k = 2 * j + kk
                    last = A(mixT[:, 4 + k, :], bank(f"yT{j}")[:, kk * T:(kk + 1) * T], ACT.Copy, scale=c("ssm_norm", k))
                last.then_inc(act_drained, 1)
            square(1, added("out0"))
            ffn(0)
            square(2, added("ffn0"))
            norm_T(2)
            square(3, added("out1"))
            ffn(1)
            square("first", added("ffn1"))
            square(4, lambda tc: (x_final, tc + 1))
            norm_T(4)
            copy("fq0", qT[:, 0:2, :])
            copy("fk0", kT[:, 0:2, :])
            for tc in range(NT):
                copy(f"fv{tc}", v_tok[:, tc, :])
            for tc in range(NT):
                act.wait_ge(*O.ready(f"misc2_{tc}"))
                A(f_in[:, tc, :], bank(f"misc2_{tc}")[:, 0:8], ACT.Copy)
                A(rope_x[:, tc, 512:640], bank(f"misc2_{tc}")[:, 8:136], ACT.Copy)
                A(sv[:, tc, :], bank(f"misc2_{tc}")[:, 136:264], ACT.Copy).then_inc(act_drained, 1)
            act.wait_ge(f_abs, 1)
            A(f_u, f_tmp[:, 0, :], ACT.Exp, scale=-1.0).then_inc(f_exp, 1)
            for tc in range(NT):
                copy(f"sq{tc}", rope_x[:, tc, 0:512])
            act.wait_ge(angles, 1)
            A(sin_t[:, :, :], red[:, :, :], ACT.Sin).then_inc(sincos, 1)
            A(cos_t[:, :, :], cosr[:, :, :], ACT.Sin).then_inc(sincos, 1)
            for gi, n in enumerate(("gf", "gs")):
                for j in range(4):
                    act.wait_ge(*O.ready(f"{n}{j}"))
                    for m in range(2):
                        ch = 2 * j + m
                        last = A(gates[:, gi, ch, :], bank(f"{n}{j}")[:, m * T:(m + 1) * T], ACT.Sigmoid,
                                 bias=c("b_gate", gi * KD + ch))
                    last.then_inc(act_drained, 1)
            attention("fox")
            for j in range(2):
                copy(f"sqT{j}", sqT[:, 2 * j:2 * j + 2, :])
            copy("skT", skT[:, :, :])
            attention("swa")
            square(5, added("out2"))
            norm_T(5)
            act.wait_ge(r_sub, 1)
            A(g_exp[:, :, :], g_exp[:, :, :], ACT.Exp).then_inc(r_exp, 1)
            act.wait_ge(r_sub, 2)
            A(e_x, e_d, ACT.Exp).then_inc(r_exp, 1)
            act.wait_ge(r_pass, 1)
            passes = act.value_load(passes_i[0:1, 0:1], min_val=1, max_val=T // CAP)
            with act.Fori(0, passes) as p:
                with act.Fori(0, N_GROUPS) as g:
                    n = act.snap(p * N_GROUPS + g)
                    n8 = act.snap(n * PER_GROUP)
                    act.wait_ge(m_gate, n + 1)
                    A(gate_g[:, :, :], psum[:, G_BANK, :].rearrange("p (a b) -> p a b", a=PER_GROUP),
                      ACT.Copy).then_inc(m_gate_sb, 1)
                    act.wait_ge(m_selT, n + 1)
                    A(sel_gT[0:CAP, :], psum[0:CAP, T_BANK[1], 0:T], ACT.Copy).then_inc(m_selT_sb, 1)
                    for e in range(PER_GROUP):
                        act.wait_ge(m_h, n8 + e + 1)
                        A(sg_e[:, e % 2, :], psum[:, H_BANK[e % 2], 0:NE * CAP], ACT.Silu).then_inc(m_silu, 1)
                    act.wait_ge(m_y, n8 + PER_GROUP)
                    A(yT_g, psum[:, Y_BANK, :], ACT.Copy).then_inc(m_yT, 1)
                    act.wait_ge(m_tp, n + 1)
                    y_half = y_g[0:CAP, :].rearrange("p (j h c) -> p j h c", h=2, c=P)
                    for i in range(2):
                        A(y_half[:, :, i, :], psum[i * CAP:(i + 1) * CAP, T_BANK[0], :].rearrange("p (j c) -> p j c", c=P),
                          ACT.Copy).then_inc(m_yg, 1)
            square("last", lambda tc: (moe_done, 1))

        @block.vector
        def _(dve):
            V = nc.vector
            step = Steps(dve, dve_step)

            def drain(name, ins):
                ins.then_inc(dve_drained, 1)
                dve.wait_ge(*O.drained(name))

            def norm(n):
                for tc in range(NT):
                    dve.wait_ge(rstd_ready, NT * NORMS[n] + tc + 1)
                    V.tensor_scalar(xn[:, tc, :], x[:, tc, :], rstd[:, NORMS[n], tc:tc + 1], None,
                                    ALU.mult).then_inc(xn_ready, 1)
                for j in (1, 3):
                    dve.wait_ge(*O.ready(f"norm{n}_{j}"))
                    for kk in range(2):
                        k = 2 * j + kk
                        last = V.tensor_scalar(xnT[:, k, :], bank(f"norm{n}_{j}")[:, kk * T:(kk + 1) * T], c(GAIN[n], k),
                                               None, ALU.mult)
                    last.then_inc(dve_drained, 1)

            def scaled_norm(n, done, row):
                dve.wait_ge(row_in, row)
                for tc in range(NT):
                    dve.wait_ge(rstd_ready, NT * NORMS[n] + tc + 1)
                    V.scalar_tensor_tensor(x[:, tc, :], x[:, tc, :], rstd[:, NORMS[n], tc:tc + 1], norm_row[:, :],
                                           ALU.mult, ALU.mult).then_inc(done, 1)
                    dve.wait_ge(done, tc + 1)

            def add_out(name):
                for tc, h in RES:
                    tile = f"{name}_{tc}{h}"
                    dve.wait_ge(*O.ready(tile))
                    part_x = x[:, tc, h * 512:(h + 1) * 512]
                    drain(tile, V.tensor_tensor(part_x, part_x, bank(tile), ALU.add))

            def copy(name, dst):
                dve.wait_ge(*O.ready(name))
                src = bank(name)
                if len(dst.shape) == 3:
                    src = src.rearrange("p (a b) -> p a b", a=dst.shape[1])
                drain(name, V.tensor_copy(dst, src))

            def log1p(u, tmp, dst):
                a, s, s2, q = (tmp[:, i, :] for i in range(4))
                step(V.tensor_scalar(a, u, 2.0, None, ALU.add))
                step(V.reciprocal(a, a))
                step(V.tensor_tensor(s, u, a, ALU.mult))
                step(V.tensor_tensor(s2, s, s, ALU.mult))
                step(V.tensor_scalar(q, s2, LOG1P[0], None, ALU.mult))
                for coef in LOG1P[1:]:
                    step(V.scalar_tensor_tensor(q, q, coef, s2, ALU.add, ALU.mult))
                step(V.scalar_tensor_tensor(q, q, 1.0, s, ALU.add, ALU.mult))
                step(V.tensor_scalar(dst, q, 2.0, None, ALU.mult))

            def attention(kind, mask_of, dst):
                K = KINDS[kind]

                def masked(u):
                    tc, col, heads, w = UNITS[u]
                    nh = len(heads)
                    sinks = c("sinks")[:, heads[0]::2][:, 0:nh]
                    if kind == "fox":
                        name = f"fox_b{u}"
                        dve.wait_ge(*O.ready(name))
                        for i, h in enumerate(heads):
                            last = V.scalar_tensor_tensor(fox_d[:, u % 2, i * w:(i + 1) * w], bank(name)[:, i * w:(i + 1) * w],
                                                          fox_c[:, tc, h:h + 1], mask_of(tc), ALU.subtract, ALU.add)
                        drain(name, last)
                        mask = fox_d[:, u % 2, :].rearrange("p (a b) -> p a b", a=nh)
                    else:
                        mask = mask_of(tc).unsqueeze(1).to_broadcast([P, nh, w])
                    name = f"{kind}_l{u}"
                    dve.wait_ge(*O.ready(name))
                    dst_l = lm[:, u % 2, :].rearrange("p (a b) -> p a b", a=nh)
                    drain(name, V.scalar_tensor_tensor(dst_l, bank(name).rearrange("p (a b) -> p a b", a=nh), DH ** -0.5,
                                                       mask, ALU.mult, ALU.add))
                    m = top_max[:, K, col:col + nh]
                    step(V.tensor_reduce(m, dst_l, AX_X, ALU.max))
                    if kind == "swa":
                        step(V.tensor_tensor(m, m, sinks, ALU.max))
                    V.tensor_scalar(neg_max[:, K, col:col + nh], m, -1.0, None, ALU.mult).then_inc(logits_masked, 1)
                    if kind == "swa":
                        V.tensor_tensor(sink_d[:, col:col + nh], sinks, m, ALU.subtract).then_inc(sink_sub, 1)

                def invert(u):
                    tc, col, heads, w = UNITS[u]
                    nh = len(heads)
                    rs = row_sum[:, K, col:col + nh]
                    dve.wait_ge(probs_raw, K * NU + u + 1)
                    if kind == "swa":
                        dve.wait_ge(sink_exp, u + 1)
                        step(V.tensor_tensor(rs, rs, sink_e[:, col:col + nh], ALU.add))
                    V.reciprocal(row_inv[:, K, col:col + nh], rs).then_inc(sums_inverted, 1)

                def mixed(u):
                    tc, _, heads, w = UNITS[u]
                    nh, a = len(heads), DH * (heads[0] % 2)
                    name = f"{kind}_o{u}"
                    dve.wait_ge(*O.ready(name))
                    out_u = dst[a:a + DH, heads[0] // 2:heads[0] // 2 + nh, tc * P:(tc + 1) * P]
                    src = bank(name)[a:a + DH, 0:nh * P].rearrange("p (a b) -> p a b", a=nh)
                    drain(name, V.tensor_copy(out_u, src))

                for u in range(NU + 2):
                    if u < NU:
                        masked(u)
                    if 1 <= u <= NU:
                        invert(u - 1)
                    if u >= 2:
                        mixed(u - 2)

            def ffn(n):
                norm(2 * n + 1)
                base = O.at[f"ffn{n}_11"] + 1
                with dve.Fori(0, NF // 2) as i:
                    for b in range(2):
                        dve.wait_ge(ffn_silu, i * 2 + (n * NF + b + 1))
                        V.tensor_tensor(h_f[:, b, :], sg_f[:, b, :], psum[:, (base + b) % 8, T:2 * T],
                                        ALU.mult).then_inc(ffn_h, 1)
                add_out(f"ffn{n}")

            dve.wait_ge(small_in, 32)
            dve.wait_ge(x_in, 16)
            norm(0)
            copy("iq1", iqT[:, 2:4, :])
            for tc in range(NT):
                name = f"misc{tc}"
                dve.wait_ge(*O.ready(name))
                step(V.tensor_scalar(iw[:, tc, :], bank(name)[:, 256:264], DH ** -0.5 * HEADS ** -0.5, None, ALU.mult))
                step(V.tensor_tensor(dt_in[:, tc, :], bank(name)[:, 264:280], c("dt_bias"), ALU.add))
                drain(name, V.tensor_copy(ckv[:, tc, :], bank(name)[:, 0:256]))
            dt_flat = dt_in.rearrange("p a b -> p (a b)")
            V.scalar_tensor_tensor(sp[:, 0, :], dt_flat, -1.0, dt_flat, ALU.mult, ALU.max).then_inc(sp_abs, 1)
            for tc in range(NT):
                dve.wait_ge(kv_rstd, tc + 1)
                V.tensor_scalar(ckv[:, tc, :], ckv[:, tc, :], rstd_kv[:, tc, :], None, ALU.mult).then_inc(ckv_ready, 1)
            done = set()
            for u, (tc, _, heads, w) in enumerate(UNITS):
                dve.wait_ge(*O.drained(f"il{u}"))
                for i, h in enumerate(heads):
                    sc = score[:, tc, 0:w]
                    step(V.scalar_tensor_tensor(sc, lm[:, u % 2, i * w:(i + 1) * w], iw[:, tc, h:h + 1],
                                                sc if tc in done else causal_mask[tc], ALU.mult, ALU.add))
                    done.add(tc)
                V.engine_nop().then_inc(il_used, 1)
            for tc in range(NT):
                w = UNITS[-1][3] if tc else P
                sc, wk = score[:, tc, 0:w], work[:, tc, 0:w]
                for r in range(TOPK // 8):
                    src = sc if r == 0 else wk
                    step(V.max(top8[:, tc, :], src))
                    step(V.match_replace(wk, top8[:, tc, :], src, TAKEN))
                m = sel_mask[:, tc, 0:w]
                step(V.tensor_scalar(m, wk, TAKEN / 2, NEG, ALU.is_gt, ALU.mult))
                step(V.tensor_tensor(m, m, causal_mask[tc], ALU.add))
            dve.wait_ge(sp_exp, 1)
            log1p(sp[:, 1, :], sp[:, 3:7, :], sp[:, 2, :])
            dt_f = dt.rearrange("p a b -> p (a b)")
            step(V.scalar_tensor_tensor(dt_f, dt_flat, 0.0, sp[:, 2, :], ALU.max, ALU.add))
            dve.wait_ge(a_log_exp, 1)
            V.scalar_tensor_tensor(a_dt[:, :, :], dt[:, :, :], -1.0, neg_A.unsqueeze(1).to_broadcast([P, NT, 16]),
                                   ALU.mult, ALU.mult).then_inc(a_ready, 1)
            for j in range(6):
                dve.wait_ge(*O.drained(f"xb{j}"))
                for tap in range(4):
                    for m in range(2):
                        ch = 2 * j + m
                        src = xp[:, j % 2, m, 3 - tap:259 - tap]
                        wt = c("conv_w", (3 - tap) * NX + ch)
                        if tap == 0:
                            last = V.tensor_scalar(convT[:, ch, :], src, wt, None, ALU.mult)
                        else:
                            last = V.scalar_tensor_tensor(convT[:, ch, :], src, wt, convT[:, ch, :], ALU.mult, ALU.add)
                        if tap == 3 and m == 1:
                            last.then_inc(conv_sum, 1)
                        else:
                            step(last)
            attention("mla", lambda tc: sel_mask[:, tc, 0:(T if tc else P)], mixT[:, 0:4, :])
            for tc in range(NT):
                copy(f"xs{tc}1", xs[:, tc, 512:1024])
            dve.wait_ge(*O.ready("acs"))
            drain("acs", V.tensor_copy(acs[:, :, :], bank("acs")[:, 0:48].rearrange("p (a b) -> p a b", a=3)))
            V.tensor_tensor(sp[:, 2, 0:16], acs[:, 2, :], acs[:, 0, :], ALU.subtract).then_inc(end_sub, 1)

            def seg(i):
                cc, hq = i // 4, i % 4
                name = f"bc{cc}{hq}"
                dve.wait_ge(*O.ready(name))
                if i >= 2:
                    dve.wait_ge(seg_exp, i - 1)
                for k in range(4):
                    h = 4 * hq + k
                    last = V.scalar_tensor_tensor(lm[:, i % 2, k * P:(k + 1) * P], bank(name)[:, k * P:(k + 1) * P],
                                                  acs[:, cc, h:h + 1], c("causal_t"), ALU.subtract, ALU.add)
                drain(name, last)

            gated = [0]

            def gather(cc, g):
                cols = slice(g * 512, (g + 1) * 512)
                y = y_tok[:, cc, cols]
                dve.wait_ge(*O.ready(f"y{cc}{g}"))
                dve.wait_ge(scaled_ready, cc + 1)
                drain(f"y{cc}{g}", V.tensor_tensor(y, bank(f"y{cc}{g}"), xs[:, cc, cols], ALU.add))
                if cc == 1:
                    dve.wait_ge(*O.ready(f"yo{g}"))
                    t = y_part[:, 0, :]
                    dve.wait_ge(decays_ready, 2)
                    drain(f"yo{g}", V.tensor_tensor(t.rearrange("p (a b) -> p a b", a=8),
                                                    bank(f"yo{g}").rearrange("p (a b) -> p a b", a=8),
                                                    acs_exp[:, g * 8:(g + 1) * 8].unsqueeze(2).to_broadcast([P, 8, DH]),
                                                    ALU.mult))
                    step(V.tensor_tensor(y, y, t, ALU.add))
                gated[0] += 1
                V.tensor_tensor(y, y, z[:, cc, cols], ALU.mult).then_inc(y_gated, 1)

            for i in range(4):
                seg(i)
            gather(0, 0)
            seg(4)
            seg(5)
            gather(0, 1)
            seg(6)
            seg(7)
            gather(1, 0)
            gather(1, 1)
            for i in range(4):
                cc, g = i // 2, i % 2
                y = y_tok[:, cc, g * 512:(g + 1) * 512]
                dve.wait_ge(y_rstd, i + 1)
                V.tensor_scalar(y, y, rstd_g[:, cc, g:g + 1], None, ALU.mult).then_inc(y_ready, 1)
            for j in (1, 3):
                dve.wait_ge(*O.ready(f"yT{j}"))
                for kk in range(2):
                    k = 2 * j + kk
                    last = V.tensor_scalar(mixT[:, 4 + k, :], bank(f"yT{j}")[:, kk * T:(kk + 1) * T], c("ssm_norm", k),
                                           None, ALU.mult)
                last.then_inc(dve_drained, 1)
            add_out("out0")
            ffn(0)
            norm(2)
            step(V.memset(cv[:, :, 0:2], 0.0))
            for j in range(KD):
                b = j % 2
                name = f"cv{j}"
                dve.wait_ge(*O.ready(name))
                step(V.tensor_copy(c_sb[:, b, :], bank(name)[:, 0:T]))
                drain(name, V.tensor_tensor(cv[:, b, 2:T + 2], c_sb[:, b, :], bank(name)[:, T:2 * T], ALU.mult))
                step(V.tensor_scalar(sc_conv[:, b, :], cv[:, b, 2:T + 2], c("sc_w", 2 * KD + j), None, ALU.mult))
                for tap in (1, 0):
                    step(V.scalar_tensor_tensor(sc_conv[:, b, :], cv[:, b, tap:tap + T], c("sc_w", tap * KD + j),
                                                sc_conv[:, b, :], ALU.mult, ALU.add))
                dve.wait_ge(*O.ready(f"b{j}"))
                drain(f"b{j}", V.tensor_tensor(scT[:, j, :], sc_conv[:, b, :], bank(f"b{j}")[:, 0:T], ALU.mult))
            add_out("out1")
            ffn(1)
            scaled_norm("first", x_final, 16)
            norm(4)
            step(V.tensor_copy(pos_f, pos[:, :]))
            for tc in range(NT):
                step(V.tensor_scalar(ang[:, tc, :], c("freq"), pos_f[:, tc:tc + 1], None, ALU.mult))
            step(V.tensor_scalar(rope_k[:, :, :], ang[:, :, :], 1 / (2 * np.pi), ROUND, ALU.mult, ALU.add))
            step(V.tensor_scalar(rope_k[:, :, :], rope_k[:, :, :], ROUND, None, ALU.subtract))
            for part_2pi in TWO_PI:
                step(V.scalar_tensor_tensor(ang[:, :, :], rope_k[:, :, :], -part_2pi, ang[:, :, :], ALU.mult, ALU.add))
            step(V.tensor_scalar(red[:, :, :], ang[:, :, :], PI, -PI, ALU.min, ALU.max))
            step(V.scalar_tensor_tensor(cosr[:, :, :], red[:, :, :], -1.0, red[:, :, :], ALU.mult, ALU.max))
            V.tensor_scalar(cosr[:, :, :], cosr[:, :, :], -1.0, float(np.pi / 2), ALU.mult, ALU.add).then_inc(angles, 1)
            copy("fq1", qT[:, 2:4, :])
            copy("fk1", kT[:, 2:4, :])
            dve.wait_ge(*O.drained("misc2_1"))
            f_flat = f_in.rearrange("p a b -> p (a b)")
            step(V.scalar_tensor_tensor(f_neg.rearrange("p (a b) -> p a b", a=NT), f_in[:, :, :], 1.0,
                                        c("b_forget").unsqueeze(1).to_broadcast([P, NT, 8]), ALU.mult, ALU.add))
            step(V.tensor_scalar(f_neg, f_neg, -1.0, None, ALU.mult))
            V.scalar_tensor_tensor(f_tmp[:, 0, :], f_neg, -1.0, f_neg, ALU.mult, ALU.max).then_inc(f_abs, 1)
            dve.wait_ge(f_exp, 1)
            log1p(f_u, f_tmp[:, 0:4, :], f_tmp[:, 4, :])
            V.scalar_tensor_tensor(log_f.rearrange("p a b -> p (a b)"), f_neg, 0.0, f_tmp[:, 4, :], ALU.max,
                                   ALU.add).then_inc(log_f_ready, 1)
            dve.wait_ge(*O.ready("fox_c"))
            drain("fox_c", V.tensor_copy(fox_c[:, :, :], bank("fox_c")[:, 0:16].rearrange("p (a b) -> p a b", a=NT)))
            attention("fox", lambda tc: causal_mask[tc], mixT[:, 0:4, :])
            attention("swa", lambda tc: window_mask[tc], mixT[:, 4:8, :])
            for j in range(4):
                for gi, n in enumerate(("pf", "ps")):
                    dve.wait_ge(*O.ready(f"{n}{j}"))
                    drain(f"{n}{j}", V.tensor_tensor(lm[:, gi, :].rearrange("p (a b) -> p a b", a=2), bank2(f"{n}{j}"),
                                                     gates[:, gi, 2 * j:2 * j + 2, :], ALU.mult))
                V.tensor_tensor(mergedT[:, 2 * j:2 * j + 2, :], lm[:, 0, :].rearrange("p (a b) -> p a b", a=2),
                                lm[:, 1, :].rearrange("p (a b) -> p a b", a=2), ALU.add).then_inc(merged, 1)
                dve.wait_ge(merged, j + 1)
            add_out("out2")
            norm(5)

            def per_token(v, n):
                return v.unsqueeze(2).to_broadcast([P, NT, n])

            def first_max(v, eq, first, m, hot):
                step(V.tensor_reduce(m, v, AX_X, ALU.max))
                step(V.tensor_tensor(eq[:, :, :], v, per_token(m, 8), ALU.is_equal))
                step(V.tensor_tensor(eq[:, :, :], eq[:, :, :], c("down8").unsqueeze(1).to_broadcast([P, NT, 8]), ALU.mult))
                step(V.tensor_reduce(first, eq[:, :, :], AX_X, ALU.max))
                step(V.tensor_tensor(hot[:, :, :], eq[:, :, :], per_token(first, 8), ALU.is_equal))

            for tc in range(NT):
                name = f"router{tc}"
                dve.wait_ge(*O.ready(name))
                drain(name, V.tensor_tensor(r_log[:, tc, :], bank(name)[:, 0:72], c("b_router"), ALU.add))
            g_log = r_log[:, :, 0:8]
            first_max(g_log, g_eq, g_first, g_max, g_hot)
            V.tensor_tensor(g_exp[:, :, :], g_log, per_token(g_max, 8), ALU.subtract).then_inc(r_sub, 1)
            V.engine_nop().then_inc(r_gate, 1)
            for tc in range(NT):
                e8 = e_all.rearrange("p (g e) -> p g e", g=8)
                step(V.tensor_tensor(e8, r_log[:, tc, 8:72].rearrange("p (g e) -> p g e", g=8),
                                     g_hot[:, tc, :].unsqueeze(2).to_broadcast([P, 8, 8]), ALU.mult))
                step(V.tensor_reduce(e_sel[:, tc, :], e_all.rearrange("p (g e) -> p e g", g=8), AX_X, ALU.add))
            first_max(e_sel[:, :, :], e_eq1, e_f1, e_m1, e_hot1)
            step(V.scalar_tensor_tensor(e_rest[:, :, :], e_hot1[:, :, :], NEG, e_sel[:, :, :], ALU.mult, ALU.add))
            first_max(e_rest[:, :, :], e_eq2, e_f2, e_m2, e_hot2)
            V.tensor_tensor(e_d, e_m2, e_m1, ALU.subtract).then_inc(r_sub, 1)
            dve.wait_ge(r_exp, 1)
            step(V.tensor_reduce(g_sum, g_exp[:, :, :], AX_X, ALU.add))
            step(V.reciprocal(g_w, g_sum))
            dve.wait_ge(r_exp, 2)
            step(V.tensor_scalar(e_den, e_x, 1.0, None, ALU.add))
            step(V.reciprocal(e_den, e_den))
            step(V.tensor_tensor(e_w1, e_den, g_w, ALU.mult))
            step(V.tensor_tensor(e_w2, e_w1, e_x, ALU.mult))
            step(V.tensor_tensor(e_hot1[:, :, :], e_hot1[:, :, :], per_token(e_w1, 8), ALU.mult))
            step(V.tensor_tensor(e_hot2[:, :, :], e_hot2[:, :, :], per_token(e_w2, 8), ALU.mult))
            V.tensor_tensor(gate8[:, :, :], e_hot1[:, :, :], e_hot2[:, :, :], ALU.add).then_inc(r_gate, 1)
            dve.wait_ge(*O.ready("rank"))
            step(V.tensor_tensor(rank8[:, :, :], bank("rank")[:, 0:16].rearrange("p (a b) -> p a b", a=NT), g_hot[:, :, :],
                                 ALU.mult))
            drain("rank", V.tensor_reduce(most, bank("rank")[:, 16:24], AX_X, ALU.max))
            step(V.tensor_reduce(rank, rank8[:, :, :], AX_X, ALU.add))
            step(V.tensor_scalar(passes_f, most, float(CAP), 1.0, ALU.is_gt, ALU.add))
            for k in range(2, T // CAP):
                step(V.scalar_tensor_tensor(passes_f, most, float(k * CAP), passes_f, ALU.is_gt, ALU.add))
            V.tensor_copy(passes_i[:, :], passes_f).then_inc(r_pass, 1)
            dve.wait_ge(r_pass, 1)
            passes = dve.value_load(passes_i[0:1, 0:1], min_val=1, max_val=T // CAP)
            moe_at = step.base
            with dve.Fori(0, passes) as p:
                with dve.Fori(0, N_GROUPS) as g:
                    n = dve.snap(p * N_GROUPS + g)
                    n8 = dve.snap(n * PER_GROUP)
                    step.base = n * PER_GROUP + (moe_at)
                    for tc in range(NT):
                        last = V.tensor_scalar(sel_g[:, tc, :], c("iota"), rank[:, tc:tc + 1],
                                               g_hot[:, tc, bass.ds(g, 1)], ALU.is_equal, ALU.mult)
                    last.then_inc(m_sel, 1)
                    dve.wait_ge(m_xg, n + 1)
                    V.tensor_tensor(xg[:, :, :], psum[:, XG_BANK, :].rearrange("p (a b) -> p a b", a=KD),
                                    c("moe_norm").unsqueeze(2).to_broadcast([P, KD, CAP]), ALU.mult).then_inc(m_xg_sb, 1)
                    dve.wait_ge(m_gate_sb, n + 1)
                    for e in range(PER_GROUP):
                        dve.wait_ge(m_silu, n8 + e + 1)
                        hh = hh_e[:, e % 2, :]
                        step(V.tensor_tensor(hh, sg_e[:, e % 2, :], psum[:, H_BANK[e % 2], NE * CAP:], ALU.mult))
                        V.tensor_tensor(hg_e[:, e % 2, :].rearrange("p (a b) -> p a b", a=NE),
                                        hh.rearrange("p (a b) -> p a b", a=NE),
                                        gate_g[:, e, :].unsqueeze(1).to_broadcast([P, NE, CAP]), ALU.mult).then_inc(m_hg, 1)
                    for i, (tc, h) in enumerate(RES):
                        dve.wait_ge(m_sc, n * 4 + i + 1)
                        part_x = x[:, tc, h * 512:(h + 1) * 512]
                        V.tensor_tensor(part_x, part_x, psum[:, S_BANK[i], :], ALU.add).then_inc(m_scd, 1)
                rank_at = p + 1
                V.tensor_scalar(rank, rank, float(CAP), None, ALU.subtract).then_inc(scaled_ready, 1)
                dve.wait_ge(scaled_ready, rank_at + NT)
            dve.wait_ge(m_scd, passes * (4 * N_GROUPS))
            V.tensor_copy(total[:, 0:NT], rank).then_inc(moe_done, 1)
            scaled_norm("last", out_ready, 32)

        @block.gpsimd
        def _(pool):
            G = nc.gpsimd
            step = Steps(pool, pool_step)

            def inverse_root(total_, mean_, out_, size, done):
                step(G.tensor_scalar(mean_, total_, 1.0 / size, EPS, ALU.mult, ALU.add))
                G.tensor_tensor(out_, mean_, c("half", 0), ALU.pow).then_inc(done, 1)

            def norm(n):
                for tc in range(NT):
                    r = NORMS[n]
                    pool.wait_ge(squares, NT * r + tc + 1)
                    inverse_root(ss[:, r, tc:tc + 1], mean[:, r, tc:tc + 1], rstd[:, r, tc:tc + 1], D, rstd_ready)

            def attention(kind):
                K = KINDS[kind]
                for u, (tc, at, heads, w) in enumerate(UNITS):
                    pool.wait_ge(sums_inverted, K * NU + u + 1)
                    for i in range(len(heads)):
                        col = at + i
                        pu = pr[:, u % 2, i * w:(i + 1) * w]
                        last = G.tensor_scalar(pu, pu, row_inv[:, K, col:col + 1], None, ALU.mult)
                    last.then_inc(probs_ready, 1)

            pool.wait_ge(small_in, 32)
            norm(0)
            for tc in range(NT):
                pool.wait_ge(kv_sq, tc + 1)
                inverse_root(ss_kv[:, tc, :], mean_kv[:, tc, :], rstd_kv[:, tc, :], LATENT, kv_rstd)
            pool.wait_ge(*O.ready("il5"))
            G.memset(xp[:, :, :, 0:3], 0.0).then_inc(pads_zero, 1)
            attention("mla")
            pool.wait_ge(*O.drained("xs10"))
            pool.wait_ge(*O.drained("xs11"))

            def by_head(v):
                return v.rearrange("p (h d) -> p h d", d=DH)

            def spread(v, h=SSM_HEADS):
                return v.unsqueeze(2).to_broadcast([P, h, DH])

            for tc in range(NT):
                G.tensor_tensor(by_head(xdt[:, tc, :]), by_head(xs[:, tc, :]), spread(dt[:, tc, :]),
                                ALU.mult).then_inc(xdt_ready, 1)
            pool.wait_ge(decays_ready, 1)
            pool.wait_ge(xdt_ready, 2)
            G.tensor_tensor(by_head(xdt_end[:, :]), by_head(xdt[:, 0, :]), spread(end_exp), ALU.mult).then_inc(xdt_ready, 1)

            def decayed(i):
                cc, hq = i // 4, i % 4
                pool.wait_ge(seg_exp, i + 1)
                if i == 0:
                    pool.wait_ge(*O.drained("cbT"))
                if i >= 2:
                    pool.wait_ge(*y_rows_used(i - 2))
                G.tensor_tensor(pT[:, i % 2, :].rearrange("p (a b) -> p a b", a=4),
                                pr[:, i % 2, :].rearrange("p (a b) -> p a b", a=4),
                                cbT[:, 2 * cc + hq // 2, :].unsqueeze(1).to_broadcast([P, 4, P]), ALU.mult).then_inc(ssm_w, 1)

            decayed(0)
            decayed(1)
            for tc in range(NT):
                G.tensor_tensor(by_head(xs[:, tc, :]), by_head(xs[:, tc, :]), spread(c("Dskip")),
                                ALU.mult).then_inc(scaled_ready, 1)
            for i in range(2, 8):
                decayed(i)
            for i in range(4):
                cc, g = i // 2, i % 2
                pool.wait_ge(y_sq, i + 1)
                inverse_root(ssg[:, cc, g:g + 1], mean_g[:, cc, g:g + 1], rstd_g[:, cc, g:g + 1], SSM_IN // 2, y_rstd)
            norm(1)
            norm(2)
            norm(3)
            norm("first")
            norm(4)
            pool.wait_ge(sincos, 2)
            for tc in range(NT):
                pool.wait_ge(*O.drained(f"sq{tc}"))
                v = rope_x[:, tc, :].rearrange("p (h a b) -> p h a b", a=2, b=DH // 2)
                ra = rope_a.rearrange("p (h a b) -> p h a b", a=2, b=DH // 2)
                rb = rope_b.rearrange("p (h a b) -> p h a b", a=2, b=DH // 2)
                co = cos_t[:, tc, :].unsqueeze(1).to_broadcast([P, 10, DH // 2])
                si = sin_t[:, tc, :].unsqueeze(1).to_broadcast([P, 10, DH // 2])
                for a in range(2):
                    step(G.tensor_tensor(ra[:, :, a, :], v[:, :, a, :], co, ALU.mult))
                    step(G.tensor_tensor(rb[:, :, a, :], v[:, :, 1 - a, :], si, ALU.mult))
                step(G.tensor_tensor(v[:, :, 0, :], ra[:, :, 0, :], rb[:, :, 0, :], ALU.subtract))
                G.tensor_tensor(v[:, :, 1, :], ra[:, :, 1, :], rb[:, :, 1, :], ALU.add).then_inc(roped, 1)
                pool.wait_ge(roped, tc + 1)
            attention("fox")
            attention("swa")
            norm(5)
            pool.wait_ge(moe_done, 1)
            norm("last")


IN_NAMES = ["small", "x", "positions", "w_router", "in_w", "misc", "w_uk", "w_uv", "out_w0", "gate0", "up0", "down0",
            "l1_in", "out_w1", "gate1", "up1", "down1", "final_norm", "w_in2", "misc2", "proj_fox", "proj_swa", "out_w2",
            "final_norm2", "w1", "w3", "w2"]


def layout(i):
    def chunked(w):
        return w.reshape(P, KD, -1, P).transpose(2, 0, 1, 3)

    def all_rows(v):
        return np.broadcast_to(v.reshape(1, -1), (P, v.size))

    def chan(v):
        return v.reshape(-1, P).T

    q, kk = np.arange(P)[:, None], np.arange(P)[None, :]
    neg = np.float32(NEG)
    causal = np.where(kk <= q, np.float32(0), neg)
    parts = {
        "ident": q == kk, "tri": q <= kk, "strict": q < kk, "ones": np.ones((P, P)), "open": np.zeros((P, P)),
        "causal": causal, "band": np.where(kk > q, np.float32(0), neg), "causal2": causal, "causal_t": causal.T,
        "iota": all_rows(np.arange(CAP)), "down8": all_rows(8 - np.arange(8)),
        "freq": all_rows(np.float32(10000.0) ** (-np.arange(32, dtype=np.float32) * np.float32(2) / np.float32(64))),
        "half": np.full((P, 8), -0.5),
        "attn_norm": i["l0_attn_norm"].reshape(P, KD), "ffn_norm": i["l0_ffn_norm"].reshape(P, KD),
        "l1_norm": i["l1_conv_norm"].reshape(P, KD), "ffn1_norm": i["l1_ffn_norm"].reshape(P, KD),
        "attn2_norm": i["attn_norm_2"].reshape(P, KD), "moe_norm": i["ffn_norm_2"].reshape(P, KD),
        "kv_norm": chan(i["l0_kv_norm"]),
        "conv_w": i["l0_conv_w"].reshape(4 * NX, P).T, "conv_b": chan(i["l0_conv_b"]),
        "dt_bias": all_rows(i["l0_dt_bias"]), "A_log": all_rows(i["l0_A_log"]), "Dskip": all_rows(i["l0_D"]),
        "ssm_norm": chan(i["l0_ssm_norm"]), "sc_w": i["l1_conv_w"].reshape(3 * KD, P).T,
        "b_forget": all_rows(i["b_forget_2"]), "b_gate": i["b_gate_2"].reshape(2 * KD, P).T,
        "sinks": all_rows(i["attn_sinks_2"]),
        "b_router": all_rows(np.concatenate([i["b_group_2"].ravel(), i["b_expert_2"].ravel()])),
    }
    small = np.empty((P, N_SMALL), np.float32)
    for name, (at, width) in AT.items():
        small[:, at:at + width] = parts[name]
    in_w, w_in2 = i["l0_in_w"], i["w_in_2"][0]
    l1 = i["l1_in_w"].reshape(P, KD, 3, KD, P)[:, :, [1, 2, 0]].transpose(3, 0, 1, 2, 4)
    return {
        "small": small,
        "x": i["x"][0],
        "positions": i["positions_2"].reshape(NT, P).T,
        "w_router": np.concatenate([i["w_group_2"][0], i["w_expert_2"][0]], axis=1),
        "in_w": in_w,
        "misc": np.concatenate([in_w[:, 512:768], in_w[:, 1344:1352], in_w[:, 3912:3928], in_w[:, 1280:1344]], axis=1),
        "w_uk": i["l0_w_uk"].transpose(2, 0, 1).reshape(LATENT, 512),
        "w_uv": i["l0_w_uv"].transpose(1, 0, 2).reshape(LATENT, 512),
        "out_w0": i["l0_out_w"],
        "gate0": chunked(i["l0_w_gate"]), "up0": chunked(i["l0_w_up"]), "down0": i["l0_w_down"].reshape(NF, P, D),
        "l1_in": l1.reshape(KD, P, 3 * KD * P),
        "out_w1": i["l1_out_w"],
        "gate1": chunked(i["l1_w_gate"]), "up1": chunked(i["l1_w_up"]), "down1": i["l1_w_down"].reshape(NF, P, D),
        "final_norm": i["final_norm"].reshape(1, D),
        "w_in2": w_in2,
        "misc2": np.concatenate([w_in2[:, 1536:1544], w_in2[:, 2056:2312]], axis=1),
        "proj_fox": i["w_proj_fox_2"][0], "proj_swa": i["w_proj_swa_2"][0], "out_w2": i["w_out_2"][0],
        "final_norm2": i["final_norm_2"].reshape(1, D),
        "w1": i["w1_2"].reshape(N_EXPERTS, P, KD * D_EXPERT), "w3": i["w3_2"].reshape(N_EXPERTS, P, KD * D_EXPERT),
        "w2": i["w2_2"].reshape(N_EXPERTS * NE, P, D),
    }


def kernel(**inputs):
    import concourse.bacc as bacc
    from concourse.bass_utils import run_bass_kernel_spmd

    given = {name: np.asarray(a) for name, a in inputs.items()}
    arrays = {name: np.ascontiguousarray(a) for name, a in layout(given).items()}
    nc = bacc.Bacc("TRN2", target_bir_lowering=False, num_devices=1)
    d = {name: nc.dram_tensor(f"in_{name}", arrays[name].shape, mybir.dt.from_np(arrays[name].dtype),
                              kind="ExternalInput").ap() for name in IN_NAMES}
    out = nc.dram_tensor("out", (T, D), F32, kind="ExternalOutput").ap()
    program(nc, d, out)
    r = run_bass_kernel_spmd(nc, [{f"in_{name}": arrays[name] for name in IN_NAMES}], core_ids=[0])
    return np.asarray(r.results[0]["out"]).reshape(1, T, D)
```

```python
from contextlib import ExitStack

import numpy as np

import concourse.bass as bass
from concourse import mybir

F32 = mybir.dt.float32
F32R = mybir.dt.float32r
I32 = mybir.dt.int32
ALU = mybir.AluOpType
ACT = mybir.ActivationFunctionType
AX_X = mybir.AxisListType.X

P = 128
T = 256
NT = T // P
D = 1024
KD = D // P
EPS = 1e-6
NEG = -1e30
TAKEN = -3e38

HEADS = 8
DH = 64
LATENT = 256
TOPK = 64
SSM_HEADS = 16
SSM_IN = 1024
D_STATE = 128
CONV_CH = 1536
NX = CONV_CH // P
D_FF = 2816
NF = D_FF // P
N_GROUPS = 8
PER_GROUP = 8
N_EXPERTS = 64
D_EXPERT = 512
NE = D_EXPERT // P
CAP = 128

SLOTS = 6
SLOT = 4096
HI_SLOTS = 3
FFN_RING = 4
FFN_WORDS = 3072
PI = 3.1415925
TWO_PI = (6.28125, 0.0019350051879882812, 3.019915981956753e-07)
ROUND = 12582912.0
ARENA = 18176
STAT = 1056
LOG1P = [1 / (2 * k + 1) for k in range(8, 0, -1)]

UNITS = [(0, 0, (0, 2, 4, 6), P), (0, 4, (1, 3, 5, 7), P),
         (1, 8, (0, 2), T), (1, 10, (1, 3), T), (1, 12, (4, 6), T), (1, 14, (5, 7), T)]

SMALL = [
    ("ident", P), ("tri", P), ("strict", P), ("ones", P), ("open", P), ("causal", P), ("band", P), ("causal2", P),
    ("causal_t", P), ("iota", CAP), ("down8", N_GROUPS), ("freq", DH // 2), ("half", 8),
    ("attn_norm", KD), ("ffn_norm", KD), ("l1_norm", KD), ("ffn1_norm", KD), ("attn2_norm", KD), ("moe_norm", KD),
    ("kv_norm", 2), ("conv_w", 4 * NX), ("conv_b", NX), ("dt_bias", 16), ("A_log", 16), ("Dskip", 16),
    ("ssm_norm", KD), ("sc_w", 3 * KD), ("b_forget", 8), ("b_gate", 2 * KD), ("sinks", 8), ("b_router", 72),
]
AT = {}
_at = 0
for _name, _width in SMALL:
    AT[_name] = (_at, _width)
    _at += _width
N_SMALL = _at


class PsumOrder:

    def __init__(self, tile_ready, act_drained, dve_drained):
        self.tile_ready = tile_ready
        self.sem = {"act": act_drained, "dve": dve_drained}
        self.at, self.info, self.count = {}, [], {"act": 0, "dve": 0}
        self.n = 0

    def add(self, name, drainer):
        assert name not in self.at, name
        self.at[name] = len(self.info)
        self.n += 1
        self.count[drainer] += 1
        self.info.append((name, drainer, self.n, self.count[drainer]))

    def skip(self):
        self.info.append(None)

    def bank(self, name):
        return self.at[name] % 8

    def ready(self, name):
        return self.tile_ready, self.info[self.at[name]][2]

    def drained(self, name):
        _, drainer, _, k = self.info[self.at[name]]
        return self.sem[drainer], k

    def bank_free(self, name):
        before = self.at[name] - 8
        if before < 0 or self.info[before] is None:
            return None
        return self.drained(self.info[before][0])


class WeightRing:

    def __init__(self, landed):
        self.landed_sem = landed
        self.next = 0
        self.dmas = [0] * SLOTS
        self.last = [None] * SLOTS
        self.unit = {}

    def add(self, name, n_dma, release, slot=None):
        if slot is None:
            slot, self.next = self.next % SLOTS, self.next + 1
        before = self.last[slot]
        self.dmas[slot] += n_dma
        self.unit[name] = (slot, before, 16 * self.dmas[slot])
        self.last[slot] = release
        return slot

    def slot(self, name):
        return self.unit[name][0]

    def landed(self, name):
        slot, _, value = self.unit[name]
        return self.landed_sem[slot], value

    def vacated(self, name):
        return self.unit[name][1]


class SplitOrder:

    def __init__(self, high, low):
        self.high_sem, self.low_sem = high, low
        self.unit = {}

    def add(self, name, at, words, release):
        before = [r for a, w, r in self.places() if a < at + words and at < a + w]
        self.unit[name] = (len(self.unit) + 1, at, words, release, before)

    def places(self):
        return [(at, words, release) for _, at, words, release, _ in self.unit.values()]

    def high(self, name):
        return self.high_sem, self.unit[name][0]

    def low(self, name):
        return self.low_sem, self.unit[name][0]

    def vacated(self, name):
        last = {}
        for semaphore, value in self.unit[name][4]:
            at = max(value, last[semaphore.name][1]) if semaphore.name in last else value
            last[semaphore.name] = (semaphore, at)
        return list(last.values())


class Steps:

    def __init__(self, eng, sem):
        self.eng, self.sem, self.base = eng, sem, 0

    def __call__(self, ins):
        self.base = self.base + 1
        ins.then_inc(self.sem, 1)
        self.eng.wait_ge(self.sem, self.base)


def program(nc, d, out):
    with ExitStack() as ctx:
        def sb(name, shape, dt=F32):
            return ctx.enter_context(nc.sbuf_tensor(name, shape, dt))

        def sem(name):
            return ctx.enter_context(nc.semaphore(name))

        small = sb("small", [P, N_SMALL])
        pos = sb("pos", [P, NT], I32)
        passes_i = sb("passes_i", [P, 1], I32)
        x = sb("x", [P, NT, D])
        xn = sb("xn", [P, NT, D])
        norm_row = sb("norm_row", [P, D])
        stat = sb("stat", [P, STAT])
        w_router = sb("w_router", [P, KD, 72])

        with ExitStack() as float32_names:
            ring, xnT, arena = [float32_names.enter_context(nc.sbuf_tensor(name, shape, F32)) for name, shape in (
                ("ring", [P, SLOTS, SLOT]), ("xnT", [P, KD, T]), ("arena", [P, ARENA]))]
        ring_r = [sb(f"ring_r{i}", [P, SLOT], F32R) for i in range(SLOTS)]
        xnT_r, arena_r = sb("xnT_r", [P, KD, T], F32R), sb("arena_r", [P, ARENA], F32R)

        def part(of, at, shape):
            n = int(np.prod(shape))
            assert at + n <= of.shape[-1], (at, shape)
            v = of[:, at:at + n]
            if len(shape) == 2:
                v = v.rearrange("p (a b) -> p a b", a=shape[0])
            if len(shape) == 3:
                v = v.rearrange("p (a b c) -> p a b c", a=shape[0], b=shape[1])
            return v

        arena_at, stat_at = [0], [0]

        def carve(*shape, of=arena):
            v = part(of, arena_at[0], shape)
            arena_at[0] += int(np.prod(shape))
            return v

        def few(*shape):
            v = part(stat, stat_at[0], shape)
            stat_at[0] += int(np.prod(shape))
            return v

        def c(name, a=None, b=None):
            at, width = AT[name]
            a, b = (0, width) if a is None else (a, a + 1 if b is None else b)
            return small[:, at + a:at + b]

        ident, tri, strict, ones = c("ident"), c("tri"), c("strict"), c("ones")

        def two(name):
            return small[:, AT[name][0]:AT[name][0] + T]

        causal_mask = [c("causal"), two("open")]
        window_mask = [c("causal"), two("band")]

        ss, mean, rstd = few(8, NT), few(8, NT), few(8, NT)
        top_max = few(3, 2 * HEADS)
        neg_max = few(3, 2 * HEADS)
        row_sum = few(3, 2 * HEADS)
        row_inv = few(3, 2 * HEADS)

        qT, kT, v_tok = carve(4, T), carve(4, T), carve(NT, 512)
        lm, pr, pT = carve(2, 512), carve(2, 512), carve(2, 512)
        mixT = carve(12, T)
        shared = arena_at[0]
        iqT, ikT = carve(4, T), carve(T)
        xp = part(arena, shared, (2, 2, 259))
        sel_mask, ckvT, ckv = carve(NT, T), carve(2, T), carve(NT, LATENT)
        score, work = carve(NT, T), carve(NT, T)
        z, convT = carve(NT, D), carve(NX, T)
        y_tok = xn
        xs = xnT[:, :, :].rearrange("p k t -> p (k t)").rearrange("p (a b) -> p a b", a=NT)
        xdt = convT[:, 0:8, :].rearrange("p k t -> p (k t)").rearrange("p (a b) -> p a b", a=NT)
        xdt_end = norm_row
        state = qT.rearrange("p a b -> p (a b)").rearrange("p (g n) -> p g n", g=2)
        cbT = kT.rearrange("p a b -> p (a b)")[:, 0:512].rearrange("p (a b) -> p a b", a=4)
        B_tok = kT.rearrange("p a b -> p (a b)")[:, 512:768].rearrange("p (a b) -> p a b", a=2)
        y_part = v_tok
        iw, dt_in, dt, a_dt = few(NT, 8), few(NT, 16), few(NT, 16), few(NT, 16)
        neg_A = few(16)
        acs, acs_exp, end_exp = few(3, 16), few(16), few(16)
        top8 = few(NT, 8)
        sp = few(7, NT * 16)
        ssg, mean_g, rstd_g = few(NT, 2), few(NT, 2), few(NT, 2)
        ss_kv, mean_kv, rstd_kv = few(NT, 1), few(NT, 1), few(NT, 1)

        arena_at[0] = 0
        xn_lo = carve(KD, T, of=arena_r)
        sg_f, h_f, h_hi, h_lo = carve(2, T), carve(2, T), carve(2, T, of=arena_r), carve(2, T, of=arena_r)
        arena_at[0] = KD * T
        c_sb, cv, sc_conv = carve(2, T), carve(2, T + 2), carve(2, T)
        sc_hi, sc_lo = carve(KD, T, of=arena_r), carve(KD, T, of=arena_r)
        HIGH = [ARENA - FFN_WORDS * (i + 1) for i in range(FFN_RING)]
        HIGH_OUT1 = [HIGH[2], ARENA - SLOT]

        arena_at[0] = shared
        arena_at[0] = shared - 4 * T
        sqT, skT, sv = carve(4, T), carve(2, T), carve(NT, P)
        rope_x, rope_a, rope_b = carve(NT, 640), carve(640), carve(640)
        fox_d = carve(2, 512)
        gates = carve(2, KD, T)
        mergedT = xn[:, :, :].rearrange("p a b -> p (a b)").rearrange("p (k t) -> p k t", k=KD)
        stat_mark = stat_at[0]
        stat_at[0] = 240
        f_in, log_f, fox_c, f_neg, f_u, f_tmp = few(NT, 8), few(NT, 8), few(NT, 8), few(NT * 8), few(NT * 8), few(5, NT * 8)
        pos_f, rope_k = few(NT), few(NT, 32)
        ang, red, cosr = few(NT, 32), few(NT, 32), few(NT, 32)
        sin_t, cos_t = few(NT, 32), few(NT, 32)
        sink_d, sink_e = few(2 * HEADS), few(2 * HEADS)

        arena_at[0] = 0
        w_hi = carve(HI_SLOTS, SLOT, of=arena_r)
        sel_g = carve(NT, CAP)
        sel_gT = carve(T, of=arena_r)
        h_e = carve(2, D_EXPERT)
        hT_hi, hT_lo = carve(2, D_EXPERT, of=arena_r), carve(2, D_EXPERT, of=arena_r)
        y_hi, y_lo = carve(D, of=arena_r), carve(D, of=arena_r)
        flat = xnT_r[:, :, :].rearrange("p k t -> p (k t)")
        xg_hi, xg_lo = flat[:, 0:KD * CAP], flat[:, KD * CAP:2 * KD * CAP]
        stat_at[0] = 48
        r_log = few(NT, 72)
        gate_g = few(PER_GROUP)
        g_max, g_exp, g_sum, g_w = few(NT), few(NT, 8), few(NT), few(NT)
        g_eq, g_first, g_hot_9 = few(NT, 8), few(NT), few(NT, 9)
        g_hot = g_hot_9[:, :, 0:8]
        e_all, e_sel = few(64), few(NT, 8)
        e_m1, e_eq1, e_f1, e_hot1 = few(NT), few(NT, 8), few(NT), few(NT, 8)
        e_rest, e_m2, e_eq2, e_f2, e_hot2 = few(NT, 8), few(NT), few(NT, 8), few(NT), few(NT, 8)
        e_d, e_x, e_den, e_w1, e_w2 = few(NT), few(NT), few(NT), few(NT), few(NT)
        gate8, rank8, rank = few(NT, 8), few(NT, 8), few(NT)
        total, most, over, passes_f = few(8), few(1), few(1), few(1)

        psum = ctx.enter_context(nc.psum_tensor("psum", [P, 8, 512], F32))

        small_in, x_in, row_in, router_in = sem("small_in"), sem("x_in"), sem("row_in"), sem("router_in")
        landed = [sem(f"landed{i}") for i in range(SLOTS)]
        tile_ready, act_drained, dve_drained = sem("tile_ready"), sem("act_drained"), sem("dve_drained")
        act_step, dve_step, pool_step = sem("act_step"), sem("dve_step"), sem("pool_step")
        squares, rstd_ready, xn_ready = sem("squares"), sem("rstd_ready"), sem("xn_ready")
        part_used = sem("part_used")
        kv_sq, kv_rstd, ckv_ready = sem("kv_sq"), sem("kv_rstd"), sem("ckv_ready")
        pads_zero = sem("pads_zero")
        logits_masked, probs_raw, sums_inverted, probs_ready = (
            sem("logits_masked"), sem("probs_raw"), sem("sums_inverted"), sem("probs_ready"))
        conv_sum, conv_done = sem("conv_sum"), sem("conv_done")
        il_used, ssm_y, end_sub = sem("il_used"), sem("ssm_y"), sem("end_sub")
        sp_abs, sp_exp, a_ready, a_log_exp = sem("sp_abs"), sem("sp_exp"), sem("a_ready"), sem("a_log_exp")
        xdt_ready, decays_ready = sem("xdt_ready"), sem("decays_ready")
        seg_ready, seg_exp, ssm_w = sem("seg_ready"), sem("seg_exp"), sem("ssm_w")
        state_ready, y_sq, y_rstd, y_ready = sem("state_ready"), sem("y_sq"), sem("y_rstd"), sem("y_ready")
        f_abs, f_exp, log_f_ready = sem("f_abs"), sem("f_exp"), sem("log_f_ready")
        angles, sincos, roped = sem("angles"), sem("sincos"), sem("roped")
        sink_sub, sink_exp = sem("sink_sub"), sem("sink_exp")
        merged = sem("merged")
        ffn_in, ffn_silu, ffn_h, ffn_part = sem("ffn_in"), sem("ffn_silu"), sem("ffn_h"), sem("ffn_part")
        h_made, h_rounded, sc_split = sem("h_made"), sem("h_rounded"), sem("sc_split")
        x_high, w_high, w_low = sem("x_high"), sem("w_high"), sem("w_low")
        sc_ready, x_final, scaled_ready = sem("sc_ready"), sem("x_final"), sem("scaled_ready")
        y_gated = sem("y_gated")
        r_sub, r_exp, r_gate, r_pass = sem("r_sub"), sem("r_exp"), sem("r_gate"), sem("r_pass")
        x_rows, m_sel, m_xg, m_xg_hi, m_xg_lo = sem("x_rows"), sem("m_sel"), sem("m_xg"), sem("m_xg_hi"), sem("m_xg_lo")
        m_small, m_selT, m_gate = sem("m_small"), sem("m_selT"), sem("m_gate")
        m_hi, m_lo, m_unit, m_silu, m_h = sem("m_hi"), sem("m_lo"), sem("m_unit"), sem("m_silu"), sem("m_h")
        m_turned, m_hT_hi, m_hT_lo = sem("m_turned"), sem("m_hT_hi"), sem("m_hT_lo")
        m_y_hi, m_y_lo, m_sc, m_scd = sem("m_y_hi"), sem("m_y_lo"), sem("m_sc"), sem("m_scd")
        moe_done, out_ready, out_sent = sem("moe_done"), sem("out_ready"), sem("out_sent")

        O = PsumOrder(tile_ready, act_drained, dve_drained)
        SPLIT_NORMS = {1: 0, 2: 1, 3: 2}
        RES = [(tc, h) for tc in range(NT) for h in range(2)]

        def plan_norm(n):
            for j in range(4):
                O.add(f"norm{n}_{j}", "dve" if n in SPLIT_NORMS or j % 2 else "act")

        def plan_attention(kind, before=lambda u: None):
            for u in range(len(UNITS) + 2):
                if u < len(UNITS):
                    before(u)
                    O.add(f"{kind}_l{u}", "dve")
                if 1 <= u <= len(UNITS):
                    O.add(f"{kind}_t{u - 1}", "act")
                if u >= 2:
                    O.add(f"{kind}_o{u - 2}", "dve")

        def plan_out(name):
            for tc, h in RES:
                O.add(f"{name}_{tc}{h}", "dve")

        def plan_ffn(n):
            plan_norm(2 * n + 1)
            plan_out(f"ffn{n}")
            O.skip()
            O.skip()

        plan_norm(0)
        for j in range(2):
            O.add(f"iq{j}", "act" if j == 0 else "dve")
        O.add("ik", "act")
        for tc in range(NT):
            O.add(f"misc{tc}", "dve")
        for u in range(len(UNITS)):
            O.add(f"il{u}", "act")
        for j in range(2):
            O.add(f"q{j}", "act")
        for j in range(NX // 2):
            O.add(f"xb{j}", "act")
        for h in range(2):
            for tc in range(NT):
                O.add(f"z{tc}{h}", "act")
        O.add("ckvT", "act")
        for j in range(2):
            O.add(f"k{j}", "act")
        for s in range(NT):
            O.add(f"v{s}", "act")
        plan_attention("mla")
        for tc in range(NT):
            for h in range(2):
                O.add(f"xs{tc}{h}", "act" if h == 0 else "dve")
        O.add("B_tok", "act")
        O.add("cbT", "act")
        O.add("acs", "dve")
        for name, drainer in (("bc00", "dve"), ("bc01", "dve"), ("st0", "act"), ("st1", "act"), ("bc02", "dve"),
                              ("bc03", "dve"), ("y00", "dve"), ("bc10", "dve"), ("bc11", "dve"), ("y01", "dve"),
                              ("bc12", "dve"), ("bc13", "dve"), ("y10", "dve"), ("yo0", "dve"), ("y11", "dve"),
                              ("yo1", "dve")):
            O.add(name, drainer)
        for j in range(4):
            O.add(f"yT{j}", "act" if j % 2 == 0 else "dve")
        plan_out("out0")
        plan_ffn(0)
        plan_norm(2)
        for j in range(KD):
            O.add(f"cv{j}", "dve")
            O.add(f"b{j}", "dve")
        plan_out("out1")
        plan_ffn(1)
        plan_norm(4)
        for n in ("fq", "fk"):
            for j in range(2):
                O.add(f"{n}{j}", "act" if j == 0 else "dve")
        for tc in range(NT):
            O.add(f"fv{tc}", "act")
        for tc in range(NT):
            O.add(f"misc2_{tc}", "act")
        for tc in range(NT):
            O.add(f"sq{tc}", "act")
        for n in ("gf", "gs"):
            for j in range(4):
                O.add(f"{n}{j}", "act")
        O.add("fox_c", "dve")
        plan_attention("fox", lambda u: O.add(f"fox_b{u}", "dve"))
        for j in range(2):
            O.add(f"sqT{j}", "act")
        O.add("skT", "act")
        plan_attention("swa")
        for j in range(4):
            O.add(f"pf{j}", "dve")
            O.add(f"ps{j}", "dve")
        plan_out("out2")
        plan_norm(5)
        for tc in range(NT):
            O.add(f"router{tc}", "dve")
        O.add("rank", "dve")

        W = WeightRing(landed)
        for n, last in (("iq", "iq1"), ("misc", "misc1"), ("q", "q1"), ("xb0", "xb1"), ("xb1", "xb3"), ("xb2", "xb5"),
                        ("z0", "z10"), ("z1", "z11")):
            W.add(n, 1, O.ready(last))
        W.add("kv", 2, O.ready("v1"))
        parts = [0]

        def part_release():
            parts[0] += 1
            return part_used, parts[0]

        def plan_rows(name, n, tiles):
            for i in range(n):
                W.add(f"{name}w{i}", 1, O.ready(f"{tiles}_11") if i == n - 1 else part_release())

        plan_rows("out0", 3, "out0")
        FFN_SLOT, FFN_HIGH = {}, {0: HIGH, 1: [HIGH[2], HIGH[0], HIGH[1], HIGH[3]]}
        S = SplitOrder(w_high, w_low)

        def plan_ffn_weights(n):
            for j in range(NF):
                first = W.next
                slot = (first + j % FFN_RING) % SLOTS
                release = (ffn_part, n * (NF - 1) + j + 1) if j < NF - 1 else O.ready(f"ffn{n}_11")
                W.add(f"ffn{n}_{j}", 3, release, slot)
                S.add(f"ffn{n}_{j}", FFN_HIGH[n][j % FFN_RING], FFN_WORDS, release)
            FFN_SLOT[n] = [(W.next + b) % SLOTS for b in range(FFN_RING)]
            W.next += FFN_RING

        plan_ffn_weights(0)
        for j in range(KD):
            W.add(f"l1_{j}", 1, O.ready(f"b{j}"))
            S.add(f"l1_{j}", HIGH[(j + 2) % 3], FFN_WORDS, O.ready(f"b{j}"))
        plan_rows("out1", 2, "out1")
        for i in range(2):
            S.add(f"out1w{i}", HIGH_OUT1[i], SLOT, W.last[W.slot(f"out1w{i}")])
        plan_ffn_weights(1)
        for n, last in (("fq", "fq1"), ("fk", "fk1"), ("fv", "fv1"), ("misc2", "misc2_1"), ("sq", "sq1"),
                        ("gf0", "gf1"), ("gf1", "gf3"), ("gs0", "gs1"), ("gs1", "gs3"), ("pf", "pf3"), ("ps", "ps3")):
            W.add(n, 1, O.ready(last))
        plan_rows("out2", 2, "out2")
        MOE = []
        for e in range(PER_GROUP):
            MOE += [("w1", e), ("w3", e)] + ([("w2", e - 1)] if e else [])
        MOE.append(("w2", PER_GROUP - 1))
        assert len(MOE) == 3 * PER_GROUP and len(MOE) % SLOTS == 0
        MOE_SLOT = [(W.next + u) % SLOTS for u in range(len(MOE))]
        MOE_BEFORE = [W.last[s] for s in MOE_SLOT[:SLOTS]]
        MOE_BASE = [W.dmas[s] * 16 for s in MOE_SLOT]
        PER_SLOT = len(MOE) // SLOTS
        NM = len(MOE)

        def slot8(s, n=512):
            return ring[:, s, 0:KD * n].rearrange("p (k n) -> p k n", k=KD)

        def bank(name):
            return psum[:, O.bank(name), :]

        def bank2(name, w=T):
            return bank(name)[:, 0:2 * w].rearrange("p (a b) -> p a b", a=2)

        block = ctx.enter_context(nc.Block())

        def high_half(name):
            at, words = S.unit[name][1:3]
            return arena_r[:, at:at + words]

        def unit_rows(name):
            return ring[:, W.slot(name), :].rearrange("p (k n) -> p k n", k=4)

        def y_rows_used(i):
            cc, hq = i // 4, i % 4
            return O.ready(f"y{cc}{hq // 2}") if hq % 2 else (ssm_y, 2 * cc + hq // 2 + 1)

        NORMS = {0: 0, 1: 1, 2: 2, 3: 3, "first": 4, 4: 5, 5: 6, "last": 7}
        GAIN = ["attn_norm", "ffn_norm", "l1_norm", "ffn1_norm", "attn2_norm", "moe_norm"]
        KINDS = {"mla": 0, "fox": 1, "swa": 2}
        NU = len(UNITS)
        H1_BANK, H3_BANK, Y_BANK, T_BANK, SMALL_BANK, XG_BANK, S_BANK = (0, 2), (1, 3), (4, 5), 6, 7, (2, 3), (0, 6, 4, 5)

        def hi_lo_passes(x_hi, x_lo, u_hi, u_lo):
            return ((x_hi, u_hi), (x_hi, u_lo), (x_lo, u_hi))

        PREFETCH = MOE[:SLOTS]

        @block.sync
        def _(sp):
            sp.dma_start(small[:, :], d["small"]).then_inc(small_in, 16)
            sp.dma_start(x[:, :, :], d["x"].rearrange("(a p) n -> p a n", p=P)).then_inc(x_in, 16)
            sp.dma_start(pos[:, :], d["positions"]).then_inc(small_in, 16)
            sp.dma_start(w_router[:, :, :], d["w_router"].rearrange("(p k) n -> p k n", k=KD)).then_inc(router_in, 16)

            def load(name, *pieces):
                if W.vacated(name):
                    sp.wait_ge(*W.vacated(name))
                for dst, src in pieces:
                    sp.dma_start(dst, src).then_inc(landed[W.slot(name)], 16)

            def columns(name, w, n=512):
                load(name, (slot8(W.slot(name), n), w.rearrange("(p k) n -> p k n", k=KD)))

            def rows(name, w, n):
                for i in range(n):
                    load(f"{name}w{i}", (unit_rows(f"{name}w{i}"), w[i * 512:(i + 1) * 512].rearrange("(k p) n -> p k n", p=P)))

            def ffn(n, gate, up, down):
                def pieces(slot, j):
                    yield ring[:, slot, 0:1024].rearrange("p (k n) -> p k n", k=KD), gate[j]
                    yield ring[:, slot, 1024:2048].rearrange("p (k n) -> p k n", k=KD), up[j]
                    yield ring[:, slot, 2048:3072], down[j]

                for j in range(FFN_RING):
                    load(f"ffn{n}_{j}", *pieces(FFN_SLOT[n][j], j))
                with sp.Fori(1, NF // FFN_RING) as i:
                    for b in range(FFN_RING):
                        sp.wait_ge(ffn_part, i * FFN_RING + (n * (NF - 1) + b - FFN_RING + 1))
                        for dst, src in pieces(FFN_SLOT[n][b], i * FFN_RING + b):
                            sp.dma_start(dst, src).then_inc(landed[FFN_SLOT[n][b]], 16)
                for j in range(NF // FFN_RING * FFN_RING, NF):
                    load(f"ffn{n}_{j}", *pieces(FFN_SLOT[n][j % FFN_RING], j))

            in_w = d["in_w"]
            columns("iq", in_w[:, 768:1280])
            columns("misc", d["misc"], 344)
            columns("q", in_w[:, 0:512])
            for i in range(3):
                columns(f"xb{i}", in_w[:, 2376 + 512 * i:2888 + 512 * i])
            for i in range(2):
                columns(f"z{i}", in_w[:, 1352 + 512 * i:1864 + 512 * i])
            s = W.slot("kv")
            load("kv", (ring[:, s, 0:1024].rearrange("p (k n) -> p k n", k=2), d["w_uk"].rearrange("(k p) n -> p k n", p=P)),
                 (ring[:, s, 1024:2048].rearrange("p (k n) -> p k n", k=2), d["w_uv"].rearrange("(k p) n -> p k n", p=P)))
            rows("out0", d["out_w0"], 3)
            ffn(0, d["gate0"], d["up0"], d["down0"])
            for j in range(KD):
                load(f"l1_{j}", (ring[:, W.slot(f"l1_{j}"), 0:3072], d["l1_in"][j]))
            rows("out1", d["out_w1"], 2)
            sp.wait_ge(*O.ready("st1"))
            sp.dma_start(norm_row[:, :], d["final_norm"].to_broadcast([P, D])).then_inc(row_in, 16)
            ffn(1, d["gate1"], d["up1"], d["down1"])
            w2 = d["w_in2"]
            columns("fq", w2[:, 0:512])
            columns("fk", w2[:, 512:1024])
            columns("fv", w2[:, 1024:1536])
            columns("misc2", d["misc2"], 264)
            columns("sq", w2[:, 1544:2056])
            for i in range(2):
                columns(f"gf{i}", w2[:, 2312 + 512 * i:2824 + 512 * i])
            for i in range(2):
                columns(f"gs{i}", w2[:, 3336 + 512 * i:3848 + 512 * i])
            load("pf", (unit_rows("pf"), d["proj_fox"].rearrange("(k p) n -> p k n", p=P)))
            load("ps", (unit_rows("ps"), d["proj_swa"].rearrange("(k p) n -> p k n", p=P)))
            rows("out2", d["out_w2"], 2)
            sp.wait_ge(x_final, NT)
            sp.dma_start(norm_row[:, :], d["moe_norm"].to_broadcast([P, D])).then_inc(row_in, 16)

            def expert_load(kind, e, u):
                slot = MOE_SLOT[u]
                if kind == "w2":
                    dst, src = unit_rows_at(slot), d["w2"][bass.ds(e * NE, NE)].rearrange("k p n -> p k n")
                else:
                    dst, src = ring[:, slot, :], d[kind][bass.ds(e, 1)].rearrange("a p n -> p (a n)")
                sp.dma_start(dst, src).then_inc(landed[slot], 16)

            def unit_rows_at(slot):
                return ring[:, slot, :].rearrange("p (k n) -> p k n", k=NE)

            for u, (kind, e) in enumerate(PREFETCH):
                if MOE_BEFORE[u]:
                    sp.wait_ge(*MOE_BEFORE[u])
                expert_load(kind, e, u)
            sp.wait_ge(x_rows, NT)
            sp.dma_start(norm_row[:, :], d["final_norm2"].to_broadcast([P, D])).then_inc(row_in, 16)
            sp.wait_ge(r_pass, 1)
            passes = sp.value_load(passes_i[0:1, 0:1], min_val=1, max_val=T // CAP)

            def rest_of_group(n, g8):
                for u in range(SLOTS, NM):
                    kind, e = MOE[u]
                    sp.wait_ge(m_unit, n * NM + (u - SLOTS + 1))
                    expert_load(kind, g8 + e, u)

            def first_of_group(n, g8):
                for u, (kind, e) in enumerate(PREFETCH):
                    sp.wait_ge(m_unit, n * NM + (NM - SLOTS + u + 1))
                    expert_load(kind, g8 + e, u)

            with sp.Fori(0, passes) as p:
                with sp.Fori(0, N_GROUPS - 1) as g:
                    n = sp.snap(p * N_GROUPS + g)
                    rest_of_group(n, g * PER_GROUP)
                    first_of_group(n, g * PER_GROUP + PER_GROUP)
                n = sp.snap(p * N_GROUPS + (N_GROUPS - 1))
                rest_of_group(n, N_EXPERTS - PER_GROUP)
                with sp.If(p + 1 < passes):
                    first_of_group(n, 0)
            for tc in range(NT):
                sp.wait_ge(out_ready, tc + 1)
                sp.dma_start(out[tc * P:(tc + 1) * P, :], x[:, tc, :]).then_inc(out_sent, 16)
            sp.wait_ge(out_sent, 16 * NT)

        @block.tensor
        def _(pe):
            mm = nc.tensor.matmul
            seen = [0]

            def begin(name):
                if O.bank_free(name):
                    pe.wait_ge(*O.bank_free(name))

            def end(name, ins):
                seen[0] += 1
                assert O.ready(name)[1] == seen[0], name
                ins.then_inc(tile_ready, 1)

            def norm_T(n):
                pe.wait_ge(xn_ready, NT * (n + 1))
                for j in range(4):
                    name = f"norm{n}_{j}"
                    begin(name)
                    for kk in range(2):
                        for tc in range(NT):
                            at = kk * T + tc * P
                            last = nc.tensor.transpose(bank(name)[:, at:at + P], xn[:, tc, 2 * j + kk::KD], ident)
                    end(name, last)

            def normed(n):
                for j in ((3,) if n in SPLIT_NORMS else (2, 3)):
                    pe.wait_ge(*O.drained(f"norm{n}_{j}"))

            def channels(name, unit, first, count=2, n=512):
                w = slot8(W.slot(unit), n)
                begin(name)
                for m in range(count):
                    for k in range(KD):
                        last = mm(bank(name)[:, m * T:(m + 1) * T], w[:, k, (first + m) * P:(first + m + 1) * P],
                                  xnT[:, k, :], start=(k == 0), stop=(k == KD - 1))
                end(name, last)

            def tokens(name, unit, tc, width, n=512):
                w = slot8(W.slot(unit), n)
                begin(name)
                for k in range(KD):
                    last = mm(bank(name)[:, 0:width], xnT[:, k, tc * P:(tc + 1) * P], w[:, k, 0:width],
                              start=(k == 0), stop=(k == KD - 1))
                end(name, last)

            def out_rows(name, src, n):
                for tc, h in RES:
                    begin(f"{name}_{tc}{h}")
                for kc in range(4 * n):
                    unit = f"{name}w{kc // 4}"
                    if kc % 4 == 0:
                        pe.wait_ge(*W.landed(unit))
                    for tc, h in RES:
                        last = mm(bank(f"{name}_{tc}{h}"), src[:, kc, tc * P:(tc + 1) * P],
                                  unit_rows(unit)[:, kc % 4, h * 512:(h + 1) * 512],
                                  start=(kc == 0), stop=(kc == 4 * n - 1))
                        if kc == 4 * n - 1:
                            end(f"{name}_{tc}{h}", last)
                    if kc % 4 == 3 and kc < 4 * n - 1:
                        last.then_inc(part_used, 1)

            def out_rows_split(name, src_hi, src_lo, n):
                for tc, h in RES:
                    begin(f"{name}_{tc}{h}")
                for kc in range(4 * n):
                    unit = f"{name}w{kc // 4}"
                    if kc % 4 == 0:
                        pe.wait_ge(*S.low(unit))
                    u_hi, u_lo = high_half(unit), ring_r[W.slot(unit)]
                    for tc in range(NT):
                        for i, (a, b) in enumerate(hi_lo_passes(src_hi, src_lo, u_hi, u_lo)):
                            for h in range(2):
                                at = kc % 4 * D + h * 512
                                last = mm(bank(f"{name}_{tc}{h}"), a[:, kc, tc * P:(tc + 1) * P], b[:, at:at + 512],
                                          start=(kc == 0 and i == 0), stop=(kc == 4 * n - 1 and i == 2))
                                if kc == 4 * n - 1 and i == 2:
                                    end(f"{name}_{tc}{h}", last)
                    if kc % 4 == 3 and kc < 4 * n - 1:
                        last.then_inc(part_used, 1)

            def attention(kind, q, k_of, v_of, before=lambda u: None):
                K = KINDS[kind] * NU

                def logits(u):
                    tc, _, heads, w = UNITS[u]
                    name = f"{kind}_l{u}"
                    begin(name)
                    for i, h in enumerate(heads):
                        a = DH * (h % 2)
                        last = mm(bank(name)[:, i * w:(i + 1) * w], q[a:a + DH, h // 2, tc * P:(tc + 1) * P],
                                  k_of(h)[a:a + DH, 0:w], start=True, stop=True)
                    end(name, last)

                def turn(u):
                    name = f"{kind}_t{u}"
                    pe.wait_ge(probs_ready, K + u + 1)
                    begin(name)
                    for blk in range(4):
                        last = nc.tensor.transpose(bank(name)[:, blk * P:(blk + 1) * P],
                                                   pr[:, u % 2, blk * P:(blk + 1) * P], ident)
                    end(name, last)

                def mix(u):
                    tc, _, heads, w = UNITS[u]
                    name = f"{kind}_o{u}"
                    pe.wait_ge(*O.drained(f"{kind}_t{u}"))
                    begin(name)
                    ns = w // P
                    for i, h in enumerate(heads):
                        a = DH * (h % 2)
                        for s in range(ns):
                            last = mm(bank(name)[a:a + DH, i * P:(i + 1) * P], v_of(h, s),
                                      pT[:, u % 2, (i * ns + s) * P:(i * ns + s + 1) * P],
                                      start=(s == 0), stop=(s == ns - 1))
                    end(name, last)

                for u in range(NU + 2):
                    if u < NU:
                        before(u)
                        logits(u)
                    if 1 <= u <= NU:
                        turn(u - 1)
                    if u >= 2:
                        mix(u - 2)

            def ffn(n):
                norm_T(2 * n + 1)
                normed(2 * n + 1)
                base = O.at[f"ffn{n}_11"] + 1
                gu = [psum[:, (base + b) % 8, :] for b in range(2)]
                for tc, h in RES:
                    begin(f"ffn{n}_{tc}{h}")

                def gate_up(b, slot):
                    u_hi, u_lo = arena_r[:, FFN_HIGH[n][b % FFN_RING]:][:, 0:FFN_WORDS], ring_r[slot]
                    for m in range(2):
                        for k in range(KD):
                            for i, (a, w) in enumerate(hi_lo_passes(xnT_r, xn_lo, u_hi, u_lo)):
                                last = mm(gu[b % 2][:, m * T:(m + 1) * T], w[:, (m * KD + k) * P:(m * KD + k + 1) * P],
                                          a[:, k, :], start=(k == 0 and i == 0), stop=(k == KD - 1 and i == 2))
                    last.then_inc(ffn_in, 1)

                def down(b, slot, start=False, stop=False):
                    u_hi, u_lo = arena_r[:, FFN_HIGH[n][b % FFN_RING]:][:, 0:FFN_WORDS], ring_r[slot]
                    for tc in range(NT):
                        for i, (a, w) in enumerate(hi_lo_passes(h_hi, h_lo, u_hi, u_lo)):
                            for h in range(2):
                                last = mm(bank(f"ffn{n}_{tc}{h}"), a[:, b % 2, tc * P:(tc + 1) * P],
                                          w[:, 2048 + h * 512:2560 + h * 512], start=(start and i == 0),
                                          stop=(stop and i == 2), skip_group_check=True)
                                if stop and i == 2:
                                    end(f"ffn{n}_{tc}{h}", last)
                    if not stop:
                        last.then_inc(ffn_part, 1)

                s = FFN_SLOT[n]
                for j in range(2):
                    pe.wait_ge(*S.low(f"ffn{n}_{j}"))
                    gate_up(j, s[j])
                pe.wait_ge(ffn_h, n * NF + 1)
                down(0, s[0], start=True)
                with pe.Fori(0, NF // FFN_RING) as i:
                    for b in range(1, FFN_RING + 1):
                        nxt = b + 1
                        slot = s[nxt % FFN_RING]
                        pe.wait_ge(w_low, i * FFN_RING + S.low(f"ffn{n}_{nxt}")[1])
                        gate_up(nxt, slot)
                        pe.wait_ge(ffn_h, i * FFN_RING + (n * NF + b + 1))
                        down(b, s[b % FFN_RING])
                pe.wait_ge(ffn_h, (n + 1) * NF)
                down(NF - 1, s[(NF - 1) % FFN_RING], stop=True)

            pe.wait_ge(small_in, 32)
            norm_T(0)
            normed(0)
            pe.wait_ge(*W.landed("iq"))
            for j in range(2):
                channels(f"iq{j}", "iq", 2 * j)
            pe.wait_ge(*W.landed("misc"))
            w = slot8(W.slot("misc"), 344)
            begin("ik")
            for half in range(2):
                for k in range(KD):
                    last = mm(bank("ik")[half * DH:(half + 1) * DH, 0:T], w[:, k, 280:344], xnT[:, k, :],
                              start=(k == 0), stop=(k == KD - 1))
            end("ik", last)
            for tc in range(NT):
                tokens(f"misc{tc}", "misc", tc, 280, 344)
            for name in ("iq0", "iq1", "ik"):
                pe.wait_ge(*O.drained(name))
            for u, (tc, _, heads, wd) in enumerate(UNITS):
                name = f"il{u}"
                begin(name)
                for i, h in enumerate(heads):
                    a = DH * (h % 2)
                    last = mm(bank(name)[:, i * wd:(i + 1) * wd], iqT[a:a + DH, h // 2, tc * P:(tc + 1) * P],
                              ikT[a:a + DH, 0:wd], start=True, stop=True)
                end(name, last)
            pe.wait_ge(*W.landed("q"))
            for j in range(2):
                channels(f"q{j}", "q", 2 * j)
            for j in range(6):
                if j % 2 == 0:
                    pe.wait_ge(*W.landed(f"xb{j // 2}"))
                channels(f"xb{j}", f"xb{j // 2}", 2 * (j % 2))
            for h in range(2):
                pe.wait_ge(*W.landed(f"z{h}"))
                for tc in range(NT):
                    tokens(f"z{tc}{h}", f"z{h}", tc, 512)
            pe.wait_ge(ckv_ready, NT)
            begin("ckvT")
            for cc in range(2):
                for tc in range(NT):
                    last = nc.tensor.transpose(bank("ckvT")[:, cc * T + tc * P:cc * T + (tc + 1) * P],
                                               ckv[:, tc, cc * P:(cc + 1) * P], ident)
            end("ckvT", last)
            pe.wait_ge(*W.landed("kv"))
            pe.wait_ge(*O.drained("ckvT"))
            w_uk = ring[:, W.slot("kv"), 0:1024].rearrange("p (k n) -> p k n", k=2)
            w_uv = ring[:, W.slot("kv"), 1024:2048].rearrange("p (k n) -> p k n", k=2)
            for j in range(2):
                begin(f"k{j}")
                for m in range(2):
                    for kc in range(2):
                        last = mm(bank(f"k{j}")[:, m * T:(m + 1) * T], w_uk[:, kc, (2 * j + m) * P:(2 * j + m + 1) * P],
                                  ckvT[:, kc, :], start=(kc == 0), stop=(kc == 1))
                end(f"k{j}", last)
            for s in range(NT):
                begin(f"v{s}")
                for kc in range(2):
                    last = mm(bank(f"v{s}"), ckvT[:, kc, s * P:(s + 1) * P], w_uv[:, kc, :],
                              start=(kc == 0), stop=(kc == 1))
                end(f"v{s}", last)
            pe.wait_ge(*O.drained("v1"))
            attention("mla", qT, lambda h: kT[:, h // 2, :], lambda h, s: v_tok[:, s, h * DH:(h + 1) * DH])
            pe.wait_ge(conv_done, 6)
            for tc in range(NT):
                for h in range(2):
                    name = f"xs{tc}{h}"
                    begin(name)
                    for q in range(4):
                        last = nc.tensor.transpose(bank(name)[:, q * P:(q + 1) * P],
                                                   convT[:, 4 * h + q, tc * P:(tc + 1) * P], ident)
                    end(name, last)
            begin("B_tok")
            for g in range(2):
                last = nc.tensor.transpose(bank("B_tok")[:, g * P:(g + 1) * P], convT[:, 8 + g, 0:P], ident)
            end("B_tok", last)
            begin("cbT")
            for cc in range(NT):
                for g in range(2):
                    at = (2 * cc + g) * P
                    last = mm(bank("cbT")[:, at:at + P], convT[:, 8 + g, cc * P:(cc + 1) * P],
                              convT[:, 10 + g, cc * P:(cc + 1) * P], start=True, stop=True)
            end("cbT", last)
            pe.wait_ge(a_ready, 1)
            begin("acs")
            mm(bank("acs")[:, 0:16], tri, a_dt[:, 0, :], start=True, stop=True)
            mm(bank("acs")[:, 16:32], tri, a_dt[:, 1, :], start=True, stop=True)
            end("acs", mm(bank("acs")[:, 32:48], ones, a_dt[:, 0, :], start=True, stop=True))

            def cumulative(cc, hq):
                name = f"bc{cc}{hq}"
                begin(name)
                for i in range(4):
                    last = mm(bank(name)[:, i * P:(i + 1) * P],
                              a_dt[:, cc, 4 * hq + i:4 * hq + i + 1].to_broadcast([P, P]), tri, start=True, stop=True)
                end(name, last)

            def states(g):
                begin(f"st{g}")
                end(f"st{g}", mm(bank(f"st{g}"), B_tok[:, g, :], xdt_end[:, g * 512:(g + 1) * 512],
                                 start=True, stop=True))

            def within(cc, g):
                name = f"y{cc}{g}"
                begin(name)
                for hq in (2 * g, 2 * g + 1):
                    pe.wait_ge(ssm_w, 4 * cc + hq + 1)
                    for i in range(4):
                        h = 4 * hq + i
                        last = mm(bank(name)[:, (h % 8) * DH:(h % 8 + 1) * DH], pT[:, hq % 2, i * P:(i + 1) * P],
                                  xdt[:, cc, h * DH:(h + 1) * DH], start=True, stop=True)
                    if hq % 2 == 0:
                        last.then_inc(ssm_y, 1)
                end(name, last)

            def across(g):
                pe.wait_ge(*O.drained(f"st{g}"))
                begin(f"yo{g}")
                end(f"yo{g}", mm(bank(f"yo{g}"), convT[:, 10 + g, P:T], state[:, g, :], start=True, stop=True))

            cumulative(0, 0)
            cumulative(0, 1)
            pe.wait_ge(xdt_ready, 3)
            pe.wait_ge(*O.drained("B_tok"))
            states(0)
            states(1)
            cumulative(0, 2)
            cumulative(0, 3)
            within(0, 0)
            cumulative(1, 0)
            cumulative(1, 1)
            within(0, 1)
            cumulative(1, 2)
            cumulative(1, 3)
            within(1, 0)
            across(0)
            within(1, 1)
            across(1)
            pe.wait_ge(y_ready, 4)
            for j in range(4):
                name = f"yT{j}"
                begin(name)
                for kk in range(2):
                    for tc in range(NT):
                        at = kk * T + tc * P
                        last = nc.tensor.transpose(bank(name)[:, at:at + P],
                                                   y_tok[:, tc, (2 * j + kk) * P:(2 * j + kk + 1) * P], ident)
                end(name, last)
            for j in (2, 3):
                pe.wait_ge(*O.drained(f"yT{j}"))
            out_rows("out0", mixT, 3)
            ffn(0)
            norm_T(2)
            normed(2)
            for j in range(KD):
                pe.wait_ge(*S.low(f"l1_{j}"))
                u_hi, u_lo = high_half(f"l1_{j}"), ring_r[W.slot(f"l1_{j}")]

                def third(dst, m):
                    for k in range(KD):
                        for i, (a, w) in enumerate(hi_lo_passes(xnT_r, xn_lo, u_hi, u_lo)):
                            last = mm(dst, w[:, (3 * k + m) * P:(3 * k + m + 1) * P], a[:, k, :],
                                      start=(k == 0 and i == 0), stop=(k == KD - 1 and i == 2))
                    return last

                begin(f"cv{j}")
                third(bank(f"cv{j}")[:, 0:T], 0)
                end(f"cv{j}", third(bank(f"cv{j}")[:, T:2 * T], 1))
                begin(f"b{j}")
                end(f"b{j}", third(bank(f"b{j}")[:, 0:T], 2))
            pe.wait_ge(sc_split, KD)
            out_rows_split("out1", sc_hi, sc_lo, 2)
            ffn(1)
            norm_T(4)
            normed(4)
            for n in ("fq", "fk"):
                pe.wait_ge(*W.landed(n))
                for j in range(2):
                    channels(f"{n}{j}", n, 2 * j)
            pe.wait_ge(*W.landed("fv"))
            for tc in range(NT):
                tokens(f"fv{tc}", "fv", tc, 512)
            pe.wait_ge(*W.landed("misc2"))
            for tc in range(NT):
                tokens(f"misc2_{tc}", "misc2", tc, 264, 264)
            pe.wait_ge(*W.landed("sq"))
            for tc in range(NT):
                tokens(f"sq{tc}", "sq", tc, 512)
            for n in ("gf", "gs"):
                for j in range(4):
                    if j % 2 == 0:
                        pe.wait_ge(*W.landed(f"{n}{j // 2}"))
                    channels(f"{n}{j}", f"{n}{j // 2}", 2 * (j % 2))
            pe.wait_ge(log_f_ready, 1)
            begin("fox_c")
            mm(bank("fox_c")[:, 0:8], tri, log_f[:, 0, :], start=True, stop=True)
            mm(bank("fox_c")[:, 8:16], ones, log_f[:, 0, :], start=True, stop=False)
            end("fox_c", mm(bank("fox_c")[:, 8:16], tri, log_f[:, 1, :], start=False, stop=True))

            def forget_sums(u):
                tc, _, heads, wd = UNITS[u]
                name = f"fox_b{u}"
                begin(name)
                for i, h in enumerate(heads):
                    f0 = log_f[:, 0, h:h + 1].to_broadcast([P, P])
                    last = mm(bank(name)[:, i * wd:i * wd + P], f0, tri, start=True, stop=True)
                    if wd == T:
                        f1 = log_f[:, 1, h:h + 1].to_broadcast([P, P])
                        mm(bank(name)[:, i * wd + P:(i + 1) * wd], f0, ones, start=True, stop=False)
                        last = mm(bank(name)[:, i * wd + P:(i + 1) * wd], f1, tri, start=False, stop=True)
                end(name, last)

            for name in ("fq1", "fk1", "fv1"):
                pe.wait_ge(*O.drained(name))
            attention("fox", qT, lambda h: kT[:, h // 2, :], lambda h, s: v_tok[:, s, h * DH:(h + 1) * DH], forget_sums)
            pe.wait_ge(roped, NT)
            for j in range(2):
                name = f"sqT{j}"
                begin(name)
                for m in range(2):
                    for tc in range(NT):
                        at = m * T + tc * P
                        last = nc.tensor.transpose(bank(name)[:, at:at + P],
                                                   rope_x[:, tc, (2 * j + m) * P:(2 * j + m + 1) * P], ident)
                end(name, last)
            begin("skT")
            for kv in range(2):
                for tc in range(NT):
                    at = kv * T + tc * P
                    for half in range(2):
                        last = mm(bank("skT")[half * DH:(half + 1) * DH, at:at + P],
                                  rope_x[:, tc, 512 + kv * DH:512 + (kv + 1) * DH], ident, start=True, stop=True)
            end("skT", last)
            pe.wait_ge(*O.drained("skT"))
            attention("swa", sqT, lambda h: skT[:, h // 4, :],
                      lambda h, s: sv[:, s, (h // 4) * DH:(h // 4 + 1) * DH])
            pe.wait_ge(*O.drained("swa_o5"))
            for n in ("pf", "ps"):
                pe.wait_ge(*W.landed(n))
            for j in range(4):
                for gi, n in enumerate(("pf", "ps")):
                    begin(f"{n}{j}")
                    for m in range(2):
                        for kc in range(4):
                            last = mm(bank(f"{n}{j}")[:, m * T:(m + 1) * T],
                                      unit_rows(n)[:, kc, (2 * j + m) * P:(2 * j + m + 1) * P], mixT[:, 4 * gi + kc, :],
                                      start=(kc == 0), stop=(kc == 3))
                    end(f"{n}{j}", last)
            pe.wait_ge(merged, 4)
            out_rows("out2", mergedT, 2)
            norm_T(5)
            normed(5)
            pe.wait_ge(router_in, 16)
            for tc in range(NT):
                begin(f"router{tc}")
                for k in range(KD):
                    last = mm(bank(f"router{tc}")[:, 0:72], xnT[:, k, tc * P:(tc + 1) * P], w_router[:, k, :],
                              start=(k == 0), stop=(k == KD - 1))
                end(f"router{tc}", last)
            pe.wait_ge(r_gate, 1)
            begin("rank")
            mm(bank("rank")[:, 0:8], strict, g_hot[:, 0, :], start=True, stop=True)
            mm(bank("rank")[:, 8:16], ones, g_hot[:, 0, :], start=True, stop=False)
            mm(bank("rank")[:, 8:16], strict, g_hot[:, 1, :], start=False, stop=True)
            mm(bank("rank")[:, 16:24], ones, g_hot[:, 0, :], start=True, stop=False)
            end("rank", mm(bank("rank")[:, 16:24], ones, g_hot[:, 1, :], start=False, stop=True))
            pe.wait_ge(r_pass, 1)
            pe.wait_ge(r_gate, 2)
            passes = pe.value_load(passes_i[0:1, 0:1], min_val=1, max_val=T // CAP)

            def turn(e, n):
                pe.wait_ge(m_h, n * PER_GROUP + (e + 1))
                for j in range(NE):
                    last = nc.tensor.transpose(psum[:, T_BANK, j * P:(j + 1) * P], h_e[:, e % 2, j * P:(j + 1) * P], ident)
                last.then_inc(m_turned, 1)

            def expert_in(u, n):
                kind, e = MOE[u]
                pe.wait_ge(m_lo, n * NM + (u + 1))
                dst = psum[:, (H1_BANK if kind == "w1" else H3_BANK)[e % 2], :]
                u_hi, u_lo = w_hi[:, u % HI_SLOTS, :], ring_r[MOE_SLOT[u]]
                for k in range(KD):
                    tokens_at, at = slice(k * CAP, (k + 1) * CAP), slice(k * D_EXPERT, (k + 1) * D_EXPERT)
                    for i, (a, b) in enumerate(hi_lo_passes(xg_hi, xg_lo, u_hi, u_lo)):
                        last = mm(dst, a[:, tokens_at], b[:, at], start=(k == 0 and i == 0),
                                  stop=(k == KD - 1 and i == 2))
                last.then_inc(m_unit, 1)

            def expert_out(u, n, halfway=lambda: None):
                e = MOE[u][1]
                pe.wait_ge(m_lo, n * NM + (u + 1))
                pe.wait_ge(m_hT_lo, n * PER_GROUP + (e + 1))
                u_hi, u_lo = w_hi[:, u % HI_SLOTS, :], ring_r[MOE_SLOT[u]]
                for j in range(NE):
                    for i, (a, b) in enumerate(hi_lo_passes(hT_hi, hT_lo, u_hi, u_lo)):
                        for h in range(2):
                            last = mm(psum[:, Y_BANK[h], :], a[:, e % 2, j * P:(j + 1) * P],
                                      b[:, j * D + h * 512:j * D + (h + 1) * 512],
                                      start=(e == 0 and j == 0 and i == 0),
                                      stop=(e == PER_GROUP - 1 and j == NE - 1 and i == 2))
                    if j == 1:
                        halfway()
                last.then_inc(m_unit, 1)

            def gather(n):
                pe.wait_ge(m_sel, n + 1)
                for k in range(KD):
                    dst = psum[:, XG_BANK[k // 4], (k % 4) * CAP:(k % 4 + 1) * CAP]
                    for tc in range(NT):
                        last = mm(dst, xn[:, tc, k::KD], sel_g[:, tc, :], start=(tc == 0), stop=(tc == NT - 1))
                last.then_inc(m_xg, 1)

            def small_parts():
                for tc in range(NT):
                    nc.tensor.transpose(psum[:, SMALL_BANK, tc * P:(tc + 1) * P], sel_g[:, tc, :], ident)
                for tc in range(NT):
                    last = mm(psum[:, SMALL_BANK, T:T + PER_GROUP], sel_g[:, tc, :], gate8[:, tc, :],
                              start=(tc == 0), stop=(tc == NT - 1))
                last.then_inc(m_small, 1)

            def send_back(n):
                pe.wait_ge(m_y_lo, n + 1)
                for i, (tc, h) in enumerate(RES):
                    for part_y in (y_hi, y_lo):
                        last = mm(psum[:, S_BANK[i], :], sel_gT[:, tc * P:(tc + 1) * P],
                                  part_y[:, h * 512:(h + 1) * 512],
                                  start=(part_y is y_hi), stop=(part_y is y_lo))
                    last.then_inc(m_sc, 1)

            pe.wait_ge(x_rows, NT)
            with pe.Fori(0, passes) as p:
                n = pe.snap(p * N_GROUPS)
                gather(n)
                small_parts()
                with pe.Fori(0, N_GROUPS) as g:
                    n = pe.snap(p * N_GROUPS + g)
                    pe.wait_ge(m_xg_lo, n + 1)
                    pe.wait_ge(m_scd, n * 4)
                    for u, (kind, e) in enumerate(MOE):
                        if kind == "w2":
                            if u == NM - 2:
                                expert_out(u, n, lambda: turn(PER_GROUP - 1, n))
                            else:
                                expert_out(u, n)
                        else:
                            expert_in(u, n)
                            if kind == "w1" and e >= 1:
                                turn(e - 1, n)
                    with pe.If(g < N_GROUPS - 1):
                        gather(n + 1)
                    pe.wait_ge(m_selT, n + 1)
                    send_back(n)
                    with pe.If(g < N_GROUPS - 1):
                        small_parts()

        @block.scalar
        def _(act):
            A = nc.scalar.activation

            def square(n, source):
                for tc in range(NT):
                    act.wait_ge(*source(tc))
                    A(xn[:, tc, :], x[:, tc, :], ACT.Square, accum_out=ss[:, NORMS[n], tc:tc + 1]).then_inc(squares, 1)

            def added(name):
                return lambda tc: O.drained(f"{name}_{tc}1")

            def norm_T(n):
                for j in (0, 2):
                    act.wait_ge(*O.ready(f"norm{n}_{j}"))
                    for kk in range(2):
                        k = 2 * j + kk
                        last = A(xnT[:, k, :], bank(f"norm{n}_{j}")[:, kk * T:(kk + 1) * T], ACT.Copy, scale=c(GAIN[n], k))
                    last.then_inc(act_drained, 1)

            def norm_T_hi(n):
                for j in range(4):
                    act.wait_ge(*O.ready(f"norm{n}_{j}"))
                    for kk in range(2):
                        k = 2 * j + kk
                        last = A(xnT_r[:, k, :], bank(f"norm{n}_{j}")[:, kk * T:(kk + 1) * T], ACT.Copy, scale=c(GAIN[n], k))
                    last.then_inc(x_high, 1)

            def split(name):
                act.wait_ge(*W.landed(name))
                for release in S.vacated(name):
                    act.wait_ge(*release)
                hi = high_half(name)
                A(hi, ring[:, W.slot(name), 0:hi.shape[-1]], ACT.Copy).then_inc(w_high, 1)

            def copy(name, dst, width=512, func=ACT.Copy):
                act.wait_ge(*O.ready(name))
                src = bank(name)[:, 0:width]
                if len(dst.shape) == 3:
                    src = src.rearrange("p (a b) -> p a b", a=dst.shape[1])
                A(dst, src, func).then_inc(act_drained, 1)

            def attention(kind):
                K = KINDS[kind]

                def probs(u):
                    tc, at, heads, w = UNITS[u]
                    nh = len(heads)
                    act.wait_ge(logits_masked, K * NU + u + 1)
                    if u >= 2:
                        act.wait_ge(*O.ready(f"{kind}_t{u - 2}"))
                    for i in range(nh):
                        col = at + i
                        last = A(pr[:, u % 2, i * w:(i + 1) * w], lm[:, u % 2, i * w:(i + 1) * w], ACT.Exp,
                                 bias=neg_max[:, K, col:col + 1], accum_out=row_sum[:, K, col:col + 1])
                    last.then_inc(probs_raw, 1)
                    if kind == "swa":
                        act.wait_ge(sink_sub, u + 1)
                        A(sink_e[:, at:at + nh], sink_d[:, at:at + nh], ACT.Exp).then_inc(sink_exp, 1)

                for u in range(NU + 1):
                    if u < NU:
                        probs(u)
                    if u >= 1:
                        copy(f"{kind}_t{u - 1}", pT[:, (u - 1) % 2, :])

            def ffn(n):
                norm_T_hi(2 * n + 1)
                base = O.at[f"ffn{n}_11"] + 1

                def silu(i, b):
                    act.wait_ge(ffn_in, i * FFN_RING + (n * NF + b + 1))
                    A(sg_f[:, b % 2, :], psum[:, (base + b % 2) % 8, 0:T],
                      ACT.Silu).then_inc(ffn_silu, 1)

                with act.Fori(0, NF // FFN_RING) as i:
                    for b in range(FFN_RING):
                        nxt, slot = b + 2, FFN_SLOT[n][(b + 2) % FFN_RING]
                        act.wait_ge(landed[slot], i * (16 * 3) + W.landed(f"ffn{n}_{nxt}")[1])
                        A(arena_r[:, FFN_HIGH[n][nxt % FFN_RING]:][:, 0:FFN_WORDS], ring[:, slot, 0:FFN_WORDS],
                          ACT.Copy).then_inc(w_high, 1)
                        silu(i, b)
                for b in range(2):
                    silu(NF // FFN_RING, b)

            act.wait_ge(small_in, 32)
            square(0, lambda tc: (x_in, 16))
            norm_T(0)
            act.wait_ge(*O.ready("iq0"))
            copy("iq0", iqT[:, 0:2, :])
            copy("ik", ikT, T)
            for tc in range(NT):
                act.wait_ge(*O.drained(f"misc{tc}"))
                A(work[:, tc, :], ckv[:, tc, :], ACT.Square, accum_out=ss_kv[:, tc, :]).then_inc(kv_sq, 1)
            for u in range(NU):
                if u >= 2:
                    act.wait_ge(il_used, u - 1)
                copy(f"il{u}", lm[:, u % 2, :], 512, ACT.Relu)
            for j in range(2):
                copy(f"q{j}", qT[:, 2 * j:2 * j + 2, :])
            act.wait_ge(sp_abs, 1)
            A(sp[:, 1, :], sp[:, 0, :], ACT.Exp, scale=-1.0).then_inc(sp_exp, 1)
            A(neg_A, c("A_log"), ACT.Exp).then_inc(a_log_exp, 1)
            act.wait_ge(pads_zero, 1)

            def conv_silu(j):
                act.wait_ge(conv_sum, j + 1)
                for m in range(2):
                    ch = 2 * j + m
                    last = A(convT[:, ch, :], convT[:, ch, :], ACT.Silu, bias=c("conv_b", ch))
                last.then_inc(conv_done, 1)

            for j in range(6):
                if j >= 2:
                    act.wait_ge(conv_sum, j - 1)
                act.wait_ge(*O.ready(f"xb{j}"))
                A(xp[:, j % 2, :, 3:259], bank2(f"xb{j}"), ACT.Copy).then_inc(act_drained, 1)
                if j >= 1:
                    conv_silu(j - 1)
            conv_silu(5)
            for h in range(2):
                for tc in range(NT):
                    copy(f"z{tc}{h}", z[:, tc, h * 512:(h + 1) * 512], 512, ACT.Silu)
            act.wait_ge(*O.ready("ckvT"))
            for cc in range(2):
                last = A(ckvT[:, cc, :], bank("ckvT")[:, cc * T:(cc + 1) * T], ACT.Copy, scale=c("kv_norm", cc))
            last.then_inc(act_drained, 1)
            for j in range(2):
                copy(f"k{j}", kT[:, 2 * j:2 * j + 2, :])
            for s in range(NT):
                copy(f"v{s}", v_tok[:, s, :])
            attention("mla")
            for tc in range(NT):
                copy(f"xs{tc}0", xs[:, tc, 0:512])
            copy("B_tok", B_tok[:, :, :], 256)
            copy("cbT", cbT[:, :, :])
            act.wait_ge(end_sub, 1)
            A(end_exp, sp[:, 2, 0:16], ACT.Exp).then_inc(decays_ready, 1)
            A(acs_exp, acs[:, 1, :], ACT.Exp).then_inc(decays_ready, 1)

            def seg(i):
                act.wait_ge(*O.drained(f"bc{i // 4}{i % 4}"))
                if i >= 2:
                    act.wait_ge(ssm_w, i - 1)
                A(pr[:, i % 2, :], lm[:, i % 2, :], ACT.Exp).then_inc(seg_exp, 1)

            seg(0)
            seg(1)
            copy("st0", state[:, 0, :])
            copy("st1", state[:, 1, :])
            for i in range(2, 8):
                seg(i)
            for i in range(4):
                cc, g = i // 2, i % 2
                act.wait_ge(y_gated, i + 1)
                A(xs[:, cc, g * 512:(g + 1) * 512], y_tok[:, cc, g * 512:(g + 1) * 512], ACT.Square,
                  accum_out=ssg[:, cc, g:g + 1]).then_inc(y_sq, 1)
            for j in (0, 2):
                act.wait_ge(*O.ready(f"yT{j}"))
                for kk in range(2):
                    k = 2 * j + kk
                    last = A(mixT[:, 4 + k, :], bank(f"yT{j}")[:, kk * T:(kk + 1) * T], ACT.Copy, scale=c("ssm_norm", k))
                last.then_inc(act_drained, 1)
            act.wait_ge(*O.ready("yT3"))
            for j in range(2):
                split(f"ffn0_{j}")
            square(1, added("out0"))
            ffn(0)
            split("l1_0")
            square(2, added("ffn0"))
            split("l1_1")
            norm_T_hi(2)
            for j in range(2, KD):
                split(f"l1_{j}")
            split("out1w0")
            split("out1w1")
            split("ffn1_0")
            square(3, added("out1"))
            split("ffn1_1")
            ffn(1)
            square("first", added("ffn1"))
            square(4, lambda tc: (x_final, tc + 1))
            norm_T(4)
            copy("fq0", qT[:, 0:2, :])
            copy("fk0", kT[:, 0:2, :])
            for tc in range(NT):
                copy(f"fv{tc}", v_tok[:, tc, :])
            for tc in range(NT):
                act.wait_ge(*O.ready(f"misc2_{tc}"))
                A(f_in[:, tc, :], bank(f"misc2_{tc}")[:, 0:8], ACT.Copy)
                A(rope_x[:, tc, 512:640], bank(f"misc2_{tc}")[:, 8:136], ACT.Copy)
                A(sv[:, tc, :], bank(f"misc2_{tc}")[:, 136:264], ACT.Copy).then_inc(act_drained, 1)
            act.wait_ge(f_abs, 1)
            A(f_u, f_tmp[:, 0, :], ACT.Exp, scale=-1.0).then_inc(f_exp, 1)
            for tc in range(NT):
                copy(f"sq{tc}", rope_x[:, tc, 0:512])
            act.wait_ge(angles, 1)
            A(sin_t[:, :, :], red[:, :, :], ACT.Sin).then_inc(sincos, 1)
            A(cos_t[:, :, :], cosr[:, :, :], ACT.Sin).then_inc(sincos, 1)
            for gi, n in enumerate(("gf", "gs")):
                for j in range(4):
                    act.wait_ge(*O.ready(f"{n}{j}"))
                    for m in range(2):
                        ch = 2 * j + m
                        last = A(gates[:, gi, ch, :], bank(f"{n}{j}")[:, m * T:(m + 1) * T], ACT.Sigmoid,
                                 bias=c("b_gate", gi * KD + ch))
                    last.then_inc(act_drained, 1)
            attention("fox")
            for j in range(2):
                copy(f"sqT{j}", sqT[:, 2 * j:2 * j + 2, :])
            copy("skT", skT[:, :, :])
            attention("swa")
            square(5, added("out2"))
            norm_T(5)
            act.wait_ge(r_sub, 1)
            A(g_exp[:, :, :], g_exp[:, :, :], ACT.Exp).then_inc(r_exp, 1)
            act.wait_ge(r_sub, 2)
            A(e_x, e_d, ACT.Exp).then_inc(r_exp, 1)
            act.wait_ge(r_pass, 1)
            passes = act.value_load(passes_i[0:1, 0:1], min_val=1, max_val=T // CAP)

            def split_hi(u, n):
                at = u % NM
                act.wait_ge(landed[MOE_SLOT[at]], n * (16 * PER_SLOT) + (MOE_BASE[at] + 16 * (u // SLOTS + 1)))
                act.wait_ge(m_unit, n * NM + (u - HI_SLOTS + 1))
                A(w_hi[:, u % HI_SLOTS, :], ring[:, MOE_SLOT[at], :], ACT.Copy).then_inc(m_hi, 1)

            for u in range(2):
                act.wait_ge(landed[MOE_SLOT[u]], MOE_BASE[u] + 16)
                A(w_hi[:, u % HI_SLOTS, :], ring[:, MOE_SLOT[u], :], ACT.Copy).then_inc(m_hi, 1)

            def gathered(n):
                act.wait_ge(m_xg, n + 1)
                for i in range(2):
                    A(xg_hi[:, i * 512:(i + 1) * 512], psum[:, XG_BANK[i], :], ACT.Copy).then_inc(m_xg_hi, 1)

            def selection(n):
                act.wait_ge(m_small, n + 1)
                A(sel_gT, psum[:, SMALL_BANK, 0:T], ACT.Copy).then_inc(m_selT, 1)

            def turned_hi(e, n):
                act.wait_ge(m_turned, n * PER_GROUP + (e + 1))
                A(hT_hi[:, e % 2, :], psum[:, T_BANK, :], ACT.Copy).then_inc(m_hT_hi, 1)

            with act.Fori(0, passes) as p:
                n = act.snap(p * N_GROUPS)
                gathered(n)
                selection(n)
                with act.Fori(0, N_GROUPS) as g:
                    n = act.snap(p * N_GROUPS + g)
                    for u, (kind, e) in enumerate(MOE):
                        if u + 2 < NM:
                            if u == 0:
                                act.wait_ge(landed[MOE_SLOT[2]], n * (16 * PER_SLOT) + (MOE_BASE[2] + 16))
                                act.wait_ge(m_unit, n * NM)
                                A(w_hi[:, 2, :], ring[:, MOE_SLOT[2], :], ACT.Copy).then_inc(m_hi, 1)
                            else:
                                split_hi(u + 2, n)
                        else:
                            with act.If(n + 1 < passes * N_GROUPS):
                                split_hi(u + 2, n)
                        if kind == "w1":
                            act.wait_ge(m_unit, n * NM + (u + 1))
                            A(h_e[:, e % 2, :], psum[:, H1_BANK[e % 2], :], ACT.Silu).then_inc(m_silu, 1)
                            if e >= 1:
                                turned_hi(e - 1, n)
                        if u == NM - 2:
                            turned_hi(PER_GROUP - 1, n)
                    act.wait_ge(m_unit, n * NM + NM)
                    for i in range(2):
                        A(y_hi[:, i * 512:(i + 1) * 512], psum[:, Y_BANK[i], :], ACT.Copy).then_inc(m_y_hi, 1)
                    with act.If(g < N_GROUPS - 1):
                        gathered(n + 1)
                        selection(n + 1)
            square("last", lambda tc: (moe_done, 1))

        @block.vector
        def _(dve):
            V = nc.vector
            step = Steps(dve, dve_step)

            def drain(name, ins):
                ins.then_inc(dve_drained, 1)
                dve.wait_ge(*O.drained(name))

            def norm(n):
                for tc in range(NT):
                    dve.wait_ge(rstd_ready, NT * NORMS[n] + tc + 1)
                    V.tensor_scalar(xn[:, tc, :], x[:, tc, :], rstd[:, NORMS[n], tc:tc + 1], None,
                                    ALU.mult).then_inc(xn_ready, 1)
                for j in (1, 3):
                    dve.wait_ge(*O.ready(f"norm{n}_{j}"))
                    for kk in range(2):
                        k = 2 * j + kk
                        last = V.tensor_scalar(xnT[:, k, :], bank(f"norm{n}_{j}")[:, kk * T:(kk + 1) * T], c(GAIN[n], k),
                                               None, ALU.mult)
                    last.then_inc(dve_drained, 1)

            def split(name):
                dve.wait_ge(*S.high(name))
                hi, slot = high_half(name).bitcast(F32), W.slot(name)
                words = hi.shape[-1]
                V.tensor_tensor(ring_r[slot][:, 0:words], ring[:, slot, 0:words], hi, ALU.subtract).then_inc(w_low, 1)

            def norm_lo(n, meanwhile=lambda: None):
                for tc in range(NT):
                    dve.wait_ge(rstd_ready, NT * NORMS[n] + tc + 1)
                    V.tensor_scalar(xn[:, tc, :], x[:, tc, :], rstd[:, NORMS[n], tc:tc + 1], None,
                                    ALU.mult).then_inc(xn_ready, 1)
                meanwhile()
                for j in range(4):
                    dve.wait_ge(x_high, 4 * SPLIT_NORMS[n] + j + 1)
                    for kk in range(2):
                        k = 2 * j + kk
                        last = V.scalar_tensor_tensor(xn_lo[:, k, :], bank(f"norm{n}_{j}")[:, kk * T:(kk + 1) * T],
                                                      c(GAIN[n], k), xnT_r[:, k, :].bitcast(F32), ALU.mult,
                                                      ALU.subtract)
                    last.then_inc(dve_drained, 1)

            def scaled_norm(n, done, row):
                dve.wait_ge(row_in, row)
                for tc in range(NT):
                    dve.wait_ge(rstd_ready, NT * NORMS[n] + tc + 1)
                    V.scalar_tensor_tensor(x[:, tc, :], x[:, tc, :], rstd[:, NORMS[n], tc:tc + 1], norm_row[:, :],
                                           ALU.mult, ALU.mult).then_inc(done, 1)
                    dve.wait_ge(done, tc + 1)

            def add_out(name):
                for tc, h in RES:
                    tile = f"{name}_{tc}{h}"
                    dve.wait_ge(*O.ready(tile))
                    part_x = x[:, tc, h * 512:(h + 1) * 512]
                    drain(tile, V.tensor_tensor(part_x, part_x, bank(tile), ALU.add))

            def copy(name, dst):
                dve.wait_ge(*O.ready(name))
                src = bank(name)
                if len(dst.shape) == 3:
                    src = src.rearrange("p (a b) -> p a b", a=dst.shape[1])
                drain(name, V.tensor_copy(dst, src))

            def log1p(u, tmp, dst):
                a, s, s2, q = (tmp[:, i, :] for i in range(4))
                step(V.tensor_scalar(a, u, 2.0, None, ALU.add))
                step(V.reciprocal(a, a))
                step(V.tensor_tensor(s, u, a, ALU.mult))
                step(V.tensor_tensor(s2, s, s, ALU.mult))
                step(V.tensor_scalar(q, s2, LOG1P[0], None, ALU.mult))
                for coef in LOG1P[1:]:
                    step(V.scalar_tensor_tensor(q, q, coef, s2, ALU.add, ALU.mult))
                step(V.scalar_tensor_tensor(q, q, 1.0, s, ALU.add, ALU.mult))
                step(V.tensor_scalar(dst, q, 2.0, None, ALU.mult))

            def attention(kind, mask_of, dst):
                K = KINDS[kind]

                def masked(u):
                    tc, col, heads, w = UNITS[u]
                    nh = len(heads)
                    sinks = c("sinks")[:, heads[0]::2][:, 0:nh]
                    if kind == "fox":
                        name = f"fox_b{u}"
                        dve.wait_ge(*O.ready(name))
                        for i, h in enumerate(heads):
                            last = V.scalar_tensor_tensor(fox_d[:, u % 2, i * w:(i + 1) * w], bank(name)[:, i * w:(i + 1) * w],
                                                          fox_c[:, tc, h:h + 1], mask_of(tc), ALU.subtract, ALU.add)
                        drain(name, last)
                        mask = fox_d[:, u % 2, :].rearrange("p (a b) -> p a b", a=nh)
                    else:
                        mask = mask_of(tc).unsqueeze(1).to_broadcast([P, nh, w])
                    name = f"{kind}_l{u}"
                    dve.wait_ge(*O.ready(name))
                    dst_l = lm[:, u % 2, :].rearrange("p (a b) -> p a b", a=nh)
                    drain(name, V.scalar_tensor_tensor(dst_l, bank(name).rearrange("p (a b) -> p a b", a=nh), DH ** -0.5,
                                                       mask, ALU.mult, ALU.add))
                    m = top_max[:, K, col:col + nh]
                    step(V.tensor_reduce(m, dst_l, AX_X, ALU.max))
                    if kind == "swa":
                        step(V.tensor_tensor(m, m, sinks, ALU.max))
                    V.tensor_scalar(neg_max[:, K, col:col + nh], m, -1.0, None, ALU.mult).then_inc(logits_masked, 1)
                    if kind == "swa":
                        V.tensor_tensor(sink_d[:, col:col + nh], sinks, m, ALU.subtract).then_inc(sink_sub, 1)

                def invert(u):
                    tc, col, heads, w = UNITS[u]
                    nh = len(heads)
                    rs = row_sum[:, K, col:col + nh]
                    dve.wait_ge(probs_raw, K * NU + u + 1)
                    if kind == "swa":
                        dve.wait_ge(sink_exp, u + 1)
                        step(V.tensor_tensor(rs, rs, sink_e[:, col:col + nh], ALU.add))
                    V.reciprocal(row_inv[:, K, col:col + nh], rs).then_inc(sums_inverted, 1)

                def mixed(u):
                    tc, _, heads, w = UNITS[u]
                    nh, a = len(heads), DH * (heads[0] % 2)
                    name = f"{kind}_o{u}"
                    dve.wait_ge(*O.ready(name))
                    out_u = dst[a:a + DH, heads[0] // 2:heads[0] // 2 + nh, tc * P:(tc + 1) * P]
                    src = bank(name)[a:a + DH, 0:nh * P].rearrange("p (a b) -> p a b", a=nh)
                    drain(name, V.tensor_copy(out_u, src))

                for u in range(NU + 2):
                    if u < NU:
                        masked(u)
                    if 1 <= u <= NU:
                        invert(u - 1)
                    if u >= 2:
                        mixed(u - 2)

            def ffn(n):
                norm_lo(2 * n + 1, lambda: split(f"ffn{n}_1"))
                base = O.at[f"ffn{n}_11"] + 1

                def hidden(i, b):
                    j, b = i * FFN_RING + (n * NF + b + 1), b % 2
                    dve.wait_ge(ffn_silu, j)
                    V.tensor_tensor(h_f[:, b, :], sg_f[:, b, :], psum[:, (base + b) % 8, T:2 * T],
                                    ALU.mult).then_inc(h_made, 1)
                    dve.wait_ge(h_made, j)
                    V.tensor_copy(h_hi[:, b, :], h_f[:, b, :]).then_inc(h_rounded, 1)
                    dve.wait_ge(h_rounded, j)
                    V.tensor_tensor(h_lo[:, b, :], h_f[:, b, :], h_hi[:, b, :].bitcast(F32), ALU.subtract).then_inc(ffn_h, 1)

                with dve.Fori(0, NF // FFN_RING) as i:
                    for b in range(FFN_RING):
                        nxt, slot = b + 2, FFN_SLOT[n][(b + 2) % FFN_RING]
                        dve.wait_ge(w_high, i * FFN_RING + S.high(f"ffn{n}_{nxt}")[1])
                        V.tensor_tensor(ring_r[slot][:, 0:FFN_WORDS], ring[:, slot, 0:FFN_WORDS],
                                        arena_r[:, FFN_HIGH[n][nxt % FFN_RING]:][:, 0:FFN_WORDS].bitcast(F32),
                                        ALU.subtract).then_inc(w_low, 1)
                        hidden(i, b)
                for b in range(2):
                    hidden(NF // FFN_RING, b)

            dve.wait_ge(small_in, 32)
            dve.wait_ge(x_in, 16)
            norm(0)
            copy("iq1", iqT[:, 2:4, :])
            for tc in range(NT):
                name = f"misc{tc}"
                dve.wait_ge(*O.ready(name))
                step(V.tensor_scalar(iw[:, tc, :], bank(name)[:, 256:264], DH ** -0.5 * HEADS ** -0.5, None, ALU.mult))
                step(V.tensor_tensor(dt_in[:, tc, :], bank(name)[:, 264:280], c("dt_bias"), ALU.add))
                drain(name, V.tensor_copy(ckv[:, tc, :], bank(name)[:, 0:256]))
            dt_flat = dt_in.rearrange("p a b -> p (a b)")
            V.scalar_tensor_tensor(sp[:, 0, :], dt_flat, -1.0, dt_flat, ALU.mult, ALU.max).then_inc(sp_abs, 1)
            for tc in range(NT):
                dve.wait_ge(kv_rstd, tc + 1)
                V.tensor_scalar(ckv[:, tc, :], ckv[:, tc, :], rstd_kv[:, tc, :], None, ALU.mult).then_inc(ckv_ready, 1)
            done = set()
            for u, (tc, _, heads, w) in enumerate(UNITS):
                dve.wait_ge(*O.drained(f"il{u}"))
                for i, h in enumerate(heads):
                    sc = score[:, tc, 0:w]
                    step(V.scalar_tensor_tensor(sc, lm[:, u % 2, i * w:(i + 1) * w], iw[:, tc, h:h + 1],
                                                sc if tc in done else causal_mask[tc], ALU.mult, ALU.add))
                    done.add(tc)
                V.engine_nop().then_inc(il_used, 1)
            for tc in range(NT):
                w = UNITS[-1][3] if tc else P
                sc, wk = score[:, tc, 0:w], work[:, tc, 0:w]
                for r in range(TOPK // 8):
                    src = sc if r == 0 else wk
                    step(V.max(top8[:, tc, :], src))
                    step(V.match_replace(wk, top8[:, tc, :], src, TAKEN))
                m = sel_mask[:, tc, 0:w]
                step(V.tensor_scalar(m, wk, TAKEN / 2, NEG, ALU.is_gt, ALU.mult))
                step(V.tensor_tensor(m, m, causal_mask[tc], ALU.add))
            dve.wait_ge(sp_exp, 1)
            log1p(sp[:, 1, :], sp[:, 3:7, :], sp[:, 2, :])
            dt_f = dt.rearrange("p a b -> p (a b)")
            step(V.scalar_tensor_tensor(dt_f, dt_flat, 0.0, sp[:, 2, :], ALU.max, ALU.add))
            dve.wait_ge(a_log_exp, 1)
            V.scalar_tensor_tensor(a_dt[:, :, :], dt[:, :, :], -1.0, neg_A.unsqueeze(1).to_broadcast([P, NT, 16]),
                                   ALU.mult, ALU.mult).then_inc(a_ready, 1)
            for j in range(6):
                dve.wait_ge(*O.drained(f"xb{j}"))
                for tap in range(4):
                    for m in range(2):
                        ch = 2 * j + m
                        src = xp[:, j % 2, m, 3 - tap:259 - tap]
                        wt = c("conv_w", (3 - tap) * NX + ch)
                        if tap == 0:
                            last = V.tensor_scalar(convT[:, ch, :], src, wt, None, ALU.mult)
                        else:
                            last = V.scalar_tensor_tensor(convT[:, ch, :], src, wt, convT[:, ch, :], ALU.mult, ALU.add)
                        if tap == 3 and m == 1:
                            last.then_inc(conv_sum, 1)
                        else:
                            step(last)
            attention("mla", lambda tc: sel_mask[:, tc, 0:(T if tc else P)], mixT[:, 0:4, :])
            for tc in range(NT):
                copy(f"xs{tc}1", xs[:, tc, 512:1024])
            dve.wait_ge(*O.ready("acs"))
            drain("acs", V.tensor_copy(acs[:, :, :], bank("acs")[:, 0:48].rearrange("p (a b) -> p a b", a=3)))
            V.tensor_tensor(sp[:, 2, 0:16], acs[:, 2, :], acs[:, 0, :], ALU.subtract).then_inc(end_sub, 1)

            def seg(i):
                cc, hq = i // 4, i % 4
                name = f"bc{cc}{hq}"
                dve.wait_ge(*O.ready(name))
                if i >= 2:
                    dve.wait_ge(seg_exp, i - 1)
                for k in range(4):
                    h = 4 * hq + k
                    last = V.scalar_tensor_tensor(lm[:, i % 2, k * P:(k + 1) * P], bank(name)[:, k * P:(k + 1) * P],
                                                  acs[:, cc, h:h + 1], c("causal_t"), ALU.subtract, ALU.add)
                drain(name, last)

            gated = [0]

            def gather(cc, g):
                cols = slice(g * 512, (g + 1) * 512)
                y = y_tok[:, cc, cols]
                dve.wait_ge(*O.ready(f"y{cc}{g}"))
                dve.wait_ge(scaled_ready, cc + 1)
                drain(f"y{cc}{g}", V.tensor_tensor(y, bank(f"y{cc}{g}"), xs[:, cc, cols], ALU.add))
                if cc == 1:
                    dve.wait_ge(*O.ready(f"yo{g}"))
                    t = y_part[:, 0, :]
                    dve.wait_ge(decays_ready, 2)
                    drain(f"yo{g}", V.tensor_tensor(t.rearrange("p (a b) -> p a b", a=8),
                                                    bank(f"yo{g}").rearrange("p (a b) -> p a b", a=8),
                                                    acs_exp[:, g * 8:(g + 1) * 8].unsqueeze(2).to_broadcast([P, 8, DH]),
                                                    ALU.mult))
                    step(V.tensor_tensor(y, y, t, ALU.add))
                gated[0] += 1
                V.tensor_tensor(y, y, z[:, cc, cols], ALU.mult).then_inc(y_gated, 1)

            for i in range(4):
                seg(i)
            gather(0, 0)
            seg(4)
            seg(5)
            gather(0, 1)
            seg(6)
            seg(7)
            gather(1, 0)
            gather(1, 1)
            for i in range(4):
                cc, g = i // 2, i % 2
                y = y_tok[:, cc, g * 512:(g + 1) * 512]
                dve.wait_ge(y_rstd, i + 1)
                V.tensor_scalar(y, y, rstd_g[:, cc, g:g + 1], None, ALU.mult).then_inc(y_ready, 1)
            for j in (1, 3):
                dve.wait_ge(*O.ready(f"yT{j}"))
                for kk in range(2):
                    k = 2 * j + kk
                    last = V.tensor_scalar(mixT[:, 4 + k, :], bank(f"yT{j}")[:, kk * T:(kk + 1) * T], c("ssm_norm", k),
                                           None, ALU.mult)
                last.then_inc(dve_drained, 1)
            split("ffn0_0")
            add_out("out0")
            ffn(0)
            split("l1_0")
            add_out("ffn0")
            norm_lo(2, lambda: split("l1_1"))
            step(V.memset(cv[:, :, 0:2], 0.0))
            for j in range(KD):
                b = j % 2
                name = f"cv{j}"
                split(f"l1_{j + 2}" if j + 2 < KD else f"out1w{j + 2 - KD}")
                dve.wait_ge(*O.ready(name))
                step(V.tensor_copy(c_sb[:, b, :], bank(name)[:, 0:T]))
                drain(name, V.tensor_tensor(cv[:, b, 2:T + 2], c_sb[:, b, :], bank(name)[:, T:2 * T], ALU.mult))
                step(V.tensor_scalar(sc_conv[:, b, :], cv[:, b, 2:T + 2], c("sc_w", 2 * KD + j), None, ALU.mult))
                for tap in (1, 0):
                    step(V.scalar_tensor_tensor(sc_conv[:, b, :], cv[:, b, tap:tap + T], c("sc_w", tap * KD + j),
                                                sc_conv[:, b, :], ALU.mult, ALU.add))
                dve.wait_ge(*O.ready(f"b{j}"))
                drain(f"b{j}", V.tensor_tensor(sc_conv[:, b, :], sc_conv[:, b, :], bank(f"b{j}")[:, 0:T], ALU.mult))
                step(V.tensor_copy(sc_hi[:, j, :], sc_conv[:, b, :]))
                V.tensor_tensor(sc_lo[:, j, :], sc_conv[:, b, :], sc_hi[:, j, :].bitcast(F32),
                                ALU.subtract).then_inc(sc_split, 1)
            split("ffn1_0")
            add_out("out1")
            ffn(1)
            add_out("ffn1")
            scaled_norm("first", x_final, 16)
            norm(4)
            step(V.tensor_copy(pos_f, pos[:, :]))
            for tc in range(NT):
                step(V.tensor_scalar(ang[:, tc, :], c("freq"), pos_f[:, tc:tc + 1], None, ALU.mult))
            step(V.tensor_scalar(rope_k[:, :, :], ang[:, :, :], 1 / (2 * np.pi), ROUND, ALU.mult, ALU.add))
            step(V.tensor_scalar(rope_k[:, :, :], rope_k[:, :, :], ROUND, None, ALU.subtract))
            for part_2pi in TWO_PI:
                step(V.scalar_tensor_tensor(ang[:, :, :], rope_k[:, :, :], -part_2pi, ang[:, :, :], ALU.mult, ALU.add))
            step(V.tensor_scalar(red[:, :, :], ang[:, :, :], PI, -PI, ALU.min, ALU.max))
            step(V.scalar_tensor_tensor(cosr[:, :, :], red[:, :, :], -1.0, red[:, :, :], ALU.mult, ALU.max))
            V.tensor_scalar(cosr[:, :, :], cosr[:, :, :], -1.0, float(np.pi / 2), ALU.mult, ALU.add).then_inc(angles, 1)
            copy("fq1", qT[:, 2:4, :])
            copy("fk1", kT[:, 2:4, :])
            dve.wait_ge(*O.drained("misc2_1"))
            f_flat = f_in.rearrange("p a b -> p (a b)")
            step(V.scalar_tensor_tensor(f_neg.rearrange("p (a b) -> p a b", a=NT), f_in[:, :, :], 1.0,
                                        c("b_forget").unsqueeze(1).to_broadcast([P, NT, 8]), ALU.mult, ALU.add))
            step(V.tensor_scalar(f_neg, f_neg, -1.0, None, ALU.mult))
            V.scalar_tensor_tensor(f_tmp[:, 0, :], f_neg, -1.0, f_neg, ALU.mult, ALU.max).then_inc(f_abs, 1)
            dve.wait_ge(f_exp, 1)
            log1p(f_u, f_tmp[:, 0:4, :], f_tmp[:, 4, :])
            V.scalar_tensor_tensor(log_f.rearrange("p a b -> p (a b)"), f_neg, 0.0, f_tmp[:, 4, :], ALU.max,
                                   ALU.add).then_inc(log_f_ready, 1)
            dve.wait_ge(*O.ready("fox_c"))
            drain("fox_c", V.tensor_copy(fox_c[:, :, :], bank("fox_c")[:, 0:16].rearrange("p (a b) -> p a b", a=NT)))
            attention("fox", lambda tc: causal_mask[tc], mixT[:, 0:4, :])
            attention("swa", lambda tc: window_mask[tc], mixT[:, 4:8, :])
            for j in range(4):
                for gi, n in enumerate(("pf", "ps")):
                    dve.wait_ge(*O.ready(f"{n}{j}"))
                    drain(f"{n}{j}", V.tensor_tensor(lm[:, gi, :].rearrange("p (a b) -> p a b", a=2), bank2(f"{n}{j}"),
                                                     gates[:, gi, 2 * j:2 * j + 2, :], ALU.mult))
                V.tensor_tensor(mergedT[:, 2 * j:2 * j + 2, :], lm[:, 0, :].rearrange("p (a b) -> p a b", a=2),
                                lm[:, 1, :].rearrange("p (a b) -> p a b", a=2), ALU.add).then_inc(merged, 1)
                dve.wait_ge(merged, j + 1)
            add_out("out2")
            norm(5)

            def per_token(v, n):
                return v.unsqueeze(2).to_broadcast([P, NT, n])

            def first_max(v, eq, first, m, hot):
                step(V.tensor_reduce(m, v, AX_X, ALU.max))
                step(V.tensor_tensor(eq[:, :, :], v, per_token(m, 8), ALU.is_equal))
                step(V.tensor_tensor(eq[:, :, :], eq[:, :, :], c("down8").unsqueeze(1).to_broadcast([P, NT, 8]), ALU.mult))
                step(V.tensor_reduce(first, eq[:, :, :], AX_X, ALU.max))
                step(V.tensor_tensor(hot[:, :, :], eq[:, :, :], per_token(first, 8), ALU.is_equal))

            for tc in range(NT):
                name = f"router{tc}"
                dve.wait_ge(*O.ready(name))
                drain(name, V.tensor_tensor(r_log[:, tc, :], bank(name)[:, 0:72], c("b_router"), ALU.add))
            g_log = r_log[:, :, 0:8]
            first_max(g_log, g_eq, g_first, g_max, g_hot)
            V.tensor_tensor(g_exp[:, :, :], g_log, per_token(g_max, 8), ALU.subtract).then_inc(r_sub, 1)
            V.engine_nop().then_inc(r_gate, 1)
            for tc in range(NT):
                e8 = e_all.rearrange("p (g e) -> p g e", g=8)
                step(V.tensor_tensor(e8, r_log[:, tc, 8:72].rearrange("p (g e) -> p g e", g=8),
                                     g_hot[:, tc, :].unsqueeze(2).to_broadcast([P, 8, 8]), ALU.mult))
                step(V.tensor_reduce(e_sel[:, tc, :], e_all.rearrange("p (g e) -> p e g", g=8), AX_X, ALU.add))
            first_max(e_sel[:, :, :], e_eq1, e_f1, e_m1, e_hot1)
            step(V.scalar_tensor_tensor(e_rest[:, :, :], e_hot1[:, :, :], NEG, e_sel[:, :, :], ALU.mult, ALU.add))
            first_max(e_rest[:, :, :], e_eq2, e_f2, e_m2, e_hot2)
            V.tensor_tensor(e_d, e_m2, e_m1, ALU.subtract).then_inc(r_sub, 1)
            dve.wait_ge(r_exp, 1)
            step(V.tensor_reduce(g_sum, g_exp[:, :, :], AX_X, ALU.add))
            step(V.reciprocal(g_w, g_sum))
            dve.wait_ge(r_exp, 2)
            step(V.tensor_scalar(e_den, e_x, 1.0, None, ALU.add))
            step(V.reciprocal(e_den, e_den))
            step(V.tensor_tensor(e_w1, e_den, g_w, ALU.mult))
            step(V.tensor_tensor(e_w2, e_w1, e_x, ALU.mult))
            step(V.tensor_tensor(e_hot1[:, :, :], e_hot1[:, :, :], per_token(e_w1, 8), ALU.mult))
            step(V.tensor_tensor(e_hot2[:, :, :], e_hot2[:, :, :], per_token(e_w2, 8), ALU.mult))
            V.tensor_tensor(gate8[:, :, :], e_hot1[:, :, :], e_hot2[:, :, :], ALU.add).then_inc(r_gate, 1)
            dve.wait_ge(*O.ready("rank"))
            step(V.tensor_tensor(rank8[:, :, :], bank("rank")[:, 0:16].rearrange("p (a b) -> p a b", a=NT), g_hot[:, :, :],
                                 ALU.mult))
            drain("rank", V.tensor_reduce(most, bank("rank")[:, 16:24], AX_X, ALU.max))
            step(V.tensor_reduce(rank, rank8[:, :, :], AX_X, ALU.add))
            step(V.tensor_scalar(passes_f, most, float(CAP), 1.0, ALU.is_gt, ALU.add))
            V.tensor_copy(passes_i[:, :], passes_f).then_inc(r_pass, 1)
            dve.wait_ge(r_pass, 1)
            passes = dve.value_load(passes_i[0:1, 0:1], min_val=1, max_val=T // CAP)
            dve.wait_ge(row_in, 32)
            for tc in range(NT):
                V.tensor_tensor(xn[:, tc, :], xn[:, tc, :], norm_row[:, :], ALU.mult).then_inc(x_rows, 1)

            def split_lo(u, n):
                dve.wait_ge(m_hi, n * NM + (u + 1))
                raw = ring[:, MOE_SLOT[u % NM], :]
                V.tensor_tensor(ring_r[MOE_SLOT[u % NM]][:, :], raw, w_hi[:, u % HI_SLOTS, :].bitcast(F32), ALU.subtract).then_inc(m_lo, 1)

            def select(group, n):
                for tc in range(NT):
                    last = V.tensor_scalar(sel_g[:, tc, :], c("iota"), rank[:, tc:tc + 1],
                                           g_hot_9[:, tc, bass.ds(group, 1)], ALU.is_equal, ALU.mult)
                last.then_inc(m_sel, 1)

            def gathered(n):
                for i in range(2):
                    at = slice(i * 512, (i + 1) * 512)
                    dve.wait_ge(m_xg_hi, n * 2 + (i + 1))
                    last = V.tensor_tensor(xg_lo[:, at], psum[:, XG_BANK[i], :], xg_hi[:, at].bitcast(F32), ALU.subtract)
                last.then_inc(m_xg_lo, 1)

            def turned_lo(e, n):
                dve.wait_ge(m_hT_hi, n * PER_GROUP + (e + 1))
                V.tensor_tensor(hT_lo[:, e % 2, :], psum[:, T_BANK, :], hT_hi[:, e % 2, :].bitcast(F32),
                                ALU.subtract).then_inc(m_hT_lo, 1)

            for u in range(2):
                split_lo(u, 0)
            with dve.Fori(0, passes) as p:
                n = dve.snap(p * N_GROUPS)
                select(0, n)
                gathered(n)
                with dve.Fori(0, N_GROUPS) as g:
                    n = dve.snap(p * N_GROUPS + g)
                    dve.wait_ge(m_selT, n + 1)
                    V.tensor_copy(gate_g, psum[:, SMALL_BANK, T:T + PER_GROUP]).then_inc(m_gate, 1)
                    for u, (kind, e) in enumerate(MOE):
                        if u + 2 < NM:
                            split_lo(u + 2, n)
                        else:
                            with dve.If(n + 1 < passes * N_GROUPS):
                                split_lo(u + 2, n)
                        if kind == "w1" and e >= 1:
                            turned_lo(e - 1, n)
                        if kind == "w3":
                            dve.wait_ge(m_silu, n * PER_GROUP + (e + 1))
                            dve.wait_ge(m_unit, n * NM + (u + 1))
                            if e == 0:
                                dve.wait_ge(m_gate, n + 1)
                            V.scalar_tensor_tensor(h_e[:, e % 2, :], psum[:, H3_BANK[e % 2], :], gate_g[:, e:e + 1],
                                                   h_e[:, e % 2, :], ALU.mult, ALU.mult).then_inc(m_h, 1)
                        if u == NM - 2:
                            turned_lo(PER_GROUP - 1, n)
                        if u == 4:
                            with dve.If(g < N_GROUPS - 1):
                                select(g + 1, n)
                    for i in range(2):
                        at = slice(i * 512, (i + 1) * 512)
                        dve.wait_ge(m_y_hi, n * 2 + (i + 1))
                        last = V.tensor_tensor(y_lo[:, at], psum[:, Y_BANK[i], :], y_hi[:, at].bitcast(F32), ALU.subtract)
                    last.then_inc(m_y_lo, 1)
                    with dve.If(g < N_GROUPS - 1):
                        gathered(n + 1)
                    for i, (tc, h) in enumerate(RES):
                        dve.wait_ge(m_sc, n * 4 + (i + 1))
                        part_x = x[:, tc, h * 512:(h + 1) * 512]
                        V.tensor_tensor(part_x, part_x, psum[:, S_BANK[i], :], ALU.add).then_inc(m_scd, 1)
                V.tensor_scalar(rank, rank, float(CAP), None, ALU.subtract).then_inc(scaled_ready, 1)
                dve.wait_ge(scaled_ready, p + (1 + NT))
            dve.wait_ge(m_scd, passes * (4 * N_GROUPS))
            V.tensor_copy(total[:, 0:NT], rank).then_inc(moe_done, 1)
            scaled_norm("last", out_ready, 48)

        @block.gpsimd
        def _(pool):
            G = nc.gpsimd
            step = Steps(pool, pool_step)

            def inverse_root(total_, mean_, out_, size, done):
                step(G.tensor_scalar(mean_, total_, 1.0 / size, EPS, ALU.mult, ALU.add))
                G.tensor_tensor(out_, mean_, c("half", 0), ALU.pow).then_inc(done, 1)

            def norm(n):
                for tc in range(NT):
                    r = NORMS[n]
                    pool.wait_ge(squares, NT * r + tc + 1)
                    inverse_root(ss[:, r, tc:tc + 1], mean[:, r, tc:tc + 1], rstd[:, r, tc:tc + 1], D, rstd_ready)

            def attention(kind):
                K = KINDS[kind]
                for u, (tc, at, heads, w) in enumerate(UNITS):
                    pool.wait_ge(sums_inverted, K * NU + u + 1)
                    for i in range(len(heads)):
                        col = at + i
                        pu = pr[:, u % 2, i * w:(i + 1) * w]
                        last = G.tensor_scalar(pu, pu, row_inv[:, K, col:col + 1], None, ALU.mult)
                    last.then_inc(probs_ready, 1)

            pool.wait_ge(small_in, 32)
            norm(0)
            for tc in range(NT):
                pool.wait_ge(kv_sq, tc + 1)
                inverse_root(ss_kv[:, tc, :], mean_kv[:, tc, :], rstd_kv[:, tc, :], LATENT, kv_rstd)
            pool.wait_ge(*O.ready("il5"))
            G.memset(xp[:, :, :, 0:3], 0.0).then_inc(pads_zero, 1)
            attention("mla")
            pool.wait_ge(*O.drained("xs10"))
            pool.wait_ge(*O.drained("xs11"))

            def by_head(v):
                return v.rearrange("p (h d) -> p h d", d=DH)

            def spread(v, h=SSM_HEADS):
                return v.unsqueeze(2).to_broadcast([P, h, DH])

            for tc in range(NT):
                G.tensor_tensor(by_head(xdt[:, tc, :]), by_head(xs[:, tc, :]), spread(dt[:, tc, :]),
                                ALU.mult).then_inc(xdt_ready, 1)
            pool.wait_ge(decays_ready, 1)
            pool.wait_ge(xdt_ready, 2)
            G.tensor_tensor(by_head(xdt_end[:, :]), by_head(xdt[:, 0, :]), spread(end_exp), ALU.mult).then_inc(xdt_ready, 1)

            def decayed(i):
                cc, hq = i // 4, i % 4
                pool.wait_ge(seg_exp, i + 1)
                if i == 0:
                    pool.wait_ge(*O.drained("cbT"))
                if i >= 2:
                    pool.wait_ge(*y_rows_used(i - 2))
                G.tensor_tensor(pT[:, i % 2, :].rearrange("p (a b) -> p a b", a=4),
                                pr[:, i % 2, :].rearrange("p (a b) -> p a b", a=4),
                                cbT[:, 2 * cc + hq // 2, :].unsqueeze(1).to_broadcast([P, 4, P]), ALU.mult).then_inc(ssm_w, 1)

            decayed(0)
            decayed(1)
            for tc in range(NT):
                G.tensor_tensor(by_head(xs[:, tc, :]), by_head(xs[:, tc, :]), spread(c("Dskip")),
                                ALU.mult).then_inc(scaled_ready, 1)
            for i in range(2, 8):
                decayed(i)
            for i in range(4):
                cc, g = i // 2, i % 2
                pool.wait_ge(y_sq, i + 1)
                inverse_root(ssg[:, cc, g:g + 1], mean_g[:, cc, g:g + 1], rstd_g[:, cc, g:g + 1], SSM_IN // 2, y_rstd)
            norm(1)
            norm(2)
            norm(3)
            norm("first")
            norm(4)
            pool.wait_ge(sincos, 2)
            for tc in range(NT):
                pool.wait_ge(*O.drained(f"sq{tc}"))
                v = rope_x[:, tc, :].rearrange("p (h a b) -> p h a b", a=2, b=DH // 2)
                ra = rope_a.rearrange("p (h a b) -> p h a b", a=2, b=DH // 2)
                rb = rope_b.rearrange("p (h a b) -> p h a b", a=2, b=DH // 2)
                co = cos_t[:, tc, :].unsqueeze(1).to_broadcast([P, 10, DH // 2])
                si = sin_t[:, tc, :].unsqueeze(1).to_broadcast([P, 10, DH // 2])
                for a in range(2):
                    step(G.tensor_tensor(ra[:, :, a, :], v[:, :, a, :], co, ALU.mult))
                    step(G.tensor_tensor(rb[:, :, a, :], v[:, :, 1 - a, :], si, ALU.mult))
                step(G.tensor_tensor(v[:, :, 0, :], ra[:, :, 0, :], rb[:, :, 0, :], ALU.subtract))
                G.tensor_tensor(v[:, :, 1, :], ra[:, :, 1, :], rb[:, :, 1, :], ALU.add).then_inc(roped, 1)
                pool.wait_ge(roped, tc + 1)
            attention("fox")
            attention("swa")
            norm(5)
            pool.wait_ge(moe_done, 1)
            norm("last")


IN_NAMES = ["small", "x", "positions", "w_router", "in_w", "misc", "w_uk", "w_uv", "out_w0", "gate0", "up0", "down0",
            "l1_in", "out_w1", "gate1", "up1", "down1", "final_norm", "w_in2", "misc2", "proj_fox", "proj_swa", "out_w2",
            "moe_norm", "final_norm2", "w1", "w3", "w2"]


def layout(i):
    def chunked(w):
        return w.reshape(P, KD, -1, P).transpose(2, 0, 1, 3)

    def all_rows(v):
        return np.broadcast_to(v.reshape(1, -1), (P, v.size))

    def chan(v):
        return v.reshape(-1, P).T

    q, kk = np.arange(P)[:, None], np.arange(P)[None, :]
    neg = np.float32(NEG)
    causal = np.where(kk <= q, np.float32(0), neg)
    parts = {
        "ident": q == kk, "tri": q <= kk, "strict": q < kk, "ones": np.ones((P, P)), "open": np.zeros((P, P)),
        "causal": causal, "band": np.where(kk > q, np.float32(0), neg), "causal2": causal, "causal_t": causal.T,
        "iota": all_rows(np.arange(CAP)), "down8": all_rows(8 - np.arange(8)),
        "freq": all_rows(np.float32(10000.0) ** (-np.arange(32, dtype=np.float32) * np.float32(2) / np.float32(64))),
        "half": np.full((P, 8), -0.5),
        "attn_norm": i["l0_attn_norm"].reshape(P, KD), "ffn_norm": i["l0_ffn_norm"].reshape(P, KD),
        "l1_norm": i["l1_conv_norm"].reshape(P, KD), "ffn1_norm": i["l1_ffn_norm"].reshape(P, KD),
        "attn2_norm": i["attn_norm_2"].reshape(P, KD), "moe_norm": i["ffn_norm_2"].reshape(P, KD),
        "kv_norm": chan(i["l0_kv_norm"]),
        "conv_w": i["l0_conv_w"].reshape(4 * NX, P).T, "conv_b": chan(i["l0_conv_b"]),
        "dt_bias": all_rows(i["l0_dt_bias"]), "A_log": all_rows(i["l0_A_log"]), "Dskip": all_rows(i["l0_D"]),
        "ssm_norm": chan(i["l0_ssm_norm"]), "sc_w": i["l1_conv_w"].reshape(3 * KD, P).T,
        "b_forget": all_rows(i["b_forget_2"]), "b_gate": i["b_gate_2"].reshape(2 * KD, P).T,
        "sinks": all_rows(i["attn_sinks_2"]),
        "b_router": all_rows(np.concatenate([i["b_group_2"].ravel(), i["b_expert_2"].ravel()])),
    }
    small = np.empty((P, N_SMALL), np.float32)
    for name, (at, width) in AT.items():
        small[:, at:at + width] = parts[name]
    in_w, w_in2 = i["l0_in_w"], i["w_in_2"][0]
    l1 = i["l1_in_w"].reshape(P, KD, 3, KD, P)[:, :, [1, 2, 0]].transpose(3, 0, 1, 2, 4)
    return {
        "small": small,
        "x": i["x"][0],
        "positions": i["positions_2"].reshape(NT, P).T,
        "w_router": np.concatenate([i["w_group_2"][0], i["w_expert_2"][0]], axis=1),
        "in_w": in_w,
        "misc": np.concatenate([in_w[:, 512:768], in_w[:, 1344:1352], in_w[:, 3912:3928], in_w[:, 1280:1344]], axis=1),
        "w_uk": i["l0_w_uk"].transpose(2, 0, 1).reshape(LATENT, 512),
        "w_uv": i["l0_w_uv"].transpose(1, 0, 2).reshape(LATENT, 512),
        "out_w0": i["l0_out_w"],
        "gate0": chunked(i["l0_w_gate"]), "up0": chunked(i["l0_w_up"]), "down0": i["l0_w_down"].reshape(NF, P, D),
        "l1_in": l1.reshape(KD, P, 3 * KD * P),
        "out_w1": i["l1_out_w"],
        "gate1": chunked(i["l1_w_gate"]), "up1": chunked(i["l1_w_up"]), "down1": i["l1_w_down"].reshape(NF, P, D),
        "final_norm": i["final_norm"].reshape(1, D),
        "w_in2": w_in2,
        "misc2": np.concatenate([w_in2[:, 1536:1544], w_in2[:, 2056:2312]], axis=1),
        "proj_fox": i["w_proj_fox_2"][0], "proj_swa": i["w_proj_swa_2"][0], "out_w2": i["w_out_2"][0],
        "moe_norm": i["ffn_norm_2"].reshape(1, D),
        "final_norm2": i["final_norm_2"].reshape(1, D),
        "w1": i["w1_2"].reshape(N_EXPERTS, P, KD * D_EXPERT), "w3": i["w3_2"].reshape(N_EXPERTS, P, KD * D_EXPERT),
        "w2": i["w2_2"].reshape(N_EXPERTS * NE, P, D),
    }


def kernel(**inputs):
    import concourse.bacc as bacc
    from concourse.bass_utils import run_bass_kernel_spmd

    given = {name: np.asarray(a) for name, a in inputs.items()}
    arrays = {name: np.ascontiguousarray(a) for name, a in layout(given).items()}
    nc = bacc.Bacc("TRN2", target_bir_lowering=False, num_devices=1)
    d = {name: nc.dram_tensor(f"in_{name}", arrays[name].shape, mybir.dt.from_np(arrays[name].dtype),
                              kind="ExternalInput").ap() for name in IN_NAMES}
    out = nc.dram_tensor("out", (T, D), F32, kind="ExternalOutput").ap()
    program(nc, d, out)
    r = run_bass_kernel_spmd(nc, [{f"in_{name}": arrays[name] for name in IN_NAMES}], core_ids=[0])
    return np.asarray(r.results[0]["out"]).reshape(1, T, D)
```
